# Optimizing a Trainium2 kernel written in Bass

```python
import math
import jax, jax.numpy as jnp
from jax import lax
import numpy as np

D_MODEL = 1024
BATCH = 1
SEQ = 256
DEPTH = 1

MEM_LEN = 256
POOL_WINDOWS = (2, 4, 8, 16)
POOL_GROUPS = 4
POOL_GROUP_DIM = D_MODEL // 8
POOL_DIM = POOL_GROUPS * POOL_GROUP_DIM
MLA_HEADS = 8
QK_NOPE_DIM = 128
QK_ROPE_DIM = 64
V_HEAD_DIM = 128
Q_LORA_RANK = 384
KV_LORA_RANK = 256
MLA_V_DIM = MLA_HEADS * V_HEAD_DIM
ROPE_THETA = 10000.0
Q_BLOCK = 128
XATTN_HEADS = 4
XATTN_HEAD_DIM = 128
XATTN_DIM = XATTN_HEADS * XATTN_HEAD_DIM
N_BRANCHES = 3
IN_SPLIT_SIZES = (POOL_DIM, Q_LORA_RANK, KV_LORA_RANK, QK_ROPE_DIM, XATTN_DIM, N_BRANCHES * D_MODEL)
D_IN = sum(IN_SPLIT_SIZES)
N_GROUPS = 4
EXPERTS_PER_GROUP = 8
N_EXPERTS = N_GROUPS * EXPERTS_PER_GROUP
TOP_K = 2
D_EXPERT = D_MODEL // 4
MOE_BLOCK = 128
RMS_EPS = 1e-6
NEG_INF = -1e30


def rms_norm(x, g):
    xf = x.astype(jnp.float32)
    xf = xf * lax.rsqrt(jnp.mean(xf * xf, axis=-1, keepdims=True) + RMS_EPS)
    return xf.astype(x.dtype) * g

def rope_tables(positions):
    inv_freq = 1.0 / (ROPE_THETA ** (jnp.arange(0, QK_ROPE_DIM, 2, dtype=jnp.float32) / QK_ROPE_DIM))
    ang = positions.astype(jnp.float32)[..., None] * inv_freq
    return jnp.cos(ang), jnp.sin(ang)

def apply_rope(x, cos, sin):
    xf = x.astype(jnp.float32)
    half = xf.shape[-1] // 2
    x1, x2 = xf[..., :half], xf[..., half:]
    return jnp.concatenate([x1 * cos - x2 * sin, x2 * cos + x1 * sin], axis=-1).astype(x.dtype)

def pool_mixer(u, pool_w, pool_scale):
    B, S, _ = u.shape
    uf = u.astype(jnp.float32)
    cs = jnp.pad(jnp.cumsum(uf, axis=1), ((0, 0), (1, 0), (0, 0)))
    cnt_base = jnp.arange(S) + 1
    outs = []
    for g, w in enumerate(POOL_WINDOWS):
        sl = slice(g * POOL_GROUP_DIM, (g + 1) * POOL_GROUP_DIM)
        cg = cs[..., sl]
        lag = jnp.pad(cg[:, :S + 1 - w], ((0, 0), (w - 1, 0), (0, 0)))
        cnt = jnp.minimum(cnt_base, w).astype(jnp.float32)[None, :, None]
        outs.append((cg[:, 1:] - lag) / cnt - uf[..., sl])
    p = jnp.stack(outs, axis=2).astype(u.dtype)
    y = jnp.einsum('bsgc,gcd->bsgd', p, pool_w).reshape(B, S, POOL_DIM)
    return y * pool_scale

def causal_block_attention(q_nope, q_rope, k_nope, k_rope, v):
    B, S, H, _ = q_nope.shape
    nb = S // Q_BLOCK
    scale = (QK_NOPE_DIM + QK_ROPE_DIM) ** -0.5
    k_idx = jnp.arange(S)

    def one_block(args):
        qn, qr, i = args
        s = (jnp.einsum('bqhd,bkhd->bhqk', qn, k_nope)
             + jnp.einsum('bqhr,bkr->bhqk', qr, k_rope)).astype(jnp.float32) * scale
        q_idx = i * Q_BLOCK + jnp.arange(Q_BLOCK)
        s = jnp.where(k_idx[None, :] <= q_idx[:, None], s, NEG_INF)
        p = jax.nn.softmax(s, axis=-1).astype(v.dtype)
        return jnp.einsum('bhqk,bkhd->bqhd', p, v)

    qn_b = q_nope.reshape(B, nb, Q_BLOCK, H, -1).transpose(1, 0, 2, 3, 4)
    qr_b = q_rope.reshape(B, nb, Q_BLOCK, H, -1).transpose(1, 0, 2, 3, 4)
    out = lax.map(one_block, (qn_b, qr_b, jnp.arange(nb)))
    return out.transpose(1, 0, 2, 3, 4).reshape(B, S, H, V_HEAD_DIM)

def mla_branch(q_down, kv_down, k_rope_in, cos, sin, q_norm_g, w_uq, kv_norm_g, w_uk, w_uv):
    B, S, _ = q_down.shape
    c_q = rms_norm(q_down, q_norm_g)
    q = (c_q @ w_uq).reshape(B, S, MLA_HEADS, QK_NOPE_DIM + QK_ROPE_DIM)
    q_nope = q[..., :QK_NOPE_DIM]
    q_rope = apply_rope(q[..., QK_NOPE_DIM:], cos[:, :, None, :], sin[:, :, None, :])
    c_kv = rms_norm(kv_down, kv_norm_g)
    k_nope = (c_kv @ w_uk).reshape(B, S, MLA_HEADS, QK_NOPE_DIM)
    v = (c_kv @ w_uv).reshape(B, S, MLA_HEADS, V_HEAD_DIM)
    k_rope = apply_rope(k_rope_in, cos, sin)
    return causal_block_attention(q_nope, q_rope, k_nope, k_rope, v).reshape(B, S, MLA_V_DIM)

def memory_cross_attention(xq, mem_n, w_mem_kv):
    B, S, _ = xq.shape
    kv = mem_n @ w_mem_kv
    k = kv[..., :XATTN_DIM].reshape(B, -1, XATTN_HEADS, XATTN_HEAD_DIM)
    v = kv[..., XATTN_DIM:].reshape(B, -1, XATTN_HEADS, XATTN_HEAD_DIM)
    q = xq.reshape(B, S, XATTN_HEADS, XATTN_HEAD_DIM)
    s = jnp.einsum('bshd,bmhd->bhsm', q, k).astype(jnp.float32) * (XATTN_HEAD_DIM ** -0.5)
    p = jax.nn.softmax(s, axis=-1).astype(v.dtype)
    return jnp.einsum('bhsm,bmhd->bshd', p, v).reshape(B, S, XATTN_DIM)

def hierarchical_moe(h, w_rg, b_rg, w_re, b_re, w_gate_e, w_up_e, w_down_e):
    B, S, D = h.shape
    T = B * S
    xt = h.reshape(T, D)
    g_logits = (xt @ w_rg).astype(jnp.float32) + b_rg.astype(jnp.float32)
    g_probs = jax.nn.softmax(g_logits, axis=-1)
    g_idx = jnp.argmax(g_logits, axis=-1)
    p_g = jnp.take_along_axis(g_probs, g_idx[:, None], axis=1)
    e_logits = ((xt @ w_re).astype(jnp.float32) + b_re.astype(jnp.float32)).reshape(T, N_GROUPS, EXPERTS_PER_GROUP)
    e_sel = jnp.take_along_axis(e_logits, g_idx[:, None, None], axis=1)[:, 0]
    p_e = jax.nn.softmax(e_sel, axis=-1)
    top_p, top_i = lax.top_k(p_e, TOP_K)
    weights = p_g * top_p / jnp.sum(top_p, axis=-1, keepdims=True)
    expert_idx = g_idx[:, None] * EXPERTS_PER_GROUP + top_i

    A = T * TOP_K
    e_flat = expert_idx.reshape(A).astype(jnp.int32)
    tok_flat = jnp.repeat(jnp.arange(T, dtype=jnp.int32), TOP_K)
    w_flat = weights.reshape(A)
    order = jnp.argsort(e_flat)
    e_sorted = e_flat[order]
    counts = jnp.bincount(e_flat, length=N_EXPERTS)
    padded = ((counts + MOE_BLOCK - 1) // MOE_BLOCK) * MOE_BLOCK
    pad_end = jnp.cumsum(padded)
    pad_start = pad_end - padded
    start = jnp.cumsum(counts) - counts
    dest = pad_start[e_sorted] + (jnp.arange(A) - start[e_sorted])
    R = ((A + MOE_BLOCK - 1) // MOE_BLOCK) * MOE_BLOCK + N_EXPERTS * MOE_BLOCK
    n_blk = R // MOE_BLOCK
    row_tok = jnp.full((R,), T, dtype=jnp.int32).at[dest].set(tok_flat[order])
    row_w = jnp.zeros((R,), dtype=jnp.float32).at[dest].set(w_flat[order])
    blk_e = jnp.minimum(jnp.searchsorted(pad_end, jnp.arange(n_blk) * MOE_BLOCK, side='right'), N_EXPERTS - 1)
    x_pad = jnp.concatenate([xt, jnp.zeros((1, D), xt.dtype)], axis=0)

    def run_block(args):
        toks, e = args
        xb = x_pad[toks]
        a = jax.nn.silu(xb @ w_gate_e[e]) * (xb @ w_up_e[e])
        return a @ w_down_e[e]

    yb = lax.map(run_block, (row_tok.reshape(n_blk, MOE_BLOCK), blk_e))
    y = yb.reshape(R, D) * row_w[:, None].astype(yb.dtype)
    out = jax.ops.segment_sum(y, row_tok, num_segments=T + 1)[:T]
    return out.reshape(B, S, D)

def first_inputs(seed: int = 0) -> dict:
    key = jax.random.key(seed)
    ks = jax.random.split(key, 32)
    f32 = jnp.float32

    def dense(k, shape, fan_in):
        return jax.random.normal(k, shape, f32) * (fan_in ** -0.5)

    def gain(k, shape):
        return 1.0 + 0.05 * jax.random.normal(k, shape, f32)

    L = DEPTH
    return {
        "x": jax.random.normal(ks[0], (BATCH, SEQ, D_MODEL), f32),
        "mem": jax.random.normal(ks[1], (BATCH, MEM_LEN, D_MODEL), f32),
        "positions": (jnp.arange(SEQ, dtype=jnp.int32)[None, :]
                      + jax.random.randint(ks[2], (BATCH, 1), 0, 1024, dtype=jnp.int32)),
        "mix_norm_g": gain(ks[3], (L, D_MODEL)),
        "w_in": dense(ks[4], (L, D_MODEL, D_IN), D_MODEL),
        "gate_b": 0.02 * jax.random.normal(ks[5], (L, N_BRANCHES, D_MODEL), f32),
        "q_norm_g": gain(ks[6], (L, Q_LORA_RANK)),
        "w_uq": dense(ks[7], (L, Q_LORA_RANK, MLA_HEADS * (QK_NOPE_DIM + QK_ROPE_DIM)), Q_LORA_RANK),
        "kv_norm_g": gain(ks[8], (L, KV_LORA_RANK)),
        "w_uk": dense(ks[9], (L, KV_LORA_RANK, MLA_HEADS * QK_NOPE_DIM), KV_LORA_RANK),
        "w_uv": dense(ks[10], (L, KV_LORA_RANK, MLA_V_DIM), KV_LORA_RANK),
        "pool_w": dense(ks[11], (L, POOL_GROUPS, POOL_GROUP_DIM, POOL_GROUP_DIM), POOL_GROUP_DIM),
        "pool_scale": gain(ks[12], (L, POOL_DIM)),
        "mem_norm_g": gain(ks[13], (L, D_MODEL)),
        "w_mem_kv": dense(ks[14], (L, D_MODEL, 2 * XATTN_DIM), D_MODEL),
        "w_br_pool": dense(ks[15], (L, POOL_DIM, D_MODEL), POOL_DIM),
        "w_br_mla": dense(ks[16], (L, MLA_V_DIM, D_MODEL), MLA_V_DIM),
        "w_br_mem": dense(ks[17], (L, XATTN_DIM, D_MODEL), XATTN_DIM),
        "w_out": dense(ks[18], (L, D_MODEL, D_MODEL), D_MODEL),
        "ffn_norm_g": gain(ks[19], (L, D_MODEL)),
        "w_router_group": dense(ks[20], (L, D_MODEL, N_GROUPS), D_MODEL),
        "b_router_group": 0.01 * jax.random.normal(ks[21], (L, N_GROUPS), f32),
        "w_router_expert": dense(ks[22], (L, D_MODEL, N_EXPERTS), D_MODEL),
        "b_router_expert": 0.01 * jax.random.normal(ks[23], (L, N_EXPERTS), f32),
        "w_gate_e": dense(ks[24], (L, N_EXPERTS, D_MODEL, D_EXPERT), D_MODEL),
        "w_up_e": dense(ks[25], (L, N_EXPERTS, D_MODEL, D_EXPERT), D_MODEL),
        "w_down_e": dense(ks[26], (L, N_EXPERTS, D_EXPERT, D_MODEL), D_EXPERT),
        "final_norm_g": gain(ks[27], (D_MODEL,)),
    }

def first_block(x, mem, positions, mix_norm_g, w_in, gate_b, q_norm_g, w_uq, kv_norm_g, w_uk, w_uv,
              pool_w, pool_scale, mem_norm_g, w_mem_kv, w_br_pool, w_br_mla, w_br_mem, w_out,
              ffn_norm_g, w_router_group, b_router_group, w_router_expert, b_router_expert,
              w_gate_e, w_up_e, w_down_e, final_norm_g):
    B, S, D = x.shape
    cos, sin = rope_tables(positions)
    split_points = list(np.cumsum(IN_SPLIT_SIZES)[:-1])
    for l in range(DEPTH):
        h = rms_norm(x, mix_norm_g[l])
        proj = h @ w_in[l]
        u_pool, q_down, kv_down, k_rope_in, xq, gate_logits = jnp.split(proj, split_points, axis=-1)
        y_pool = pool_mixer(u_pool, pool_w[l], pool_scale[l])
        y_mla = mla_branch(q_down, kv_down, k_rope_in, cos, sin,
                           q_norm_g[l], w_uq[l], kv_norm_g[l], w_uk[l], w_uv[l])
        y_mem = memory_cross_attention(xq, rms_norm(mem, mem_norm_g[l]), w_mem_kv[l])
        gates = jax.nn.sigmoid(gate_logits.reshape(B, S, N_BRANCHES, D) + gate_b[l])
        merged = (gates[:, :, 0] * (y_pool @ w_br_pool[l])
                  + gates[:, :, 1] * (y_mla @ w_br_mla[l])
                  + gates[:, :, 2] * (y_mem @ w_br_mem[l]))
        x = x + merged @ w_out[l]
        h2 = rms_norm(x, ffn_norm_g[l])
        x = x + hierarchical_moe(h2, w_router_group[l], b_router_group[l], w_router_expert[l],
                                 b_router_expert[l], w_gate_e[l], w_up_e[l], w_down_e[l])
    return rms_norm(x, final_norm_g)


N_HEADS = 16
HEAD_DIM = D_MODEL // N_HEADS
N_MIXERS = 2
CHUNK = 64
LEFT_CHUNKS = 8
BAND = (LEFT_CHUNKS + 1) * CHUNK
REL_CLIP = 128
N_REL = (CHUNK - 1) + REL_CLIP + 1
D_FF = int(math.ceil(D_MODEL * 8 / 3 / 256) * 256)
N_A_LAYERS = (DEPTH + N_MIXERS - 1) // N_MIXERS


def rms_norm_2(x, g):
    xf = x.astype(jnp.float32)
    y = xf * lax.rsqrt(jnp.mean(xf * xf, axis=-1, keepdims=True) + RMS_EPS)
    return (y * g.astype(jnp.float32)).astype(x.dtype)

def split_heads(h, w_qkv):
    b, s, _ = h.shape
    qkv = (h @ w_qkv).reshape(b, s, 3, N_HEADS, HEAD_DIM)
    qkv = jnp.transpose(qkv, (2, 0, 3, 1, 4))
    return qkv[0], qkv[1], qkv[2]

def merge_heads(o):
    b, h, s, d = o.shape
    return jnp.transpose(o, (0, 2, 1, 3)).reshape(b, s, h * d)

def chunk_relpos_attention(h, w_qkv, w_o, rel_bias):
    b, s, _ = h.shape
    n_chunks = s // CHUNK
    q, k, v = split_heads(h, w_qkv)
    i_idx = np.arange(CHUNK)[:, None]
    j_idx = np.arange(BAND)[None, :]
    rel = np.clip(LEFT_CHUNKS * CHUNK + i_idx - j_idx, -(CHUNK - 1), REL_CLIP) + (CHUNK - 1)
    bias = jnp.take(rel_bias, jnp.asarray(rel, dtype=jnp.int32), axis=1).astype(jnp.float32)
    scale = 1.0 / math.sqrt(HEAD_DIM)
    outs = []
    for c in range(n_chunks):
        k0 = max(0, (c - LEFT_CHUNKS) * CHUNK)
        k1 = (c + 1) * CHUNK
        n_keys = k1 - k0
        q_blk = q[:, :, c * CHUNK:(c + 1) * CHUNK]
        sc = jnp.einsum('bhqd,bhkd->bhqk', q_blk, k[:, :, k0:k1]).astype(jnp.float32) * scale
        sc = sc + bias[None, :, :, BAND - n_keys:]
        p = jax.nn.softmax(sc, axis=-1).astype(v.dtype)
        outs.append(jnp.einsum('bhqk,bhkd->bhqd', p, v[:, :, k0:k1]))
    o = jnp.concatenate(outs, axis=2)
    return merge_heads(o) @ w_o

def stick_breaking_attention(h, w_qkv, w_o):
    b, s, _ = h.shape
    q, k, v = split_heads(h, w_qkv)
    scale = 1.0 / math.sqrt(HEAD_DIM)
    outs = []
    for qb in range(s // Q_BLOCK):
        n_keys = (qb + 1) * Q_BLOCK
        q_blk = q[:, :, qb * Q_BLOCK:(qb + 1) * Q_BLOCK]
        z = jnp.einsum('bhqd,bhkd->bhqk', q_blk, k[:, :, :n_keys]).astype(jnp.float32) * scale
        t_pos = qb * Q_BLOCK + np.arange(Q_BLOCK)
        causal = jnp.asarray((np.arange(n_keys)[None, :] < t_pos[:, None])[None, None])
        log_keep = jnp.where(causal, jax.nn.log_sigmoid(-z), 0.0)
        suffix = lax.cumsum(log_keep, axis=3, reverse=True) - log_keep
        a = jnp.where(causal, jnp.exp(jax.nn.log_sigmoid(z) + suffix), 0.0).astype(v.dtype)
        outs.append(jnp.einsum('bhqk,bhkd->bhqd', a, v[:, :, :n_keys]))
    o = jnp.concatenate(outs, axis=2)
    return merge_heads(o) @ w_o

def swiglu(h, w_gate, w_up, w_down):
    return (jax.nn.silu(h @ w_gate) * (h @ w_up)) @ w_down

def second_inputs(seed: int = 0) -> dict:
    key = jax.random.key(seed)
    ks = jax.random.split(key, 12)
    d, f = D_MODEL, D_FF
    nrm = lambda k, shape, fan: jax.random.normal(k, shape, jnp.float32) * (fan ** -0.5)
    gain = lambda k: 1.0 + 0.02 * jax.random.normal(k, (DEPTH, d), jnp.float32)
    return {
        "x": jax.random.normal(ks[0], (BATCH, SEQ, d), jnp.float32),
        "g_pre_mix": gain(ks[1]),
        "g_post_mix": gain(ks[2]),
        "w_qkv": nrm(ks[3], (DEPTH, d, 3 * d), d),
        "w_o": nrm(ks[4], (DEPTH, d, d), d),
        "rel_bias": 0.5 * jax.random.normal(ks[5], (N_A_LAYERS, N_HEADS, N_REL), jnp.float32),
        "g_pre_ffn": gain(ks[6]),
        "g_post_ffn": gain(ks[7]),
        "w_gate": nrm(ks[8], (DEPTH, d, f), d),
        "w_up": nrm(ks[9], (DEPTH, d, f), d),
        "w_down": nrm(ks[10], (DEPTH, f, d), f),
    }

def second_block(x, g_pre_mix, g_post_mix, w_qkv, w_o, rel_bias, g_pre_ffn, g_post_ffn, w_gate, w_up, w_down):
    for i in range(DEPTH):
        h = rms_norm_2(x, g_pre_mix[i])
        if i % N_MIXERS == 0:
            m = chunk_relpos_attention(h, w_qkv[i], w_o[i], rel_bias[i // N_MIXERS])
        else:
            m = stick_breaking_attention(h, w_qkv[i], w_o[i])
        x = x + rms_norm_2(m, g_post_mix[i])
        h = rms_norm_2(x, g_pre_ffn[i])
        x = x + rms_norm_2(swiglu(h, w_gate[i], w_up[i], w_down[i]), g_post_ffn[i])
    return x


def setup_inputs(seed=0):
    out = dict(first_inputs(seed))
    for name, value in second_inputs(seed + 1).items():
        if name != "x":
            out[name + "_2"] = value
    return out


def reference(
    x, mem, positions, mix_norm_g, w_in, gate_b, q_norm_g, w_uq, kv_norm_g, w_uk, w_uv, pool_w,
    pool_scale, mem_norm_g, w_mem_kv, w_br_pool, w_br_mla, w_br_mem, w_out, ffn_norm_g,
    w_router_group, b_router_group, w_router_expert, b_router_expert, w_gate_e, w_up_e,
    w_down_e, final_norm_g, g_pre_mix_2, g_post_mix_2, w_qkv_2, w_o_2, rel_bias_2, g_pre_ffn_2,
    g_post_ffn_2, w_gate_2, w_up_2, w_down_2,
):
    x = first_block(
        x, mem, positions, mix_norm_g, w_in, gate_b, q_norm_g, w_uq, kv_norm_g, w_uk, w_uv,
        pool_w, pool_scale, mem_norm_g, w_mem_kv, w_br_pool, w_br_mla, w_br_mem, w_out,
        ffn_norm_g, w_router_group, b_router_group, w_router_expert, b_router_expert, w_gate_e,
        w_up_e, w_down_e, final_norm_g,
    )
    return second_block(
        x, g_pre_mix_2, g_post_mix_2, w_qkv_2, w_o_2, rel_bias_2, g_pre_ffn_2, g_post_ffn_2,
        w_gate_2, w_up_2, w_down_2,
    )


_drawn_inputs = setup_inputs


def setup_inputs(seed=0):
    import zlib

    import numpy as np

    out = dict(_drawn_inputs(seed))
    spreads = {}
    factors = {'gate_b': 3.337,
     'mem_norm_g': 2.777,
     'b_router_group': 8.0,
     'b_router_expert': 2.71,
     'g_post_mix_2': 3.501,
     'g_pre_ffn_2': 3.595,
     'g_post_ffn_2': 4.84}
    for name, (base, spread) in spreads.items():
        noise = np.random.default_rng([zlib.crc32(name.encode()), seed]).standard_normal(out[name].shape)
        drawn = base * np.exp(spread * noise) if base else spread * noise
        out[name] = __import__('jax').numpy.asarray(drawn.astype(out[name].dtype))
    for name, factor in factors.items():
        out[name] = (out[name] * factor).astype(out[name].dtype)
    return out
```

```python
from contextlib import ExitStack

import numpy as np

import concourse.bass as bass
from concourse import mybir

F = mybir.dt.float32
FR = mybir.dt.float32r
I32 = mybir.dt.int32
ALU = mybir.AluOpType
ACT = mybir.ActivationFunctionType
AX = mybir.AxisListType.X

P = 128
RAW = 6
PIECES = 4
AHEAD = 3
CAP = 32
NEG = -1.0e30
EPS = 1e-6
MAGIC = 12582912.0
PI_IN = 3.1415925
TWO_PI_1 = 6.28125
TWO_PI_2 = float(np.float32(2 * np.pi - 6.28125))
TWO_PI_3 = float(2 * np.pi - 6.28125 - float(np.float32(2 * np.pi - 6.28125)))

C_ID, C_TRI, C_ONE, C_MASK, C_IOTA, C_RANK, C_INVF, C_END = np.cumsum([0, 128, 128, 1, 384, 32, 32, 32]).tolist()
G_MIX, G_MEM, G_Q, G_KV, G_POOL, G_MIX2, G_FFN2, G_END = np.cumsum([0, 8, 8, 3, 2, 4, 8, 8]).tolist()


def shape_constants():
    c = np.zeros((P, C_END), np.float32)
    c[:, C_ID:C_ID + P] = np.eye(P)
    c[:, C_TRI:C_TRI + P] = np.triu(np.ones((P, P)), 1)
    c[:, C_ONE] = 1.0
    causal = np.where(np.tril(np.ones((P, P))) > 0, 0.0, NEG)
    c[:, C_MASK:C_MASK + P] = causal
    c[:, C_MASK + 2 * P:C_MASK + 3 * P] = causal
    c[:, C_IOTA:C_IOTA + CAP] = np.arange(CAP)
    c[:, C_RANK:C_RANK + 32] = 32 - np.arange(32)
    c[:, C_INVF:C_INVF + 32] = (np.float32(1.0) / (np.float32(10000.0) ** (np.arange(0, 64, 2, dtype=np.float32) / np.float32(64)))).astype(np.float32)
    pool = np.zeros((4, 256, 256), np.float32)
    for g, w in enumerate((2, 4, 8, 16)):
        for s in range(256):
            n = min(s + 1, w)
            pool[g, s + 1 - n:s + 1, s] = np.float32(1.0) / np.float32(n)
            pool[g, s, s] -= 1.0
    pool = np.ascontiguousarray(pool.reshape(4, 2, P, 256).transpose(2, 1, 0, 3)).reshape(P, 2048)
    return c, pool


class Queue:

    def __init__(self, sem, chained):
        self.sem, self.chained, self.items, self.n = sem, chained, [], 0

    def tok(self):
        return (self.sem, self.n)

    def __call__(self, fn, *waits, inc=1, free=False):
        waits = [w for w in waits if w is not None]
        if self.chained and not free and self.n:
            waits.append(self.tok())
        self.items.append((fn, waits, inc))
        self.n += inc
        return self.tok()

    def emit(self, eng):
        seen = {}
        for fn, waits, inc in self.items:
            need = {}
            for sem, val in waits:
                key = id(sem)
                if val > seen.get(key, 0) and val > need.get(key, (None, 0))[1]:
                    need[key] = (sem, val)
            for key, (sem, val) in need.items():
                eng.wait_ge(sem, val)
                seen[key] = val
            ins = fn(eng)
            if inc:
                ins.then_inc(self.sem, inc)


class Banks:

    def __init__(self, tensors):
        self.t, self.free, self.order = tensors, [None] * len(tensors), list(range(len(tensors)))

    def take(self):
        b = self.order.pop(0)
        return b

    def give(self, b, tok):
        self.free[b] = tok
        self.order.append(b)


def build(nc, x, mem, positions, w_in, gate_b, w_uq, w_uk, w_uv, pool_w, w_mem_kv, w_br_pool, w_br_mla,
          w_br_mem, w_out, w_gate_e, w_up_e, w_down_e, w_qkv, w_o, w_gate, w_up, w_down,
          gvec, grow, w_route, b_route, rel_ext, cst, cst_pool, out, force_general=False):
    ctx = ExitStack()
    with ctx:
        def sb(name, shape, dt=F):
            return ctx.enter_context(nc.sbuf_tensor(name, shape, dt))

        def sem(name):
            return ctx.enter_context(nc.semaphore(name))

        pe = Queue(sem("q_pe"), False)
        act = Queue(sem("q_act"), True)
        dve = Queue(sem("q_dve"), True)
        pool = Queue(sem("q_pool"), True)
        sp_items = []

        def sp(fn, *waits):
            sp_items.append((fn, [w for w in waits if w is not None]))

        banks = Banks([ctx.enter_context(nc.psum_tensor(f"ps{i}", [P, 512], F)) for i in range(8)])

        def ps(b):
            return banks.t[b]

        raw = sb("raw", [P, RAW, 2048])
        wh = sb("wh", [P, PIECES, 1024], FR)
        wl = sb("wl", [P, PIECES, 1024], FR)
        fra = sb("fra", [P, 8192], FR)
        hTh, hTl = (fra[:, a:a + 2048].rearrange("p (t n) -> p t n", t=8) for a in (0, 2048))
        mTh, mTl = (fra[:, a:a + 2048].rearrange("p (t n) -> p t n", t=8) for a in (4096, 6144))
        frb = sb("frb", [P, 4096], FR)
        ymh, yml = (frb[:, a:a + 1024].rearrange("p (t n) -> p t n", t=4) for a in (0, 1024))
        yph, ypl = (frb[:, a:a + 1024].rearrange("p (t n) -> p t n", t=4) for a in (2048, 3072))
        X = sb("X", [P, 2, 1024])
        H = sb("H", [P, 2, 1024])
        junk = sb("junk", [P, 1024])
        C = sb("C", [P, C_END])
        G = sb("G", [P, G_END])
        st = sb("st", [P, 96])
        big = sb("big", [P, 9984])
        S = [sb(f"S{i}", [P, 512]) for i in range(3)]
        T = S
        PT = [junk[:, 0:512], junk[:, 512:1024]]
        cs = sb("cs", [P, 2, 2, 32])
        posi = sb("posi", [P, 2], I32)
        gb = sb("gb", [P, 2, 1024])
        rt = sb("rt", [P, 640])
        flag = sb("flag", [P, 1], I32)

        ident = C[:, C_ID:C_ID + P]

        def load(dst, src, *waits):
            s = sem(f"d_{len(sp_items)}")
            sp(lambda e: e.dma_start(dst, src).then_inc(s, 16), *waits)
            return (s, 16)

        d_mem = load(H[:, :, :], mem.rearrange("a (i p) n -> p (a i) n", p=P))
        d_c = load(C[:, :], cst)
        d_g = load(G[:, :], gvec)
        d_x = load(X[:, :, :], x.rearrange("a (i p) n -> p (a i) n", p=P))
        d_pos = load(posi[:, :], positions)

        s_raw = [sem(f"s_raw{i}") for i in range(RAW)]
        raw_free, raw_count, raw_tok = [None] * RAW, [0] * RAW, {}
        units, pieces = [], []
        at = {"unit": 0, "piece": 0, "loaded": 0, "split": 0, "late": None, "late_sp": None}

        def unit(key, src, shape, split):
            units.append((key, src, shape, split))
            if split:
                per = max(1, 1024 // shape[1])
                for a in range(0, shape[0], per):
                    pieces.append((len(units) - 1, a, min(per, shape[0] - a)))

        def raw_view(u):
            k, n = units[u][2]
            return raw[:, u % RAW, 0:k * n].rearrange("p (k n) -> p k n", k=k)

        def issue():
            while at["loaded"] < len(units) and raw_free[at["loaded"] % RAW] != "taken":
                u = at["loaded"]
                key, src, shape, split = units[u]
                if u == at["late"]:
                    at["late_sp"] = len(sp_items)
                if len(src.shape) == 4:
                    parts = [(raw_view(u)[:, a, :].rearrange("p (b c) -> p b c", b=src.shape[2]), src[:, a])
                             for a in range(src.shape[1])]
                else:
                    parts = [(raw_view(u), src)]
                for dst, part in parts:
                    sp(lambda e, dst=dst, part=part, u=u: e.dma_start(dst, part).then_inc(s_raw[u % RAW], 16),
                       raw_free[u % RAW])
                raw_count[u % RAW] += 16 * len(parts)
                raw_tok[u] = (s_raw[u % RAW], raw_count[u % RAW])
                raw_free[u % RAW] = "taken"
                at["loaded"] += 1

        def landed(u):
            return raw_tok[u]

        def release(u, tok):
            raw_free[u % RAW] = tok
            issue()

        wfree = [None] * PIECES
        piece_tok = {}

        def split_upto(n):
            while at["split"] <= min(n, len(pieces) - 1):
                q = at["split"]
                u, a, k = pieces[q]
                if u >= at["loaded"]:
                    return
                if isinstance(wfree[q % PIECES], str):
                    return
                cols = units[u][2][1]
                v = raw_view(u)[:, a:a + k, :]
                h = wh[:, q % PIECES, 0:k * cols].rearrange("p (k n) -> p k n", k=k)
                l = wl[:, q % PIECES, 0:k * cols].rearrange("p (k n) -> p k n", k=k)
                t = act(lambda e, h=h, v=v: e.copy(h, v), landed(u), wfree[q % PIECES], free=True)
                t = dve(lambda e, h=h, l=l, v=v: e.tensor_tensor(l, v, h.bitcast(F), ALU.subtract), t,
                        landed(u), wfree[q % PIECES], free=True)
                wfree[q % PIECES] = "taken"
                piece_tok[q] = (h, l, t)
                at["split"] += 1
                if a + k == units[u][2][0]:
                    release(u, t)

        def next_piece(key):
            q = at["piece"]
            assert units[pieces[q][0]][0] == key, (units[pieces[q][0]][0], key)
            split_upto(q)
            at["piece"] += 1
            return (q,) + piece_tok[q] + pieces[q][1:]

        def done_piece(q, tok):
            wfree[q % PIECES] = tok
            split_upto(q + AHEAD)

        def next_raw(key):
            while units[at["unit"]][3]:
                at["unit"] += 1
            u = at["unit"]
            assert units[u][0] == key, (units[u][0], key)
            assert u < at["loaded"], (u, at["loaded"], key)
            at["unit"] += 1
            return u, raw_view(u), landed(u)

        def k8(w, c0, c1, key, split=True):
            v = w.rearrange("(k p) n -> p k n", p=P)
            nk = v.shape[1]
            for a in range(0, nk, 4):
                unit(key, v[:, a:a + 4, c0:c1], (min(4, nk - a), c1 - c0), split)

        for c in range(2):
            k8(w_mem_kv[0], 512 * c, 512 * c + 512, ("mkv", c))
        k8(w_in[0], 1216, 1728, "xq")
        k8(w_in[0], 512, 896, "qd")
        k8(w_in[0], 896, 1216, "kvd")
        uq = w_uq[0].rearrange("(k p) (h c) -> p k h c", p=P, h=8)
        unit("uqr", uq[:, :, :, 128:192], (3, 512), False)
        for a in range(2):
            unit("uqn", uq[:, :, 4 * a:4 * a + 4, 0:128], (3, 512), False)
        unit("uk", w_uk[0].rearrange("(k p) n -> p k n", p=P), (2, 1024), False)
        unit("uv", w_uv[0].rearrange("(k p) n -> p k n", p=P), (2, 1024), False)
        k8(w_in[0], 0, 512, "pool")
        unit("poolc", cst_pool.rearrange("p (k n) -> p k n", k=8), (8, 256), False)
        unit("poolw", pool_w[0].rearrange("g c d -> c g d"), (4, 128), False)
        for c in range(2):
            for b, w in enumerate((w_br_pool, w_br_mem, w_br_mla)):
                br = (0, 2, 1)[b]
                k8(w[0], 512 * c, 512 * c + 512, ("br", br, c))
                col = 1728 + 1024 * br + 512 * c
                k8(w_in[0], col, col + 512, ("gate", br, c))
        for c in range(2):
            k8(w_out[0], 512 * c, 512 * c + 512, ("out", c))
        for g in range(8):
            for key, w in (("eg", w_gate_e), ("eu", w_up_e)):
                v = w[0, 4 * g:4 * g + 4].rearrange("e (p k) n -> p e (k n)", p=P)
                for t in range(4):
                    unit(key, v[:, :, 512 * t:512 * t + 512], (4, 512), False)
            v = w_down_e[0, 4 * g:4 * g + 4].rearrange("e (k p) n -> p e k n", p=P)
            for c in range(2):
                for t in range(2):
                    unit("ed", v[:, :, t, 512 * c:512 * c + 512], (4, 512), False)
        at["late"] = len(units)
        for c in range(6):
            k8(w_qkv[0], 512 * c, 512 * c + 512, ("qkv", c))
        for c in range(2):
            k8(w_o[0], 512 * c, 512 * c + 512, ("o", c))
        for c in range(11):
            for key, w in (("fg", w_gate), ("fu", w_up)):
                unit((key, c), w[0].rearrange("(k p) n -> p k n", p=P)[:, :, 256 * c:256 * c + 256], (8, 256), True)
            unit(("fd", c), w_down[0, 256 * c:256 * c + 256, :].rearrange("(k p) n -> p k n", p=P), (2, 1024), True)
        issue()

        def group(o, pairs, *waits, check=True):
            t = None
            for n, (a, b) in enumerate(pairs):
                last = n == len(pairs) - 1
                t = pe(lambda e, a=a, b=b, n=n, last=last: e.matmul(
                    o, a, b, start=(n == 0), stop=last, skip_group_check=not check),
                    *(waits if n == 0 else ()), inc=1 if last else 0)
            return t

        def stream_tokens(key, aT, nk, cols, *waits):
            ah, al = aT
            bs = [banks.take() for _ in range(2)]
            first, k0 = list(waits) + [banks.free[b] for b in bs], 0
            while k0 < nk:
                q, h, l, t, _, k = next_piece(key)
                for kk in range(k):
                    for i in range(2):
                        sl = slice(P * i, P * i + P)
                        for n, (a, w) in enumerate(((ah, h), (al, h), (ah, l))):
                            s0, s1 = k0 + kk == 0 and n == 0, k0 + kk == nk - 1 and n == 2
                            end = s1 or (kk == k - 1 and i == 1 and n == 2)
                            tok = pe(lambda e, o=ps(bs[i])[:, 0:cols], a=a[:, k0 + kk, sl], w=w[:, kk, :],
                                     s0=s0, s1=s1: e.matmul(o, a, w, start=s0, stop=s1),
                                     t, *first, inc=1 if end else 0)
                            first = []
                            if s1:
                                last = tok
                done_piece(q, tok)
                k0 += k
            return bs, last

        def stream_features(key, aT, nk, cols, *waits):
            ah, al = aT
            m = cols // P
            bs = [banks.take() for _ in range(m)]
            first, k0 = list(waits) + [banks.free[b] for b in bs], 0
            while k0 < nk:
                q, h, l, t, _, k = next_piece(key)
                for kk in range(k):
                    for j in range(m):
                        sl = slice(P * j, P * j + P)
                        for n, (a, w) in enumerate(((ah, h), (al, h), (ah, l))):
                            s0, s1 = k0 + kk == 0 and n == 0, k0 + kk == nk - 1 and n == 2
                            end = s1 or (kk == k - 1 and j == m - 1 and n == 2)
                            tok = pe(lambda e, o=ps(bs[j])[:, 0:256], a=a[:, k0 + kk, :], w=w[:, kk, sl],
                                     s0=s0, s1=s1: e.matmul(o, w, a, start=s0, stop=s1),
                                     t, *first, inc=1 if end else 0)
                            first = []
                done_piece(q, tok)
                k0 += k
            return bs, tok

        def copy_out(o, b, src, *waits, eng=None):
            t = (eng or act)(lambda e: (e.copy if (eng or act) is act else e.tensor_copy)(o, src), *waits)
            banks.give(b, t)
            return t

        def split_out(oh, ol, b, src, *waits):
            t = act(lambda e: e.copy(oh, src), *waits)
            t = dve(lambda e: e.tensor_tensor(ol, src, oh.bitcast(F), ALU.subtract), t)
            banks.give(b, t)
            return t

        stat = [0]

        def rstd(parts, width, *waits):
            n = len(parts)
            c = 8 * (stat[0] % 10)
            stat[0] += 1
            ss, r = st[:, c:c + n], st[:, c + 4:c + 4 + n]
            t = pool_last[0]
            for i, part in enumerate(parts):
                t = act(lambda e, i=i, part=part: e.activation(junk[:, 0:width], part, ACT.Square,
                                                               accum_out=ss[:, i:i + 1]), t, *waits)
            t = pool(lambda e: e.tensor_scalar(ss, ss, 1.0 / width, EPS, ALU.mult, ALU.add), t, dve.tok())
            t = pool(lambda e: e.tensor_tensor(r, ss, half[:, 0:n], ALU.pow), t)
            pool_last[0] = t
            return [r[:, i:i + 1] for i in range(n)], t

        half = st[:, 88:92]
        pool_last = [pool(lambda e: e.memset(half, -0.5))]

        def transposed(src, nt, gcol, store, *waits):
            t = None
            for i in range(2):
                for a in range(0, nt, 4):
                    k = min(4, nt - a)
                    b = banks.take()
                    for j in range(k):
                        t = pe(lambda e, b=b, i=i, a=a, j=j: e.transpose(
                            ps(b)[:, P * j:P * j + P], src[:, i, P * (a + j):P * (a + j) + P], ident),
                            banks.free[b], *waits, inc=1 if j == k - 1 else 0)
                    v = ps(b)[:, 0:k * P].rearrange("p (k n) -> p k n", k=k)
                    if gcol is None:
                        t = store(b, a, k, i, v, t)
                    else:
                        tb = T[i]
                        tv = tb[:, 0:k * P].rearrange("p (k n) -> p k n", k=k)
                        g = G[:, gcol + a:gcol + a + k].unsqueeze(2).to_broadcast([P, k, P])
                        t = dve(lambda e, tv=tv, v=v, g=g: e.tensor_tensor(tv, v, g, ALU.mult), t, act.tok(), pe.tok())
                        banks.give(b, t)
                        t = store(None, a, k, i, tv, t)
            return t

        def keep_split(dh, dl):
            def store(b, a, k, i, v, t):
                o = [d[:, a:a + k, P * i:P * i + P] for d in (dh, dl)]
                t = act(lambda e: e.copy(o[0], v), t)
                t = dve(lambda e: e.tensor_tensor(o[1], v, o[0].bitcast(F), ALU.subtract), t)
                if b is not None:
                    banks.give(b, t)
                return t
            return store

        def keep(d):
            def store(b, a, k, i, v, t):
                t = act(lambda e: e.copy(d[:, a:a + k, P * i:P * i + P], v), t)
                if b is not None:
                    banks.give(b, t)
                return t
            return store

        def scaled(dst, src, rs, *waits):
            t = None
            for i in range(2):
                t = dve(lambda e, i=i: e.tensor_scalar(dst[:, i, :], src[:, i, :], rs[i], None, ALU.mult), *waits)
            return t

        def attention(heads, scores, soften, values, finish):
            s_free, pt_free = [None] * 3, [None] * 2
            sc, sm, tr = {}, {}, {}
            for step in range(heads + 3):
                if step < heads:
                    sc[step] = scores(step)
                if 2 <= step and step - 2 < heads:
                    h = step - 2
                    parts, t, sb_ = sm.pop(h)
                    b = banks.take()
                    for n, (j, src) in enumerate(parts):
                        t2 = pe(lambda e, b=b, j=j, src=src: e.transpose(ps(b)[:, P * j:P * j + P], src, ident),
                                banks.free[b], t, inc=1 if n == len(parts) - 1 else 0)
                    s_free[h % 3] = t2
                    w = P * len(parts)
                    t3 = act(lambda e, b=b, h=h, w=w: e.copy(PT[h % 2][:, 0:w], ps(b)[:, 0:w]), t2, pt_free[h % 2])
                    banks.give(b, t3)
                    tr[h] = t3
                if step < heads:
                    b, t = sc.pop(step)
                    view, mx, t = soften(step, b, t, S[step % 3], s_free[step % 3])
                    c = 4 * (step % 4)
                    for i in range(2):
                        t = act(lambda e, i=i, view=view, c=c, step=step, mx=mx: e.activation(
                            view[i][1], view[i][0], ACT.Exp, bias=mx[:, i:i + 1], scale=view[i][2],
                            accum_out=rt[:, c + i:c + i + 1]), t)
                    if view[0][3] is not None:
                        banks.give(view[0][3], t)
                    t = dve(lambda e, c=c: e.reciprocal(rt[:, c + 2:c + 4], rt[:, c:c + 2]), t)
                    for i in range(2):
                        t = dve(lambda e, i=i, view=view, c=c: e.tensor_scalar(
                            view[i][1], view[i][1], rt[:, c + 2 + i:c + 3 + i], None, ALU.mult), t)
                    parts = []
                    for i, kt, off in view[2]:
                        parts.append((len(parts), view[i][1][:, P * off:P * off + P]))
                    sm[step] = (parts, t, None)
                if 3 <= step:
                    h = step - 3
                    t = values(h, PT[h % 2], tr.pop(h))
                    pt_free[h % 2] = t
                    finish(h, t)

        fr = [junk[:, 0:64].rearrange("p (i c) -> p i c", i=2), junk[:, 64:128].rearrange("p (i c) -> p i c", i=2)]
        posf = st[:, 92:94]
        t = dve(lambda e: e.tensor_copy(posf, posi[:, :]), d_pos)
        for i in range(2):
            dve(lambda e, i=i: e.tensor_scalar(fr[0][:, i, :], C[:, C_INVF:C_INVF + 32], posf[:, i:i + 1], None,
                                               ALU.mult), d_c)
        for f, shift in ((0, 0.25), (1, 0.0)):
            o = cs[:, f, :, :]
            dve(lambda e, shift=shift: e.tensor_scalar(fr[1], fr[0], float(1 / (2 * np.pi)), shift, ALU.mult, ALU.add))
            dve(lambda e: e.tensor_scalar(fr[1], fr[1], MAGIC, None, ALU.add))
            dve(lambda e: e.tensor_scalar(fr[1], fr[1], -MAGIC, None, ALU.add))
            for n, c in enumerate((TWO_PI_1, TWO_PI_2, TWO_PI_3)):
                src = fr[0] if n == 0 else o
                dve(lambda e, src=src, c=c, o=o: e.scalar_tensor_tensor(o, fr[1], -c, src, ALU.mult, ALU.add))
            if f == 0:
                dve(lambda e, o=o: e.tensor_scalar(o, o, float(np.pi / 2), None, ALU.add))
            dve(lambda e, o=o: e.tensor_scalar(o, o, PI_IN, -PI_IN, ALU.min, ALU.max))
        t_cs = act(lambda e: e.activation(cs[:, :, :, :], cs[:, :, :, :], ACT.Sin), dve.tok())
        cosb = cs[:, 0, :, :]
        sinb = cs[:, 1, :, :]

        rs, t = rstd([H[:, 0, :], H[:, 1, :]], 1024, d_mem, dve.tok())
        t = scaled(H, H, rs, t)
        t_mT = transposed(H, 8, G_MEM, keep_split(mTh, mTl), t, d_c, d_g)
        t_h0 = pe.tok()
        xkT = big[:, 0:1024].rearrange("p (t n) -> p t n", t=4)
        xv = big[:, 1024:2048].rearrange("p (t n) -> p t n", t=2)
        xqT = big[:, 2048:3072].rearrange("p (t n) -> p t n", t=4)
        bs, t = stream_features(("mkv", 0), (mTh, mTl), 8, 512, t_mT, act.tok())
        for j, b in enumerate(bs):
            copy_out(xkT[:, j, :], b, ps(b)[:, 0:256], t)
        rs, t2 = rstd([X[:, 0, :], X[:, 1, :]], 1024, d_x)
        t2 = scaled(H, X, rs, t2, t_h0)
        t_hT = transposed(H, 8, G_MIX, keep_split(hTh, hTl), t2)
        bs, t = stream_tokens(("mkv", 1), (mTh, mTl), 8, 512)
        for i, b in enumerate(bs):
            copy_out(xv[:, i, :], b, ps(b)[:, :], t)
        bs, t = stream_features("xq", (hTh, hTl), 8, 512, t_hT)
        for j, b in enumerate(bs):
            t_xq = copy_out(xqT[:, j, :], b, ps(b)[:, 0:256], t)

        XS = float(128 ** -0.5)

        def x_scores(h):
            b = banks.take()
            for i in range(2):
                t = group(ps(b)[:, 256 * i:256 * i + 256], [(xqT[:, h, P * i:P * i + P], xkT[:, h, :])],
                          banks.free[b], t_xq)
            return b, t

        def x_soften(h, b, t, s, sfree):
            mx = st[:, 80 + 2 * (h % 4):82 + 2 * (h % 4)]
            v = ps(b)[:, :].rearrange("p (i n) -> p i n", i=2)
            dve(lambda e: e.tensor_reduce(mx, v, AX, ALU.max, negate=True), t)
            t = dve(lambda e: e.tensor_scalar(mx, mx, XS, None, ALU.mult), sfree)
            view = [(v[:, i, :], s[:, 256 * i:256 * i + 256], XS, b) for i in range(2)]
            return view + [[(0, 0, 0), (1, 0, 0), (0, 1, 1), (1, 1, 1)]], mx, t

        pv_bank = {}

        def x_values(h, pt, t):
            b = banks.take()
            pv_bank[h] = b
            return group(ps(b)[:, 0:256], [(xv[:, k, P * h:P * h + P], pt[:, 256 * k:256 * k + 256]) for k in range(2)],
                         banks.free[b], t)

        def x_finish(h, t):
            b = pv_bank.pop(h)
            split_out(ymh[:, h, :], yml[:, h, :], b, ps(b)[:, 0:256], t)

        attention(4, x_scores, x_soften, x_values, x_finish)

        latent = S[0][:, 0:384]
        cqT = big[:, 3072:3840].rearrange("p (t n) -> p t n", t=3)
        ckT = big[:, 3840:4352].rearrange("p (t n) -> p t n", t=2)
        krT = [big[:, 4352 + 256 * a:4608 + 256 * a] for a in range(2)]
        qrT = big[:, 4864:5888].rearrange("p (t n) -> p t n", t=4)
        qnT = big[:, 5888:7936].rearrange("p (t n) -> p t n", t=8)
        knT = big[:, 7936:9984].rearrange("p (t n) -> p t n", t=8)
        vv = H
        lat = junk[:, 0:768].rearrange("p (i n) -> p i n", i=2)

        bs, t = stream_tokens("qd", (hTh, hTl), 8, 384)
        rs, t = rstd([ps(b)[:, 0:384] for b in bs], 384, t)
        for i, b in enumerate(bs):
            t2 = dve(lambda e, i=i, b=b, rs=rs: e.tensor_scalar(lat[:, i, :], ps(b)[:, 0:384], rs[i], None, ALU.mult), t, act.tok())
            banks.give(b, t2)
        transposed(lat, 3, G_Q, keep(cqT), t2)
        t_cq = act.tok()

        bs, t = stream_tokens("kvd", (hTh, hTl), 8, 320)
        rs, t = rstd([ps(b)[:, 0:256] for b in bs], 256, t, pe.tok())
        lat2 = junk[:, 0:512].rearrange("p (i n) -> p i n", i=2)
        rot_tmp = T[2]
        kr = junk[:, 512:768].rearrange("p (i n) -> p i n", i=2)
        for i, b in enumerate(bs):
            src = ps(b)
            dve(lambda e, i=i, src=src, rs=rs: e.tensor_scalar(lat2[:, i, :], src[:, 0:256], rs[i], None, ALU.mult),
                t, t_cs, pe.tok())
            x1, x2 = src[:, 256:288], src[:, 288:320]
            ct, sn = cosb[:, i, :], sinb[:, i, :]
            tm = rot_tmp[:, 0:128]
            dve(lambda e, x1=x1, ct=ct, tm=tm: e.tensor_tensor(tm[:, 0:32], x1, ct, ALU.mult))
            dve(lambda e, x2=x2, sn=sn, tm=tm: e.tensor_tensor(tm[:, 32:64], x2, sn, ALU.mult), free=True)
            dve(lambda e, x2=x2, ct=ct, tm=tm: e.tensor_tensor(tm[:, 64:96], x2, ct, ALU.mult), free=True)
            t2 = dve(lambda e, x1=x1, sn=sn, tm=tm: e.tensor_tensor(tm[:, 96:128], x1, sn, ALU.mult), free=True)
            banks.give(b, t2)
            for z in (0, 64):
                dve(lambda e, i=i, tm=tm, z=z: e.tensor_tensor(kr[:, i, z:z + 32], tm[:, 0:32], tm[:, 32:64], ALU.subtract))
                t2 = dve(lambda e, i=i, tm=tm, z=z: e.tensor_tensor(kr[:, i, z + 32:z + 64], tm[:, 64:96], tm[:, 96:128], ALU.add))
        transposed(lat2, 2, G_KV, keep(ckT), t2)
        b = banks.take()
        for i in range(2):
            t = pe(lambda e, i=i, b=b: e.transpose(ps(b)[:, P * i:P * i + P], kr[:, i, :], ident), banks.free[b], t2,
                   inc=i)
        dve(lambda e: e.memset(krT[0][64:128, :], 0.0))
        dve(lambda e: e.memset(krT[1][0:64, :], 0.0))
        dve(lambda e, b=b: e.tensor_copy(krT[0][0:64, :], ps(b)[0:64, 0:256]), t)
        t_kr = dve(lambda e, b=b: e.tensor_copy(krT[1][64:128, :], ps(b)[64:128, 0:256]), t)
        banks.give(b, t_kr)
        t_ck = act.tok()

        u, w, tw = next_raw("uqr")
        for i in range(2):
            b = banks.take()
            t = group(ps(b)[:, :], [(cqT[:, k, P * i:P * i + P], w[:, k, :]) for k in range(3)], banks.free[b], t_cq, tw)
            v = ps(b)[:, :].rearrange("p (h c) -> p h c", h=8)
            x1, x2 = v[:, :, 0:32], v[:, :, 32:64]
            ct = cosb[:, i, :].unsqueeze(1).to_broadcast([P, 8, 32])
            sn = sinb[:, i, :].unsqueeze(1).to_broadcast([P, 8, 32])
            ta, tb = (T[z][:, 0:256].rearrange("p (h c) -> p h c", h=8) for z in (0, 1))
            tc, td = (T[z][:, 256:512].rearrange("p (h c) -> p h c", h=8) for z in (0, 1))
            o = T[2][:, :].rearrange("p (h c) -> p h c", h=8)
            dve(lambda e, x1=x1, ct=ct, ta=ta: e.tensor_tensor(ta, x1, ct, ALU.mult), t, act.tok())
            dve(lambda e, x2=x2, sn=sn, tb=tb: e.tensor_tensor(tb, x2, sn, ALU.mult), free=True)
            dve(lambda e, x2=x2, ct=ct, tc=tc: e.tensor_tensor(tc, x2, ct, ALU.mult), free=True)
            t2 = dve(lambda e, x1=x1, sn=sn, td=td: e.tensor_tensor(td, x1, sn, ALU.mult), free=True)
            banks.give(b, t2)
            dve(lambda e, o=o, ta=ta, tb=tb: e.tensor_tensor(o[:, :, 0:32], ta, tb, ALU.subtract), pe.tok())
            t2 = dve(lambda e, o=o, tc=tc, td=td: e.tensor_tensor(o[:, :, 32:64], tc, td, ALU.add))
            b = banks.take()
            for j in range(4):
                t = pe(lambda e, b=b, j=j: e.transpose(ps(b)[:, P * j:P * j + P], T[2][:, P * j:P * j + P], ident),
                       banks.free[b], t2, inc=1 if j == 3 else 0)
            t_qr = copy_out(qrT[:, :, P * i:P * i + P], b, ps(b)[:, :].rearrange("p (j n) -> p j n", j=4), t)
        release(u, t)
        for a in range(2):
            u, w, tw = next_raw("uqn")
            for j in range(4):
                b = banks.take()
                t = group(ps(b)[:, 0:256], [(w[:, k, P * j:P * j + P], cqT[:, k, :]) for k in range(3)],
                          banks.free[b], tw)
                t_qn = copy_out(qnT[:, 4 * a + j, :], b, ps(b)[:, 0:256], t)
            release(u, t)
        u, w, tw = next_raw("uk")
        for j in range(8):
            b = banks.take()
            t = group(ps(b)[:, 0:256], [(w[:, k, P * j:P * j + P], ckT[:, k, :]) for k in range(2)],
                      banks.free[b], tw, t_ck)
            t_kn = copy_out(knT[:, j, :], b, ps(b)[:, 0:256], t)
        release(u, t)
        u, w, tw = next_raw("uv")
        for i in range(2):
            for c in range(2):
                b = banks.take()
                t = group(ps(b)[:, :], [(ckT[:, k, P * i:P * i + P], w[:, k, 512 * c:512 * c + 512]) for k in range(2)],
                          banks.free[b], tw)
                t_v = copy_out(vv[:, i, 512 * c:512 * c + 512], b, ps(b)[:, :], t)
        release(u, t)

        MS = float(192 ** -0.5)

        def m_scores(h):
            b = banks.take()
            for i in range(2):
                o = ps(b)[:, 0:128] if i == 0 else ps(b)[:, 128:384]
                n = P * (i + 1)
                sl = slice(P * i, P * i + P)
                t = group(o, [(qnT[:, h, sl], knT[:, h, 0:n]), (qrT[:, h // 2, sl], krT[h % 2][:, 0:n])],
                          banks.free[b], t_v, t_kr)
            return b, t

        def m_soften(h, b, t, s, sfree):
            mx = st[:, 80 + 2 * (h % 4):82 + 2 * (h % 4)]
            t = dve(lambda e: e.scalar_tensor_tensor(s[:, 0:384], ps(b)[:, 0:384], MS, C[:, C_MASK:C_MASK + 384],
                                                     ALU.mult, ALU.add), t, sfree)
            banks.give(b, t)
            dve(lambda e: e.tensor_reduce(mx[:, 0:1], s[:, 0:128], AX, ALU.max, negate=True))
            t = dve(lambda e: e.tensor_reduce(mx[:, 1:2], s[:, 128:384], AX, ALU.max, negate=True))
            return causal_view(s), mx, t

        def causal_view(s):
            return [(s[:, 0:128], s[:, 0:128], 1.0, None), (s[:, 128:384], s[:, 128:384], 1.0, None),
                    [(0, 0, 0), (1, 0, 0), (1, 1, 1)]]

        def causal_values(o, w, pt, b, t):
            pe(lambda e: e.matmul(o, w(0), pt[:, 0:256], start=True, stop=False), banks.free[b], t, inc=0)
            return pe(lambda e: e.matmul(o[:, 128:256], w(1), pt[:, 256:384], start=False, stop=True))

        def m_values(h, pt, t):
            b = banks.take()
            pv_bank[h] = b
            return causal_values(ps(b)[:, 0:256], lambda k: vv[:, k, P * h:P * h + P], pt, b, t)

        def m_finish(h, t):
            b = pv_bank.pop(h)
            split_out(mTh[:, h, :], mTl[:, h, :], b, ps(b)[:, 0:256], t)

        attention(8, m_scores, m_soften, m_values, m_finish)
        t_mla = dve.tok()

        uu = big[:, 0:1024].rearrange("p (i n) -> p i n", i=2)
        pT = big[:, 1024:2048].rearrange("p (g n) -> p g n", g=4)
        bs, t = stream_tokens("pool", (hTh, hTl), 8, 512)
        for i, b in enumerate(bs):
            t_u = copy_out(uu[:, i, :], b, ps(b)[:, :], t, pe.tok())
        u, w, tw = next_raw("poolc")
        u2, w2, tw2 = next_raw("poolw")
        for g in range(4):
            b = banks.take()
            t = group(ps(b)[:, 0:256], [(uu[:, k, P * g:P * g + P], w[:, 4 * k + g, :]) for k in range(2)],
                      banks.free[b], t_u, tw)
            t = copy_out(pT[:, g, :], b, ps(b)[:, 0:256], t)
            b = banks.take()
            t = group(ps(b)[:, 0:256], [(w2[:, g, :], pT[:, g, :])], banks.free[b], t, tw2)
            tv = T[g % 2][:, 0:256]
            t = dve(lambda e, tv=tv, b=b, g=g: e.tensor_scalar(tv, ps(b)[:, 0:256], G[:, G_POOL + g:G_POOL + g + 1],
                                                               None, ALU.mult), t, act.tok())
            banks.give(b, t)
            t = act(lambda e, tv=tv, g=g: e.copy(yph[:, g, :], tv), t)
            dve(lambda e, tv=tv, g=g: e.tensor_tensor(ypl[:, g, :], tv, yph[:, g, :].bitcast(F), ALU.subtract), t)
        release(u, pe.tok())
        release(u2, pe.tok())
        t_yp = dve.tok()

        gbt = [gb[:, 0, 0:512], gb[:, 0, 512:1024]]
        gb_free = [None, None]
        n_gate = 0
        merged = H
        t_vdone = pe.tok()
        for c in range(2):
            for br in (0, 2, 1):
                src = gate_b[0, br:br + 1, 512 * c:512 * c + 512].to_broadcast([P, 512])
                t_gb = load(gbt[n_gate % 2], src, gb_free[n_gate % 2])
                y = {0: (yph, ypl), 1: (mTh, mTl), 2: (ymh, yml)}[br]
                bb, t_b = stream_tokens(("br", br, c), y, 4 if br != 1 else 8, 512, t_yp)
                bg, t_g = stream_tokens(("gate", br, c), (hTh, hTl), 8, 512)
                for i in range(2):
                    s = S[i]
                    t = dve(lambda e, s=s, b=bg[i], n=n_gate: e.tensor_tensor(s[:, :], ps(b)[:, :], gbt[n % 2], ALU.add),
                            t_g, t_gb, t_vdone)
                    gb_free[n_gate % 2] = t
                    banks.give(bg[i], t)
                    t = act(lambda e, s=s: e.activation(s[:, :], s[:, :], ACT.Sigmoid), t)
                    m = merged[:, i, 512 * c:512 * c + 512]
                    if br == 0:
                        t = dve(lambda e, s=s, b=bb[i], m=m: e.tensor_tensor(m, s[:, :], ps(b)[:, :], ALU.mult), t, t_b)
                        banks.give(bb[i], t)
                    else:
                        t = dve(lambda e, s=s, b=bb[i]: e.tensor_tensor(s[:, :], s[:, :], ps(b)[:, :], ALU.mult), t, t_b)
                        banks.give(bb[i], t)
                        t = dve(lambda e, s=s, m=m: e.tensor_tensor(m, m, s[:, :], ALU.add))
                n_gate += 1
        t_sb = dve.tok()
        t = transposed(merged, 8, None, keep_split(hTh, hTl), t_sb)
        d_gffn = load(gb[:, 0, :], grow[0:1, :].to_broadcast([P, 1024]), t_sb)
        d_gfin = load(gb[:, 1, :], grow[1:2, :].to_broadcast([P, 1024]))
        wr = big[:, 0:288].rearrange("p (k n) -> p k n", k=8)
        d_wr = load(wr, w_route.rearrange("p (k n) -> p k n", k=8), t_vdone)
        d_br = load(rt[:, 0:36], b_route.to_broadcast([P, 36]), dve.tok())
        for c in range(2):
            bs, tt = stream_tokens(("out", c), (hTh, hTl), 8, 512, t)
            for i, b in enumerate(bs):
                xs = X[:, i, 512 * c:512 * c + 512]
                t2 = dve(lambda e, xs=xs, b=b: e.tensor_tensor(xs, xs, ps(b)[:, :], ALU.add), tt)
                banks.give(b, t2)

        h2T = big[:, 512:2560].rearrange("p (t n) -> p t n", t=8)
        rs, t = rstd([X[:, 0, :], X[:, 1, :]], 1024, t2)
        HN = big[:, 2560:4608].rearrange("p (i n) -> p i n", i=2)
        scaled(HN, X, rs, t, pe.tok())
        for i in range(2):
            t = dve(lambda e, i=i: e.tensor_tensor(
                H[:, i, :].rearrange("p (k c) -> p k c", k=8), HN[:, i, :].rearrange("p (c k) -> p k c", k=8),
                gb[:, 0, :].rearrange("p (c k) -> p k c", k=8), ALU.mult), d_gffn)
        t_h2 = t
        t = transposed(H, 8, None, keep(h2T), t, d_wr)
        b = banks.take()
        for i in range(2):
            t = group(ps(b)[:, 64 * i:64 * i + 36], [(h2T[:, k, P * i:P * i + P], wr[:, k, :]) for k in range(8)],
                      banks.free[b], act.tok())
        R = rt[:, 64:640]

        def col(a, n):
            return R[:, a:a + n]

        def v2(a, n):
            return R[:, a:a + 2 * n].rearrange("p (i n) -> p i n", i=2)

        L, OG, EM, O1, O2, M, W, PX = v2(0, 36), v2(72, 4), v2(80, 32), v2(144, 32), v2(208, 32), v2(272, 32), v2(336, 32), v2(400, 32)
        E4, TT = v2(464, 4), v2(472, 32)
        g1, gs, m1, m2, tm_, pg, ex = (v2(536 + 2 * n, 1) for n in range(7))
        rank = C[:, C_RANK:C_RANK + 32].unsqueeze(1).to_broadcast([P, 2, 32])

        def bc(a, n):
            return a.to_broadcast([P, 2, n])

        dve(lambda e, b=b: e.tensor_tensor(L, ps(b)[:, 0:128].rearrange("p (i n) -> p i n", i=2)[:, :, 0:36],
                                           rt[:, 0:36].unsqueeze(1).to_broadcast([P, 2, 36]), ALU.add), t, d_br)
        banks.give(b, dve.tok())
        gl, el = L[:, :, 0:4], L[:, :, 4:36]

        def pick(vals, top, onehot, tmp, n):
            dve(lambda e: e.tensor_reduce(top, vals, AX, ALU.max))
            dve(lambda e: e.tensor_tensor(tmp, vals, bc(top, n), ALU.is_equal))
            dve(lambda e: e.tensor_tensor(tmp, tmp, rank[:, :, 0:n], ALU.mult))
            dve(lambda e: e.tensor_reduce(tm_, tmp, AX, ALU.max))
            dve(lambda e: e.tensor_tensor(onehot, tmp, bc(tm_, n), ALU.is_equal))

        pick(gl, g1, OG, E4, 4)
        dve(lambda e: e.tensor_tensor(E4, gl, bc(g1, 4), ALU.subtract))
        t = act(lambda e: e.activation(E4, E4, ACT.Exp), dve.tok())
        dve(lambda e: e.tensor_reduce(gs, E4, AX, ALU.add), t)
        dve(lambda e: e.reciprocal(pg, gs))
        dve(lambda e: e.tensor_scalar(OG, OG, -NEG, NEG, ALU.mult, ALU.add))
        for i in range(2):
            dve(lambda e, i=i: e.tensor_tensor(EM[:, i, :].rearrange("p (g k) -> p g k", g=4),
                                               el[:, i, :].rearrange("p (g k) -> p g k", g=4),
                                               OG[:, i, :].unsqueeze(2).to_broadcast([P, 4, 8]), ALU.add))
        pick(EM, m1, O1, TT, 32)
        dve(lambda e: e.tensor_scalar(TT, O1, 2 * NEG, None, ALU.mult))
        dve(lambda e: e.tensor_tensor(EM, EM, TT, ALU.add))
        pick(EM, m2, O2, TT, 32)
        dve(lambda e: e.tensor_tensor(ex, m2, m1, ALU.subtract))
        t = act(lambda e: e.activation(ex, ex, ACT.Exp), dve.tok())
        dve(lambda e: e.tensor_scalar(gs, ex, 1.0, None, ALU.add), t)
        dve(lambda e: e.reciprocal(gs, gs))
        dve(lambda e: e.tensor_tensor(m1, pg, gs, ALU.mult))
        dve(lambda e: e.tensor_tensor(m2, m1, ex, ALU.mult))
        t_M = dve(lambda e: e.tensor_tensor(M, O1, O2, ALU.add))
        dve(lambda e: e.tensor_tensor(O1, O1, bc(m1, 32), ALU.mult))
        dve(lambda e: e.tensor_tensor(O2, O2, bc(m2, 32), ALU.mult))
        t_W = dve(lambda e: e.tensor_tensor(W, O1, O2, ALU.add))
        tri, ones = C[:, C_TRI:C_TRI + P], C[:, C_ONE:C_ONE + 1].to_broadcast([P, P])
        b = banks.take()
        group(ps(b)[:, 0:32], [(tri, M[:, 0, :])], banks.free[b], t_M)
        group(ps(b)[:, 32:64], [(ones, M[:, 0, :]), (tri, M[:, 1, :])])
        t = group(ps(b)[:, 64:96], [(ones, M[:, 0, :]), (ones, M[:, 1, :])])
        dve(lambda e: e.tensor_scalar(PX, M, -1000.0, 1000.0, ALU.mult, ALU.add), t)
        dve(lambda e, b=b: e.tensor_tensor(PX, PX, ps(b)[:, 0:64].rearrange("p (i n) -> p i n", i=2), ALU.add))
        t_px = dve.tok()
        dve(lambda e, b=b: e.tensor_reduce(TT[:, 0, 0:1], ps(b)[:, 64:96], AX, ALU.max))
        banks.give(b, dve.tok())
        t_flag = dve(lambda e: e.tensor_copy(flag[:, :], TT[:, 0, 0:1]))

        MO = big[:, 2560:4608].rearrange("p (i n) -> p i n", i=2)
        sel = [big[:, 4608 + 512 * z:5120 + 512 * z] for z in range(2)]
        XE = [big[:, 5632 + 1024 * z:6656 + 1024 * z].rearrange("p (t n) -> p t n", t=8) for z in range(2)]
        CM = [big[:, 7680 + 256 * z:7936 + 256 * z] for z in range(2)]
        YE = big[:, 8192:9216]
        AE = [T[0][:, 0:256], T[1][:, 0:256]]
        AT = [S[0][:, 256:512], S[1][:, 256:512]]
        xe_tok, cm_tok = {}, {}
        iota = C[:, C_IOTA:C_IOTA + CAP]

        def select(g):
            z = g % 2
            for i in range(2):
                s_ = sel[z][:, 128 * i:128 * i + 128].rearrange("p (e s) -> p e s", e=4)
                w_ = sel[z][:, 256 + 128 * i:384 + 128 * i].rearrange("p (e s) -> p e s", e=4)
                px = PX[:, i, 4 * g:4 * g + 4].unsqueeze(2).to_broadcast([P, 4, CAP])
                wt = W[:, i, 4 * g:4 * g + 4].unsqueeze(2).to_broadcast([P, 4, CAP])
                io = iota.unsqueeze(1).to_broadcast([P, 4, CAP])
                dve(lambda e, s_=s_, px=px, io=io: e.tensor_tensor(s_, io, px, ALU.is_equal), sel_free[z])
                t = dve(lambda e, s_=s_, w_=w_, wt=wt: e.tensor_tensor(w_, s_, wt, ALU.mult))
            return t

        sel_free = [None, None]

        def gather(g, t):
            z = g % 2
            for a in range(2):
                b = banks.take()
                for j in range(4):
                    tt = group(ps(b)[:, P * j:P * j + P],
                               [(H[:, i, P * (4 * a + j):P * (4 * a + j) + P], sel[z][:, P * i:P * i + P]) for i in range(2)],
                               banks.free[b], t, t_h2)
                t3 = copy_out(XE[z][:, 4 * a:4 * a + 4, :], b, ps(b)[:, :].rearrange("p (j n) -> p j n", j=4), tt,
                              xe_free[z])
            b = banks.take()
            for i in range(2):
                tt = pe(lambda e, b=b, i=i: e.transpose(ps(b)[:, P * i:P * i + P], sel[z][:, 256 + P * i:384 + P * i], ident),
                        banks.free[b], inc=i)
            sel_free[z] = tt
            xe_tok[g] = copy_out(CM[z], b, ps(b)[:, 0:256], tt, cm_free[z])

        xe_free, cm_free = [None, None], [None, None]

        def experts(g):
            z = g % 2
            b = banks.take()
            for half_ in range(2):
                for t4 in range(4):
                    u, w, tw = next_raw(("eg", "eu")[half_])
                    w = w.rearrange("p e (k n) -> p e k n", k=2)
                    for k in range(2):
                        kk = 2 * t4 + k
                        for j in range(4):
                            end = k == 1 and j == 3
                            t = pe(lambda e, w=w, k=k, kk=kk, j=j, half_=half_: e.matmul(
                                ps(b)[32 * j:32 * j + 32, 256 * half_:256 * half_ + 256],
                                XE[z][:, kk, 32 * j:32 * j + 32], w[:, j, k, :], start=(kk == 0), stop=(kk == 7)),
                                banks.free[b], tw, xe_tok[g], inc=1 if end else 0)
                    release(u, t)
            xe_free[z] = t
            a_, at_ = AE[z], AT[z]
            t2 = act(lambda e: e.activation(a_, ps(b)[:, 0:256], ACT.Silu), t, dve.tok())
            t2 = dve(lambda e: e.tensor_tensor(a_, a_, ps(b)[:, 256:512], ALU.mult), t2)
            banks.give(b, t2)
            return t2

        def experts_down(g, t2):
            z = g % 2
            a_, at_ = AE[z], AT[z]
            b = banks.take()
            for k in range(2):
                t = pe(lambda e, b=b, k=k: e.transpose(ps(b)[:, P * k:P * k + P], a_[:, P * k:P * k + P], ident),
                       banks.free[b], t2, inc=k)
            t = copy_out(at_, b, ps(b)[:, 0:256], t)
            for c in range(2):
                b = banks.take()
                for k in range(2):
                    u, w, tw = next_raw("ed")
                    for j in range(4):
                        tt = pe(lambda e, b=b, w=w, k=k, j=j: e.matmul(
                            ps(b)[32 * j:32 * j + 32, :], at_[:, P * k + 32 * j:P * k + 32 * j + 32], w[:, j, :],
                            start=(k == 0), stop=(k == 1)), banks.free[b], tw, t, inc=1 if j == 3 else 0)
                    release(u, tt)
                t_y = copy_out(YE[:, 512 * c:512 * c + 512], b, ps(b)[:, :], tt, ye_free[0])
            return t_y

        ye_free = [None]

        def combine(g, t_y):
            z = g % 2
            for i in range(2):
                for c in range(2):
                    b = banks.take()
                    t = group(ps(b)[:, :], [(CM[z][:, P * i:P * i + P], YE[:, 512 * c:512 * c + 512])], banks.free[b], t_y)
                    o = MO[:, i, 512 * c:512 * c + 512]
                    if g == 0:
                        t = dve(lambda e, o=o, b=b: e.tensor_copy(o, ps(b)[:, :]), t)
                    else:
                        t = dve(lambda e, o=o, b=b: e.tensor_tensor(o, o, ps(b)[:, :], ALU.add), t)
                    banks.give(b, t)
            ye_free[0] = cm_free[z] = pe.tok()

        gather(0, select(0))
        for g in range(8):
            if g < 7:
                t_s = select(g + 1)
            t2 = experts(g)
            if g < 7:
                gather(g + 1, t_s)
            combine(g, experts_down(g, t2))

        fast = {q: q.n for q in (pe, act, dve)}
        marks = {q: len(q.items) for q in (pe, act, dve)}
        f_go, f_w, f_g, f_s, f_a, f_y, f_end = (sem(n) for n in ("f_go", "f_w", "f_g", "f_s", "f_a", "f_y", "f_end"))
        fast_pe, fast_dve = pe.tok(), dve.tok()
        AG = junk[:, 0:512].rearrange("p (k n) -> p k n", k=2)
        WC = T[0][:, 0:64].rearrange("p (i n) -> p i n", i=2)
        WD = T[0][:, 64:128].rearrange("p (i n) -> p i n", i=2)
        limit = -1 if force_general else CAP

        def general(eng, body):
            eng.wait_ge(*t_flag)
            n = eng.value_load(flag[0:1, 0:1], min_val=0, max_val=256)
            with eng.If(n > limit):
                body(eng)

        wg_, wu_, wd_ = raw[:, 0, :], raw[:, 1, :], raw[:, 2, :]

        def general_sp(e):
            e.wait_ge(*fast_dve)
            e.wait_ge(*fast_pe)
            with e.Fori(0, 32) as n:
                e.wait_ge(f_go, 1)
                e.sem_clear(f_go)
                e.dma_start(wg_, w_gate_e[0, bass.ds(n, 1)].rearrange("e (p k) n -> p (e k n)", p=P)).then_inc(f_w, 16)
                e.dma_start(wu_, w_up_e[0, bass.ds(n, 1)].rearrange("e (p k) n -> p (e k n)", p=P)).then_inc(f_w, 16)
                e.dma_start(wd_.rearrange("p (k n) -> p k n", k=2),
                            w_down_e[0, bass.ds(n, 1)].rearrange("e (k p) n -> p (e k) n", p=P)).then_inc(f_w, 16)
            e.wait_ge(f_go, 1)

        def general_pe(e):
            wg, wu = (v.rearrange("p (k n) -> p k n", k=8) for v in (wg_, wu_))
            wd = wd_.rearrange("p (k n) -> p k n", k=2)
            with e.Fori(0, 32):
                e.wait_ge(f_w, 48)
                e.sem_clear(f_w)
                for s_, w in enumerate((wg, wu)):
                    for j in range(2):
                        for k in range(8):
                            t = e.matmul(ps(s_)[:, 256 * j:256 * j + 256], w[:, k, P * j:P * j + P], h2T[:, k, :],
                                         start=(k == 0), stop=(k == 7))
                t.then_inc(f_g, 1)
                e.wait_ge(f_a, 1)
                e.sem_clear(f_a)
                for i in range(2):
                    for c in range(2):
                        for k in range(2):
                            t = e.matmul(ps(2 + 2 * i + c)[:, :], AG[:, k, P * i:P * i + P],
                                         wd[:, k, 512 * c:512 * c + 512], start=(k == 0), stop=(k == 1))
                t.then_inc(f_y, 1)

        def general_act(e):
            with e.Fori(0, 32):
                e.wait_ge(f_g, 1)
                e.sem_clear(f_g)
                e.activation(AG, ps(0)[:, :].rearrange("p (k n) -> p k n", k=2), ACT.Silu).then_inc(f_s, 1)

        def general_dve(e):
            chain = [0]
            e.wait_ge(*fast_pe)
            e.wait_ge(act.sem, fast[act])
            e.wait_ge(*fast_dve)
            e.tensor_copy(WC, W).then_inc(f_end, 1)
            e.wait_ge(f_end, 1)
            e.memset(MO, 0.0).then_inc(f_end, 1)
            e.wait_ge(f_end, 2)
            e.sem_clear(f_end)
            with e.Fori(0, 32):
                e.sem_inc(f_go, 1)
                e.wait_ge(f_s, 1)
                e.sem_clear(f_s)
                e.tensor_tensor(AG, AG, ps(1)[:, :].rearrange("p (k n) -> p k n", k=2), ALU.mult).then_inc(f_a, 1)
                e.wait_ge(f_y, 1)
                e.sem_clear(f_y)
                for i in range(2):
                    for c in range(2):
                        o = MO[:, i, 512 * c:512 * c + 512]
                        e.scalar_tensor_tensor(o, ps(2 + 2 * i + c)[:, :], WC[:, i, 0:1], o, ALU.mult,
                                               ALU.add).then_inc(f_end, 1)
                e.tensor_copy(WD[:, :, 0:31], WC[:, :, 1:32]).then_inc(f_end, 1)
                e.wait_ge(f_end, 5)
                e.tensor_copy(WC[:, :, 0:31], WD[:, :, 0:31]).then_inc(f_end, 1)
                e.wait_ge(f_end, 6)
                e.sem_clear(f_end)
            e.sem_inc(f_go, 1)

        for i in range(2):
            t = dve(lambda e, i=i: e.tensor_tensor(X[:, i, :], X[:, i, :], MO[:, i, :], ALU.add))
        rs, t = rstd([X[:, 0, :], X[:, 1, :]], 1024, t)
        scaled(X, X, rs, t)
        for i in range(2):
            t = dve(lambda e, i=i: e.tensor_tensor(X[:, i, :], X[:, i, :], gb[:, 1, :], ALU.mult), d_gfin)
        d_pm = load(gb[:, 0, :], grow[2:3, :].to_broadcast([P, 1024]), t)
        d_pf = load(gb[:, 1, :], grow[3:4, :].to_broadcast([P, 1024]))
        rs, t = rstd([X[:, 0, :], X[:, 1, :]], 1024, t)
        t = scaled(H, X, rs, t, pe.tok())
        t = transposed(H, 8, G_MIX2, keep_split(hTh, hTl), t)
        bias = big[:, 0:4096].rearrange("p (h n) -> p h n", h=16)
        d_bias = load(bias, rel_ext, dve.tok(), pe.tok())
        t_bias = pool(lambda e: e.memset(bias[0:64, :, 192:256], NEG), d_bias)
        qT = big[:, 4096:6144].rearrange("p (t n) -> p t n", t=8)
        kT = big[:, 6144:8192].rearrange("p (t n) -> p t n", t=8)
        v2_ = H
        for c in range(4):
            bs, tt = stream_features(("qkv", c), (hTh, hTl), 8, 512, t)
            for j, b in enumerate(bs):
                d = (qT, kT)[c // 2][:, 4 * (c % 2) + j, :]
                copy_out(d, b, ps(b)[:, 0:256], tt)
        for c in range(2):
            bs, tt = stream_tokens(("qkv", 4 + c), (hTh, hTl), 8, 512)
            for i, b in enumerate(bs):
                t_q = copy_out(v2_[:, i, 512 * c:512 * c + 512], b, ps(b)[:, :], tt)

        def r_scores(h):
            b = banks.take()
            o = 64 * (h % 2)
            for i in range(2):
                t = group(ps(b)[:, 0:128] if i == 0 else ps(b)[:, 128:384],
                          [(qT[o:o + 64, h // 2, P * i:P * i + P], kT[o:o + 64, h // 2, 0:P * (i + 1)])],
                          banks.free[b], t_q)
            return b, t

        def r_soften(h, b, t, s, sfree):
            mx = st[:, 80 + 2 * (h % 4):82 + 2 * (h % 4)]
            dve(lambda e: e.scalar_tensor_tensor(s[:, 0:128], ps(b)[:, 0:128], 0.125, bias[:, h, 128:256], ALU.mult,
                                                 ALU.add), t, sfree, t_bias)
            t = dve(lambda e: e.scalar_tensor_tensor(s[:, 128:384], ps(b)[:, 128:384], 0.125, bias[:, h, :], ALU.mult,
                                                     ALU.add), free=True)
            banks.give(b, t)
            dve(lambda e: e.tensor_reduce(mx[:, 0:1], s[:, 0:128], AX, ALU.max, negate=True))
            t = dve(lambda e: e.tensor_reduce(mx[:, 1:2], s[:, 128:384], AX, ALU.max, negate=True))
            return causal_view(s), mx, t

        def r_values(h, pt, t):
            if h % 2 == 0:
                pv_bank[0] = banks.take()
            b = pv_bank[0]
            o = 64 * (h % 2)
            return causal_values(ps(b)[o:o + 64, 0:256], lambda k: v2_[:, k, 64 * h:64 * h + 64], pt, b, t)

        def r_finish(h, t):
            if h % 2:
                b = pv_bank[0]
                split_out(mTh[:, h // 2, :], mTl[:, h // 2, :], b, ps(b)[:, 0:256], t)

        attention(16, r_scores, r_soften, r_values, r_finish)
        t_o = dve.tok()
        for c in range(2):
            bs, tt = stream_tokens(("o", c), (mTh, mTl), 8, 512, t_o)
            for i, b in enumerate(bs):
                t = copy_out(H[:, i, 512 * c:512 * c + 512], b, ps(b)[:, :], tt)

        def add_normed(row, d_row):
            rs, t = rstd([H[:, 0, :], H[:, 1, :]], 1024, act.tok(), dve.tok())
            for i in range(2):
                dve(lambda e, i=i: e.scalar_tensor_tensor(H[:, i, :], H[:, i, :], rs[i], gb[:, row, :], ALU.mult,
                                                          ALU.mult), t, d_row)
                t = dve(lambda e, i=i: e.tensor_tensor(X[:, i, :], X[:, i, :], H[:, i, :], ALU.add))
            return t

        t = add_normed(0, d_pm)
        rs, t = rstd([X[:, 0, :], X[:, 1, :]], 1024, t)
        t = scaled(H, X, rs, t)
        t = transposed(H, 8, G_FFN2, keep_split(hTh, hTl), t)

        acc = [banks.take() for _ in range(4)]
        ah = [frb[:, 512 * z:512 * z + 512].rearrange("p (k n) -> p k n", k=2) for z in range(2)]
        al = [frb[:, 1024 + 512 * z:1536 + 512 * z].rearrange("p (k n) -> p k n", k=2) for z in range(2)]
        a_free = [None, None]
        pend = []

        def ffn_down(c, t):
            z = c % 2
            q, h, l, tp, _, k = None, None, None, None, None, None
            for k in range(2):
                q, h, l, tp, _, _ = next_piece(("fd", c))
                for i in range(2):
                    sl = slice(P * i, P * i + P)
                    for cc in range(2):
                        for n, (a, w) in enumerate(((ah, h), (al, h), (ah, l))):
                            end = i == 1 and cc == 1 and n == 2
                            tok = pe(lambda e, b=acc[2 * i + cc], a=a[z][:, k, sl], w=w[:, 0, 512 * cc:512 * cc + 512],
                                     s0=(c == 0 and k == 0 and n == 0), s1=(c == 10 and k == 1 and n == 2):
                                     e.matmul(ps(b)[:, :], a, w, start=s0, stop=s1),
                                     tp, t, banks.free[acc[2 * i + cc]] if c == 0 else None, inc=1 if end else 0)
                done_piece(q, tok)
            a_free[z] = tok

        for c in range(11):
            z = c % 2
            bg, _ = stream_features(("fg", c), (hTh, hTl), 8, 256, t)
            bu, tt = stream_features(("fu", c), (hTh, hTl), 8, 256)
            for j in range(2):
                s, o = S[j][:, 0:256], S[j][:, 256:512]
                t2 = act(lambda e, s=s, b=bg[j]: e.activation(s, ps(b)[:, 0:256], ACT.Silu), tt, dve.tok())
                banks.give(bg[j], t2)
                t2 = dve(lambda e, s=s, o=o, b=bu[j]: e.tensor_tensor(o, s, ps(b)[:, 0:256], ALU.mult), t2)
                banks.give(bu[j], t2)
                t2 = act(lambda e, o=o, j=j, z=z: e.copy(ah[z][:, j, :], o), t2, a_free[z])
                t2 = dve(lambda e, o=o, j=j, z=z: e.tensor_tensor(al[z][:, j, :], o, ah[z][:, j, :].bitcast(F),
                                                                  ALU.subtract), t2)
            ffn_down(c, t2)
        for i in range(2):
            for cc in range(2):
                b = acc[2 * i + cc]
                t = copy_out(H[:, i, 512 * cc:512 * cc + 512], b, ps(b)[:, :], pe.tok())
        add_normed(1, d_pf)
        s_out = sem("s_out")
        ov = out.rearrange("a (i p) n -> p (a i) n", p=P)
        for i in range(2):
            sp(lambda e, i=i: e.dma_start(ov[:, i, :], X[:, i, :]).then_inc(s_out, 16), dve.tok())

        def emit(eng, q, mark, body):
            rest = q.items[mark:]
            q.items = q.items[:mark]
            q.emit(eng)
            general(eng, body)
            q.items = rest
            q.emit(eng)

        def emit_sp(eng, items, seen):
            for fn, waits in items:
                for s, val in waits:
                    if val > seen.get(id(s), 0):
                        eng.wait_ge(s, val)
                        seen[id(s)] = val
                fn(eng)

        first_late = at["late_sp"]
        block = ctx.enter_context(nc.Block())

        @block.sync
        def _(e):
            seen = {}
            emit_sp(e, sp_items[:first_late], seen)
            general(e, general_sp)
            emit_sp(e, sp_items[first_late:], seen)
            e.wait_ge(s_out, 32)

        @block.tensor
        def _(e):
            emit(e, pe, marks[pe], general_pe)

        @block.scalar
        def _(e):
            emit(e, act, marks[act], general_act)

        @block.vector
        def _(e):
            emit(e, dve, marks[dve], general_dve)

        @block.gpsimd
        def _(e):
            pool.emit(e)


def kernel(**inputs):
    import concourse.bacc as _bacc
    from concourse import mybir as _mybir
    from concourse.bass_utils import run_bass_kernel_spmd as _run

    a = {k: np.ascontiguousarray(v) for k, v in inputs.items()}

    def cols(*names):
        return np.ascontiguousarray(np.concatenate([a[n].reshape(-1, P).T for n in names], axis=1))

    c, pool = shape_constants()
    rel = a["rel_bias_2"][0]
    rel_ext = np.concatenate([np.repeat(rel[:, 191:192], 127, axis=1), rel[:, ::-1], np.repeat(rel[:, 0:1], 65, axis=1)],
                             axis=1)
    rel_ext = np.stack([rel_ext[:, 127 - p:383 - p] for p in range(P)])
    route = np.concatenate([a["w_router_group"][0], a["w_router_expert"][0]], axis=1)
    arrays = {
        "x": a["x"], "mem": a["mem"], "positions": np.ascontiguousarray(a["positions"].reshape(2, P).T),
        "w_in": a["w_in"], "gate_b": a["gate_b"], "w_uq": a["w_uq"], "w_uk": a["w_uk"], "w_uv": a["w_uv"],
        "pool_w": a["pool_w"], "w_mem_kv": a["w_mem_kv"], "w_br_pool": a["w_br_pool"], "w_br_mla": a["w_br_mla"],
        "w_br_mem": a["w_br_mem"], "w_out": a["w_out"], "w_gate_e": a["w_gate_e"], "w_up_e": a["w_up_e"],
        "w_down_e": a["w_down_e"], "w_qkv": a["w_qkv_2"], "w_o": a["w_o_2"], "w_gate": a["w_gate_2"],
        "w_up": a["w_up_2"], "w_down": a["w_down_2"],
        "gvec": cols("mix_norm_g", "mem_norm_g", "q_norm_g", "kv_norm_g", "pool_scale", "g_pre_mix_2", "g_pre_ffn_2"),
        "grow": np.ascontiguousarray(np.stack([a["ffn_norm_g"][0], a["final_norm_g"], a["g_post_mix_2"][0],
                                               a["g_post_ffn_2"][0]])),
        "w_route": np.ascontiguousarray(route.reshape(P, 288)),
        "b_route": np.ascontiguousarray(np.concatenate([a["b_router_group"], a["b_router_expert"]], axis=1)),
        "rel_ext": np.ascontiguousarray(rel_ext), "cst": c, "cst_pool": pool,
    }
    nc = _bacc.Bacc("TRN2", target_bir_lowering=False, num_devices=1)
    args = [nc.dram_tensor(f"in_{n}", v.shape, _mybir.dt.from_np(v.dtype), kind="ExternalInput").ap()
            for n, v in arrays.items()]
    args.append(nc.dram_tensor("out_0", (1, 256, 1024), _mybir.dt.float32, kind="ExternalOutput").ap())
    build(nc, *args)
    r = _run(nc, [{f"in_{n}": v for n, v in arrays.items()}], core_ids=[0])
    return r.results[0]["out_0"]
```

```python
from contextlib import ExitStack

import numpy as np

import concourse.bass as bass
from concourse import mybir

F = mybir.dt.float32
FR = mybir.dt.float32r
I32 = mybir.dt.int32
ALU = mybir.AluOpType
ACT = mybir.ActivationFunctionType
AX = mybir.AxisListType.X

P = 128
RAW = 6
EXT = 10
PIECES = 4
AHEAD = 3
CAP = 32
NEG = -1.0e30
EPS = 1e-6
MAGIC = 12582912.0
PI_IN = 3.1415925
TWO_PI_1 = 6.28125
TWO_PI_2 = float(np.float32(2 * np.pi - 6.28125))
TWO_PI_3 = float(2 * np.pi - 6.28125 - float(np.float32(2 * np.pi - 6.28125)))

C_ID, C_TRI, C_ONE, C_MASK, C_IOTA, C_RANK, C_INVF, C_END = np.cumsum([0, 128, 128, 1, 384, 32, 32, 32]).tolist()
G_MIX, G_MEM, G_Q, G_KV, G_POOL, G_MIX2, G_FFN2, G_END = np.cumsum([0, 8, 8, 3, 2, 4, 8, 8]).tolist()


def shape_constants():
    c = np.zeros((P, C_END), np.float32)
    c[:, C_ID:C_ID + P] = np.eye(P)
    c[:, C_TRI:C_TRI + P] = np.triu(np.ones((P, P)), 1)
    c[:, C_ONE] = 1.0
    causal = np.where(np.tril(np.ones((P, P))) > 0, 0.0, NEG)
    c[:, C_MASK:C_MASK + P] = causal
    c[:, C_MASK + 2 * P:C_MASK + 3 * P] = causal
    c[:, C_IOTA:C_IOTA + CAP] = np.arange(CAP)
    c[:, C_RANK:C_RANK + 32] = 32 - np.arange(32)
    c[:, C_INVF:C_INVF + 32] = (np.float32(1.0) / (np.float32(10000.0) ** (np.arange(0, 64, 2, dtype=np.float32) / np.float32(64)))).astype(np.float32)
    pool = np.zeros((4, 256, 256), np.float32)
    for g, w in enumerate((2, 4, 8, 16)):
        for s in range(256):
            n = min(s + 1, w)
            pool[g, s + 1 - n:s + 1, s] = np.float32(1.0) / np.float32(n)
            pool[g, s, s] -= 1.0
    pool = np.ascontiguousarray(pool.reshape(4, 2, P, 256).transpose(2, 1, 0, 3)).reshape(P, 2048)
    return c, pool


class Queue:

    def __init__(self, sem, chained):
        self.sem, self.chained, self.items, self.n = sem, chained, [], 0

    def tok(self):
        return (self.sem, self.n)

    def __call__(self, fn, *waits, inc=1, free=False):
        waits = [w for w in waits if w is not None]
        if self.chained and not free and self.n:
            waits.append(self.tok())
        self.items.append((fn, waits, inc))
        self.n += inc
        return self.tok()

    def emit(self, eng):
        seen = {}
        for fn, waits, inc in self.items:
            need = {}
            for sem, val in waits:
                key = id(sem)
                if val > seen.get(key, 0) and val > need.get(key, (None, 0))[1]:
                    need[key] = (sem, val)
            for key, (sem, val) in need.items():
                eng.wait_ge(sem, val)
                seen[key] = val
            ins = fn(eng)
            if inc:
                ins.then_inc(self.sem, inc)


class Banks:

    def __init__(self, tensors):
        self.t, self.free, self.order = tensors, [None] * len(tensors), list(range(len(tensors)))

    def take(self):
        b = self.order.pop(0)
        return b

    def give(self, b, tok):
        self.free[b] = tok
        self.order.append(b)


def build(nc, x, mem, positions, w_in, gate_b, w_uq, w_uk, w_uv, pool_w, w_mem_kv, w_br_pool, w_br_mla,
          w_br_mem, w_out, w_gate_e, w_up_e, w_down_e, w_qkv, w_o, w_gate, w_up, w_down,
          gvec, grow, w_route, b_route, rel_ext, cst, cst_pool, out, force_general=False):
    ctx = ExitStack()
    with ctx:
        def sb(name, shape, dt=F):
            return ctx.enter_context(nc.sbuf_tensor(name, shape, dt))

        def sem(name):
            return ctx.enter_context(nc.semaphore(name))

        pe = Queue(sem("q_pe"), False)
        act = Queue(sem("q_act"), True)
        dve = Queue(sem("q_dve"), True)
        pool = Queue(sem("q_pool"), True)
        sp_items = []

        def sp(fn, *waits):
            sp_items.append((fn, [w for w in waits if w is not None]))

        banks = Banks([ctx.enter_context(nc.psum_tensor(f"ps{i}", [P, 512], F)) for i in range(8)])

        def ps(b):
            return banks.t[b]

        raw = sb("raw", [P, RAW, 2048])
        with ExitStack() as rounded:
            wh, wl, fra, frb = (rounded.enter_context(nc.sbuf_tensor(n, s, FR)) for n, s in (
                ("wh", [P, PIECES, 1024]), ("wl", [P, PIECES, 1024]), ("fra", [P, 8192]), ("frb", [P, 4096])))
        ext = sb("ext", [P, EXT, 2048])
        hTh, hTl = (fra[:, a:a + 2048].rearrange("p (t n) -> p t n", t=8) for a in (0, 2048))
        mTh, mTl = (fra[:, a:a + 2048].rearrange("p (t n) -> p t n", t=8) for a in (4096, 6144))
        ymh, yml = (frb[:, a:a + 1024].rearrange("p (t n) -> p t n", t=4) for a in (0, 1024))
        yph, ypl = (frb[:, a:a + 1024].rearrange("p (t n) -> p t n", t=4) for a in (2048, 3072))
        X = sb("X", [P, 2, 1024])
        H = sb("H", [P, 2, 1024])
        junk = sb("junk", [P, 1024])
        C = sb("C", [P, C_END])
        G = sb("G", [P, G_END])
        st = sb("st", [P, 96])
        big = sb("big", [P, 9984])
        S3 = sb("S3", [P, 3, 512])
        S = [S3[:, i, :] for i in range(3)]
        scr = S3[:, 0:2, :].rearrange("p a n -> p (a n)")
        T = S
        PT = [junk[:, 0:512], junk[:, 512:1024]]
        cs = sb("cs", [P, 2, 2, 32])
        posi = sb("posi", [P, 2], I32)
        gb = sb("gb", [P, 2, 1024])
        rt = sb("rt", [P, 640])
        flag = sb("flag", [P, 1], I32)

        ident = C[:, C_ID:C_ID + P]

        def load(dst, src, *waits):
            s = sem(f"d_{len(sp_items)}")
            sp(lambda e: e.dma_start(dst, src).then_inc(s, 16), *waits)
            return (s, 16)

        mv, xv_ = (v.rearrange("a (i p) n -> p (a i) n", p=P) for v in (mem, x))
        d_mem = [load(H[:, i, :], mv[:, i, :]) for i in range(2)]
        d_g = load(G[:, :], gvec)
        d_c = load(C[:, :], cst)

        s_raw = [sem(f"s_raw{i}") for i in range(RAW + EXT)]
        raw_count, raw_tok, slot_of = [0] * (RAW + EXT), {}, {}
        free_slots = [(i, None) for i in range(RAW)]
        units, pieces = [], []
        at = {"unit": 0, "piece": 0, "loaded": 0, "split": 0, "late": None, "late_sp": None, "experts": None}

        def unit(key, src, shape, split):
            units.append((key, src, shape, split))
            if split:
                per = max(1, 1024 // shape[1])
                for a in range(0, shape[0], per):
                    pieces.append((len(units) - 1, a, min(per, shape[0] - a)))

        def raw_view(u):
            k, n = units[u][2]
            z = slot_of[u]
            v = raw[:, z, 0:k * n] if z < RAW else ext[:, z - RAW, 0:k * n]
            return v.rearrange("p (k n) -> p k n", k=k)

        def issue():
            while at["loaded"] < len(units):
                u = at["loaded"]
                fit = [n for n, (z, _) in enumerate(free_slots) if z < RAW or at["experts"] <= u < at["late"]]
                if not fit:
                    return
                z, tok = free_slots.pop(fit[0])
                slot_of[u] = z
                src = units[u][1]
                if u == at["late"]:
                    at["late_sp"] = len(sp_items)
                if len(src.shape) == 4:
                    parts = [(raw_view(u)[:, a, :].rearrange("p (b c) -> p b c", b=src.shape[2]), src[:, a])
                             for a in range(src.shape[1])]
                else:
                    parts = [(raw_view(u), src)]
                for dst, part in parts:
                    sp(lambda e, dst=dst, part=part, z=z: e.dma_start(dst, part).then_inc(s_raw[z], 16), tok)
                raw_count[z] += 16 * len(parts)
                raw_tok[u] = (s_raw[z], raw_count[z])
                at["loaded"] += 1

        def landed(u):
            return raw_tok[u]

        def release(u, tok):
            free_slots.append((slot_of[u], tok))
            issue()

        wfree = [None] * PIECES
        piece_tok = {}

        def split_upto(n, *more):
            while at["split"] <= min(n, len(pieces) - 1):
                q = at["split"]
                u, a, k = pieces[q]
                if u >= at["loaded"]:
                    return
                if isinstance(wfree[q % PIECES], str):
                    return
                cols = units[u][2][1]
                v = raw_view(u)[:, a:a + k, :]
                h = wh[:, q % PIECES, 0:k * cols].rearrange("p (k n) -> p k n", k=k)
                l = wl[:, q % PIECES, 0:k * cols].rearrange("p (k n) -> p k n", k=k)
                t = act(lambda e, h=h, v=v: e.copy(h, v), landed(u), wfree[q % PIECES], *more, free=True)
                t = dve(lambda e, h=h, l=l, v=v: e.tensor_tensor(l, v, h.bitcast(F), ALU.subtract), t,
                        landed(u), wfree[q % PIECES], free=True)
                wfree[q % PIECES] = "taken"
                piece_tok[q] = (h, l, t)
                at["split"] += 1
                if a + k == units[u][2][0]:
                    release(u, t)

        def next_piece(key):
            q = at["piece"]
            assert units[pieces[q][0]][0] == key, (units[pieces[q][0]][0], key)
            split_upto(q)
            at["piece"] += 1
            return (q,) + piece_tok[q] + pieces[q][1:]

        def done_piece(q, tok):
            wfree[q % PIECES] = tok
            split_upto(q + AHEAD)

        def next_raw(key):
            while units[at["unit"]][3]:
                at["unit"] += 1
            u = at["unit"]
            assert units[u][0] == key, (units[u][0], key)
            assert u < at["loaded"], (u, at["loaded"], key)
            at["unit"] += 1
            return u, raw_view(u), landed(u)

        def k8(w, c0, c1, key, split=True):
            v = w.rearrange("(k p) n -> p k n", p=P)
            nk = v.shape[1]
            for a in range(0, nk, 4):
                unit(key, v[:, a:a + 4, c0:c1], (min(4, nk - a), c1 - c0), split)

        for c in range(2):
            k8(w_mem_kv[0], 512 * c, 512 * c + 512, ("mkv", c))
        k8(w_in[0], 1216, 1728, "xq")
        k8(w_in[0], 512, 896, "qd")
        k8(w_in[0], 896, 1216, "kvd")
        uq = w_uq[0].rearrange("(k p) (h c) -> p k h c", p=P, h=8)
        unit("uqr", uq[:, :, :, 128:192], (3, 512), False)
        for a in range(2):
            unit("uqn", uq[:, :, 4 * a:4 * a + 4, 0:128], (3, 512), False)
        unit("uk", w_uk[0].rearrange("(k p) n -> p k n", p=P), (2, 1024), False)
        unit("uv", w_uv[0].rearrange("(k p) n -> p k n", p=P), (2, 1024), False)
        k8(w_in[0], 0, 512, "pool")
        unit("poolc", cst_pool.rearrange("p (k n) -> p k n", k=8), (8, 256), False)
        unit("poolw", pool_w[0].rearrange("g c d -> c g d"), (4, 128), False)
        for br, w in ((0, w_br_pool), (2, w_br_mem), (1, w_br_mla)):
            for c in range(2):
                col = 1728 + 1024 * br + 512 * c
                k8(w_in[0], col, col + 512, ("gate", br, c))
                k8(w[0], 512 * c, 512 * c + 512, ("br", br, c))
        for c in range(2):
            k8(w_out[0], 512 * c, 512 * c + 512, ("out", c))
        at["experts"] = len(units)
        for g in range(8):
            for key, w in (("eg", w_gate_e), ("eu", w_up_e)):
                v = w[0, 4 * g:4 * g + 4].rearrange("e (p k) n -> p e (k n)", p=P)
                for t in range(4):
                    unit(key, v[:, :, 512 * t:512 * t + 512], (4, 512), False)
            v = w_down_e[0, 4 * g:4 * g + 4].rearrange("e (k p) n -> p e k n", p=P)
            for c in range(2):
                for t in range(2):
                    unit("ed", v[:, :, t, 512 * c:512 * c + 512], (4, 512), False)
        at["late"] = len(units)
        for c in (0, 2, 4, 1, 3, 5):
            k8(w_qkv[0], 512 * c, 512 * c + 512, ("qkv", c))
        for a in (0, 4):
            for c in range(2):
                unit(("o", a, c), w_o[0].rearrange("(k p) n -> p k n", p=P)[:, a:a + 4, 512 * c:512 * c + 512],
                     (4, 512), True)
        for c in range(12):
            if c < 11:
                for key, w in (("fg", w_gate), ("fu", w_up)):
                    unit((key, c), w[0].rearrange("(k p) n -> p k n", p=P)[:, :, 256 * c:256 * c + 256], (8, 256), True)
            if c:
                unit(("fd", c - 1), w_down[0, 256 * c - 256:256 * c, :].rearrange("(k p) n -> p k n", p=P), (2, 1024),
                     True)
        issue()
        d_x = [load(X[:, i, :], xv_[:, i, :]) for i in range(2)]
        d_pos = load(posi[:, :], positions)

        def group(o, pairs, *waits, check=True):
            t = None
            for n, (a, b) in enumerate(pairs):
                last = n == len(pairs) - 1
                t = pe(lambda e, a=a, b=b, n=n, last=last: e.matmul(
                    o, a, b, start=(n == 0), stop=last, skip_group_check=not check),
                    *(waits if n == 0 else ()), inc=1 if last else 0)
            return t

        def stream_tokens(key, aT, nk, cols, *waits, k0=0, total=None, bs=None, later=None):
            ah, al = aT
            total = total or nk
            first = list(waits)
            if bs is None:
                bs = [banks.take() for _ in range(2)]
                first += [banks.free[b] for b in bs]
            stop_k = k0 + nk
            while k0 < stop_k:
                q, h, l, t, _, k = next_piece(key)
                assert not (later and k0 < 4 < k0 + k)
                first += [later] if k0 >= 4 else []
                for kk in range(k):
                    for i in range(2):
                        sl = slice(P * i, P * i + P)
                        for n, (a, w) in enumerate(((ah, h), (al, h), (ah, l))):
                            s0, s1 = k0 + kk == 0 and n == 0, k0 + kk == total - 1 and n == 2
                            end = s1 or (kk == k - 1 and i == 1 and n == 2)
                            tok = pe(lambda e, o=ps(bs[i])[:, 0:cols], a=a[:, k0 + kk, sl], w=w[:, kk, :],
                                     s0=s0, s1=s1: e.matmul(o, a, w, start=s0, stop=s1),
                                     t, *first, inc=1 if end else 0)
                            first = []
                done_piece(q, tok)
                k0 += k
                yield
            return bs, tok

        def stream_features(key, aT, nk, cols, *waits, later=None):
            ah, al = aT
            m = cols // P
            bs = [banks.take() for _ in range(m)]
            first, k0 = list(waits) + [banks.free[b] for b in bs], 0
            while k0 < nk:
                q, h, l, t, _, k = next_piece(key)
                assert not (later and k0 < 4 < k0 + k)
                first += [later] if k0 >= 4 else []
                for kk in range(k):
                    for j in range(m):
                        sl = slice(P * j, P * j + P)
                        for n, (a, w) in enumerate(((ah, h), (al, h), (ah, l))):
                            s0, s1 = k0 + kk == 0 and n == 0, k0 + kk == nk - 1 and n == 2
                            end = s1 or (kk == k - 1 and j == m - 1 and n == 2)
                            tok = pe(lambda e, o=ps(bs[j])[:, 0:256], a=a[:, k0 + kk, :], w=w[:, kk, sl],
                                     s0=s0, s1=s1: e.matmul(o, w, a, start=s0, stop=s1),
                                     t, *first, inc=1 if end else 0)
                            first = []
                done_piece(q, tok)
                k0 += k
                yield
            return bs, tok

        def whole(steps):
            while True:
                try:
                    next(steps)
                except StopIteration as end:
                    return end.value

        def beside(main, fill, n):
            for _ in main:
                for _ in range(n):
                    next(fill, None)

        def copy_out(o, b, src, *waits, eng=None):
            t = (eng or act)(lambda e: (e.copy if (eng or act) is act else e.tensor_copy)(o, src), *waits)
            banks.give(b, t)
            return t

        def split_out(oh, ol, b, src, *waits):
            t = act(lambda e: e.copy(oh, src), *waits)
            t = dve(lambda e: e.tensor_tensor(ol, src, oh.bitcast(F), ALU.subtract), t)
            banks.give(b, t)
            return t

        stat = [0]
        half = st[:, 88:90]
        pool_last = [pool(lambda e: e.memset(half, -0.5))]

        def columns():
            c = 8 * (stat[0] % 10)
            stat[0] += 1
            return st[:, c:c + 8]

        def square_act(acc, part, width, *waits, scratch=None):
            o = junk[:, 0:width] if scratch is None else scratch[:, 0:width]
            return act(lambda e: e.activation(o, part, ACT.Square, accum_out=acc), pool_last[0], *waits)

        def square_dve(acc, part, width, *waits):
            return dve(lambda e: e.tensor_tensor_reduce(scr[:, 0:width], part, part, 1.0, 0.0, ALU.mult, ALU.add, acc),
                       pool_last[0], pe.tok(), *waits)

        def root(ss, r, width, *waits, more=None):
            if more is not None:
                pool(lambda e: e.tensor_tensor(ss, ss, more, ALU.add), *waits)
            pool(lambda e: e.tensor_scalar(ss, ss, 1.0 / width, EPS, ALU.mult, ALU.add), *waits, dve.tok())
            t = pool(lambda e: e.tensor_tensor(r, ss, half[:, 0:ss.shape[1]], ALU.pow))
            pool_last[0] = t
            return t

        def rstd(parts, width, *waits, scratch=None):
            k, n = columns(), len(parts)
            for i, part in enumerate(parts):
                t = square_act(k[:, i:i + 1], part, width, *waits, scratch=scratch)
            t = root(k[:, 0:n], k[:, 4:4 + n], width, t)
            return [k[:, 4 + i:5 + i] for i in range(n)], t

        def rstd_halves(parts, width, w0, w1, one="dve"):
            k = columns()
            ss = [k[:, i:i + 1] for i in range(2)]
            r = [k[:, 4 + i:5 + i] for i in range(2)]
            a0 = square_act(ss[0], parts[0], width, *w0)
            a1 = (square_dve if one == "dve" else square_act)(ss[1], parts[1], width, *w1)
            return r, [root(ss[0], r[0], width, a0), root(ss[1], r[1], width, a1)]

        def transposed(src, nt, gcol, keep_to, *waits, halves=None):
            toks_ = {}
            for i in range(2):
                for a in range(0, nt, 4):
                    k = min(4, nt - a)
                    b = banks.take()
                    for j in range(k):
                        t = pe(lambda e, b=b, i=i, a=a, j=j: e.transpose(
                            ps(b)[:, P * j:P * j + P], src[:, i, P * (a + j):P * (a + j) + P], ident),
                            banks.free[b], *waits, halves[i] if halves else None, inc=1 if j == k - 1 else 0)
                    v = ps(b)[:, 0:k * P].rearrange("p (k n) -> p k n", k=k)
                    o = [d[:, a:a + k, P * i:P * i + P] for d in keep_to]
                    if gcol is None:
                        t = act(lambda e, o=o, v=v: e.copy(o[0], v), t)
                        if len(o) == 2:
                            t = dve(lambda e, o=o, v=v: e.tensor_tensor(o[1], v, o[0].bitcast(F), ALU.subtract), t)
                    else:
                        t0 = t
                        for j in range(k):
                            g = G[:, gcol + a + j:gcol + a + j + 1]
                            t = act(lambda e, o=o, v=v, g=g, j=j: e.activation(o[0][:, j, :], v[:, j, :], ACT.Copy,
                                                                              scale=g), t0, free=True)
                        for j in range(k if len(o) == 2 else 0):
                            g = G[:, gcol + a + j:gcol + a + j + 1]
                            t2 = dve(lambda e, o=o, v=v, g=g, j=j: e.scalar_tensor_tensor(
                                o[1][:, j, :], v[:, j, :], g, o[0][:, j, :].bitcast(F), ALU.mult, ALU.subtract),
                                t, free=True)
                        t = t2 if len(o) == 2 else t
                    banks.give(b, t)
                    toks_[a] = t
            return [toks_[a] for a in range(0, nt, 4)]

        def scaled(dst, src, rs, ts, *waits):
            return [dve(lambda e, i=i: e.tensor_scalar(dst[:, i, :], src[:, i, :], rs[i], None, ALU.mult), ts[i], *waits)
                    for i in range(2)]

        def attention(heads, scores, soften, values, finish):
            s_free, pt_free = [None] * 3, [None] * 2
            exps, norms, turned = {}, {}, {}
            for step in range(heads + 3):
                if step < heads:
                    b, t = scores(step)
                if 0 <= step - 2 < heads:
                    h = step - 2
                    parts, tn = norms.pop(h)
                    bt = banks.take()
                    for n, src in enumerate(parts):
                        t2 = pe(lambda e, bt=bt, n=n, src=src: e.transpose(ps(bt)[:, P * n:P * n + P], src, ident),
                                banks.free[bt], tn, inc=1 if n == len(parts) - 1 else 0)
                    s_free[h % 3] = t2
                    w = P * len(parts)
                    t3 = act(lambda e, bt=bt, h=h, w=w: e.copy(PT[h % 2][:, 0:w], ps(bt)[:, 0:w]), t2, pt_free[h % 2])
                    banks.give(bt, t3)
                    turned[h] = t3
                if step >= 3:
                    h = step - 3
                    tv = values(h, PT[h % 2], turned.pop(h))
                    pt_free[h % 2] = tv
                if step < heads:
                    view, mx, t = soften(step, b, t, S[step % 3], s_free[step % 3])
                    c = 4 * (step % 4)
                    for i in range(2):
                        t = act(lambda e, i=i, view=view, c=c, mx=mx: e.activation(
                            view[i][1], view[i][0], ACT.Exp, bias=mx[:, i:i + 1], scale=view[i][2],
                            accum_out=rt[:, c + i:c + i + 1]), t)
                    if view[0][3] is not None:
                        banks.give(view[0][3], t)
                    exps[step] = (view, c, t)
                if 0 <= step - 1 < heads:
                    h = step - 1
                    view, c, t = exps.pop(h)
                    dve(lambda e, c=c: e.reciprocal(rt[:, c + 2:c + 4], rt[:, c:c + 2]), t)
                    t = dve.tok()
                    for i in range(2):
                        tn = dve(lambda e, i=i, view=view, c=c: e.tensor_scalar(
                            view[i][1], view[i][1], rt[:, c + 2 + i:c + 3 + i], None, ALU.mult), t, free=True)
                    norms[h] = ([view[i][1][:, P * off:P * off + P] for i, off in view[2]], tn)
                if step >= 3:
                    finish(step - 3, tv)
                yield

        rs, t = rstd_halves([H[:, 0, :], H[:, 1, :]], 1024, [d_mem[0]], [d_mem[1]])
        t = scaled(H, H, rs, t)
        t_mT = transposed(H, 8, G_MEM, (mTh, mTl), d_c, d_g, halves=t)
        t_h0 = pe.tok()
        xkT = big[:, 0:1024].rearrange("p (t n) -> p t n", t=4)
        xv = big[:, 1024:2048].rearrange("p (t n) -> p t n", t=2)
        xqT = big[:, 2048:3072].rearrange("p (t n) -> p t n", t=4)
        bs, t = whole(stream_features(("mkv", 0), (mTh, mTl), 8, 512, t_mT[0], later=t_mT[1]))
        rs, t2 = rstd_halves([X[:, 0, :], X[:, 1, :]], 1024, [d_x[0]], [d_x[1]])
        for j, b in enumerate(bs):
            copy_out(xkT[:, j, :], b, ps(b)[:, 0:256], t)
        t2 = scaled(H, X, rs, t2, t_h0)

        fr = [big[:, 8000:8064].rearrange("p (i c) -> p i c", i=2), big[:, 8064:8128].rearrange("p (i c) -> p i c", i=2)]
        posf = st[:, 92:94]
        dve(lambda e: e.tensor_copy(posf, posi[:, :]), d_pos)
        for i in range(2):
            dve(lambda e, i=i: e.tensor_scalar(fr[0][:, i, :], C[:, C_INVF:C_INVF + 32], posf[:, i:i + 1], None,
                                               ALU.mult), d_c)
        for f, shift in ((0, 0.25), (1, 0.0)):
            o = cs[:, f, :, :]
            dve(lambda e, shift=shift: e.tensor_scalar(fr[1], fr[0], float(1 / (2 * np.pi)), shift, ALU.mult, ALU.add))
            dve(lambda e: e.tensor_scalar(fr[1], fr[1], MAGIC, None, ALU.add))
            dve(lambda e: e.tensor_scalar(fr[1], fr[1], -MAGIC, None, ALU.add))
            for n, c in enumerate((TWO_PI_1, TWO_PI_2, TWO_PI_3)):
                src = fr[0] if n == 0 else o
                dve(lambda e, src=src, c=c, o=o: e.scalar_tensor_tensor(o, fr[1], -c, src, ALU.mult, ALU.add))
            if f == 0:
                dve(lambda e, o=o: e.tensor_scalar(o, o, float(np.pi / 2), None, ALU.add))
            dve(lambda e, o=o: e.tensor_scalar(o, o, PI_IN, -PI_IN, ALU.min, ALU.max))
        t_cs0 = dve.tok()
        cosb = cs[:, 0, :, :]
        sinb = cs[:, 1, :, :]

        bs, t = whole(stream_tokens(("mkv", 1), (mTh, mTl), 8, 512))
        t_hT = transposed(H, 8, G_MIX, (hTh, hTl), halves=t2)
        for i, b in enumerate(bs):
            copy_out(xv[:, i, :], b, ps(b)[:, :], t)
        t_cs = act(lambda e: e.activation(cs[:, :, :, :], cs[:, :, :, :], ACT.Sin), t_cs0)
        bs, t = whole(stream_features("xq", (hTh, hTl), 8, 512, t_hT[0], later=t_hT[1]))
        for j, b in enumerate(bs):
            t_xq = copy_out(xqT[:, j, :], b, ps(b)[:, 0:256], t)

        XS = float(128 ** -0.5)

        def x_scores(h):
            b = banks.take()
            for i in range(2):
                t = group(ps(b)[:, 256 * i:256 * i + 256], [(xqT[:, h, P * i:P * i + P], xkT[:, h, :])],
                          banks.free[b], t_xq)
            return b, t

        def x_soften(h, b, t, s, sfree):
            mx = st[:, 80 + 2 * (h % 4):82 + 2 * (h % 4)]
            v = ps(b)[:, :].rearrange("p (i n) -> p i n", i=2)
            dve(lambda e: e.tensor_reduce(mx, v, AX, ALU.max, negate=True), t)
            t = dve(lambda e: e.tensor_scalar(mx, mx, XS, None, ALU.mult), sfree)
            view = [(v[:, i, :], s[:, 256 * i:256 * i + 256], XS, b) for i in range(2)]
            return view + [[(0, 0), (1, 0), (0, 1), (1, 1)]], mx, t

        pv_bank = {}

        def x_values(h, pt, t):
            b = banks.take()
            pv_bank[h] = b
            return group(ps(b)[:, 0:256], [(xv[:, k, P * h:P * h + P], pt[:, 256 * k:256 * k + 256]) for k in range(2)],
                         banks.free[b], t)

        def x_finish(h, t):
            b = pv_bank.pop(h)
            split_out(ymh[:, h, :], yml[:, h, :], b, ps(b)[:, 0:256], t)

        cqT = big[:, 3072:3840].rearrange("p (t n) -> p t n", t=3)
        ckT = big[:, 3840:4352].rearrange("p (t n) -> p t n", t=2)
        krT = [big[:, 4352 + 256 * a:4608 + 256 * a] for a in range(2)]
        qrT = big[:, 4864:5888].rearrange("p (t n) -> p t n", t=4)
        qnT = big[:, 5888:7936].rearrange("p (t n) -> p t n", t=8)
        knT = big[:, 7936:9984].rearrange("p (t n) -> p t n", t=8)
        vv = H
        lat = big[:, 5888:6656].rearrange("p (i n) -> p i n", i=2)
        kr = big[:, 6656:6912].rearrange("p (i n) -> p i n", i=2)
        lat2 = big[:, 6912:7424].rearrange("p (i n) -> p i n", i=2)
        square = big[:, 7424:7936]
        L3 = [big[:, 8448 + 512 * z:8960 + 512 * z] for z in range(3)]
        toks = {}

        def latents():
            bs, t = yield from stream_tokens("qd", (hTh, hTl), 8, 384)
            rs, t = rstd([ps(b)[:, 0:384] for b in bs], 384, t, scratch=square)
            yield
            for i, b in enumerate(bs):
                t2 = dve(lambda e, i=i, b=b, rs=rs: e.tensor_scalar(lat[:, i, :], ps(b)[:, 0:384], rs[i], None,
                                                                    ALU.mult), t)
                banks.give(b, t2)
            bs, tt = yield from stream_tokens("kvd", (hTh, hTl), 8, 320)
            transposed(lat, 3, G_Q, (cqT,), t2)
            t_cq = act.tok()
            yield
            rs, t = rstd([ps(b)[:, 0:256] for b in bs], 256, tt, scratch=square)
            yield
            for i, b in enumerate(bs):
                src = ps(b)
                dve(lambda e, i=i, src=src, rs=rs: e.tensor_scalar(lat2[:, i, :], src[:, 0:256], rs[i], None,
                                                                   ALU.mult), t, t_cs)
                x1, x2 = src[:, 256:288], src[:, 288:320]
                ct, sn = cosb[:, i, :], sinb[:, i, :]
                tm = L3[2][:, 128 * i:128 * i + 128]
                dve(lambda e, x1=x1, ct=ct, tm=tm: e.tensor_tensor(tm[:, 0:32], x1, ct, ALU.mult))
                dve(lambda e, x2=x2, sn=sn, tm=tm: e.tensor_tensor(tm[:, 32:64], x2, sn, ALU.mult), free=True)
                dve(lambda e, x2=x2, ct=ct, tm=tm: e.tensor_tensor(tm[:, 64:96], x2, ct, ALU.mult), free=True)
                t2 = dve(lambda e, x1=x1, sn=sn, tm=tm: e.tensor_tensor(tm[:, 96:128], x1, sn, ALU.mult), free=True)
                banks.give(b, t2)
                for z in (0, 64):
                    dve(lambda e, i=i, tm=tm, z=z: e.tensor_tensor(kr[:, i, z:z + 32], tm[:, 0:32], tm[:, 32:64],
                                                                   ALU.subtract), t2, free=True)
                    t3 = dve(lambda e, i=i, tm=tm, z=z: e.tensor_tensor(kr[:, i, z + 32:z + 64], tm[:, 64:96],
                                                                        tm[:, 96:128], ALU.add), t2, free=True)
            yield
            transposed(lat2, 2, G_KV, (ckT,), t3)
            b = banks.take()
            for i in range(2):
                t = pe(lambda e, i=i, b=b: e.transpose(ps(b)[:, P * i:P * i + P], kr[:, i, :], ident), banks.free[b], t3,
                       inc=i)
            dve(lambda e: e.memset(krT[0][64:128, :], 0.0))
            dve(lambda e: e.memset(krT[1][0:64, :], 0.0))
            dve(lambda e, b=b: e.tensor_copy(krT[0][0:64, :], ps(b)[0:64, 0:256]), t)
            toks["kr"] = dve(lambda e, b=b: e.tensor_copy(krT[1][64:128, :], ps(b)[64:128, 0:256]), t)
            banks.give(b, toks["kr"])
            t_ck = act.tok()
            yield

            u, w, tw = next_raw("uqr")
            for i in range(2):
                b = banks.take()
                t = group(ps(b)[:, :], [(cqT[:, k, P * i:P * i + P], w[:, k, :]) for k in range(3)], banks.free[b],
                          t_cq, tw)
                v = ps(b)[:, :].rearrange("p (h c) -> p h c", h=8)
                x1, x2 = v[:, :, 0:32], v[:, :, 32:64]
                ct = cosb[:, i, :].unsqueeze(1).to_broadcast([P, 8, 32])
                sn = sinb[:, i, :].unsqueeze(1).to_broadcast([P, 8, 32])
                ta, tb = (L3[z][:, 0:256].rearrange("p (h c) -> p h c", h=8) for z in (0, 1))
                tc, td = (L3[z][:, 256:512].rearrange("p (h c) -> p h c", h=8) for z in (0, 1))
                o = L3[2][:, :].rearrange("p (h c) -> p h c", h=8)
                dve(lambda e, x1=x1, ct=ct, ta=ta: e.tensor_tensor(ta, x1, ct, ALU.mult), t, act.tok())
                dve(lambda e, x2=x2, sn=sn, tb=tb: e.tensor_tensor(tb, x2, sn, ALU.mult), free=True)
                dve(lambda e, x2=x2, ct=ct, tc=tc: e.tensor_tensor(tc, x2, ct, ALU.mult), free=True)
                t2 = dve(lambda e, x1=x1, sn=sn, td=td: e.tensor_tensor(td, x1, sn, ALU.mult), free=True)
                banks.give(b, t2)
                dve(lambda e, o=o, ta=ta, tb=tb: e.tensor_tensor(o[:, :, 0:32], ta, tb, ALU.subtract), pe.tok())
                t2 = dve(lambda e, o=o, tc=tc, td=td: e.tensor_tensor(o[:, :, 32:64], tc, td, ALU.add), free=True)
                if i == 1:
                    release(u, t)
                yield
                b = banks.take()
                for j in range(4):
                    t = pe(lambda e, b=b, j=j: e.transpose(ps(b)[:, P * j:P * j + P], L3[2][:, P * j:P * j + P], ident),
                           banks.free[b], t2, inc=1 if j == 3 else 0)
                copy_out(qrT[:, :, P * i:P * i + P], b, ps(b)[:, :].rearrange("p (j n) -> p j n", j=4), t)
            for a in range(2):
                u, w, tw = next_raw("uqn")
                for j in range(4):
                    b = banks.take()
                    t = group(ps(b)[:, 0:256], [(w[:, k, P * j:P * j + P], cqT[:, k, :]) for k in range(3)],
                              banks.free[b], tw)
                    copy_out(qnT[:, 4 * a + j, :], b, ps(b)[:, 0:256], t, dve.tok())
                    if j % 2:
                        yield
                release(u, t)
            u, w, tw = next_raw("uk")
            for j in range(8):
                b = banks.take()
                t = group(ps(b)[:, 0:256], [(w[:, k, P * j:P * j + P], ckT[:, k, :]) for k in range(2)],
                          banks.free[b], tw, t_ck)
                copy_out(knT[:, j, :], b, ps(b)[:, 0:256], t, dve.tok())
                if j % 4 == 3:
                    yield
            release(u, t)
            u, w, tw = next_raw("uv")
            for i in range(2):
                for c in range(2):
                    b = banks.take()
                    t = group(ps(b)[:, :], [(ckT[:, k, P * i:P * i + P], w[:, k, 512 * c:512 * c + 512]) for k in range(2)],
                              banks.free[b], tw)
                    toks["v"] = copy_out(vv[:, i, 512 * c:512 * c + 512], b, ps(b)[:, :], t)
                yield
            release(u, t)

        fill = latents()
        beside(attention(4, x_scores, x_soften, x_values, x_finish), fill, 2)
        t_ym = dve.tok()
        whole(fill)

        MS = float(192 ** -0.5)

        def m_scores(h):
            b = banks.take()
            for i in range(2):
                o = ps(b)[:, 0:128] if i == 0 else ps(b)[:, 128:384]
                n = P * (i + 1)
                sl = slice(P * i, P * i + P)
                t = group(o, [(qnT[:, h, sl], knT[:, h, 0:n]), (qrT[:, h // 2, sl], krT[h % 2][:, 0:n])],
                          banks.free[b], toks["v"], toks["kr"])
            return b, t

        def m_soften(h, b, t, s, sfree):
            mx = st[:, 80 + 2 * (h % 4):82 + 2 * (h % 4)]
            t = dve(lambda e: e.scalar_tensor_tensor(s[:, 0:384], ps(b)[:, 0:384], MS, C[:, C_MASK:C_MASK + 384],
                                                     ALU.mult, ALU.add), t, sfree)
            banks.give(b, t)
            dve(lambda e: e.tensor_reduce(mx[:, 0:1], s[:, 0:128], AX, ALU.max, negate=True))
            t = dve(lambda e: e.tensor_reduce(mx[:, 1:2], s[:, 128:384], AX, ALU.max, negate=True), t, free=True)
            return causal_view(s), mx, t

        def causal_view(s):
            return [(s[:, 0:128], s[:, 0:128], 1.0, None), (s[:, 128:384], s[:, 128:384], 1.0, None),
                    [(0, 0), (1, 0), (1, 1)]]

        def causal_values(o, w, pt, b, t):
            pe(lambda e: e.matmul(o, w(0), pt[:, 0:256], start=True, stop=False), banks.free[b], t, inc=0)
            return pe(lambda e: e.matmul(o[:, 128:256], w(1), pt[:, 256:384], start=False, stop=True))

        def m_values(h, pt, t):
            b = banks.take()
            pv_bank[h] = b
            return causal_values(ps(b)[:, 0:256], lambda k: vv[:, k, P * h:P * h + P], pt, b, t)

        def m_finish(h, t):
            b = pv_bank.pop(h)
            split_out(mTh[:, h, :], mTl[:, h, :], b, ps(b)[:, 0:256], t)

        merged = big[:, 0:2048].rearrange("p (i n) -> p i n", i=2)
        uu = big[:, 2048:3072].rearrange("p (i n) -> p i n", i=2)
        pT = big[:, 3072:4096].rearrange("p (g n) -> p g n", g=4)
        gbt = [gb[:, 0, 0:512], gb[:, 0, 512:1024]]
        gt = [gb[:, 1, 0:512], gb[:, 1, 512:1024]]
        gb_free = [None, None]
        n_gate = [0]

        def pooling():
            bs, t = yield from stream_tokens("pool", (hTh, hTl), 8, 512)
            for i, b in enumerate(bs):
                t_u = copy_out(uu[:, i, :], b, ps(b)[:, :], t)
            u, w, tw = next_raw("poolc")
            u2, w2, tw2 = next_raw("poolw")
            tb = {}
            for g in range(5):
                if g < 4:
                    b = banks.take()
                    t = group(ps(b)[:, 0:256], [(uu[:, k, P * g:P * g + P], w[:, 4 * k + g, :]) for k in range(2)],
                              banks.free[b], t_u, tw)
                    tb[g] = copy_out(pT[:, g, :], b, ps(b)[:, 0:256], t)
                if g:
                    yield
                    h = g - 1
                    b = banks.take()
                    t = group(ps(b)[:, 0:256], [(w2[:, h, :], pT[:, h, :])], banks.free[b], tb[h], tw2)
                    tv = gt[h % 2][:, 0:256]
                    t = dve(lambda e, tv=tv, b=b, h=h: e.tensor_scalar(
                        tv, ps(b)[:, 0:256], G[:, G_POOL + h:G_POOL + h + 1], None, ALU.mult), t)
                    banks.give(b, t)
                    t = act(lambda e, tv=tv, h=h: e.copy(yph[:, h, :], tv), t)
                    dve(lambda e, tv=tv, h=h: e.tensor_tensor(ypl[:, h, :], tv, yph[:, h, :].bitcast(F), ALU.subtract), t)
            release(u, pe.tok())
            release(u2, pe.tok())

        def branch(br, c, y, nk, t_y):
            n = n_gate[0]
            n_gate[0] += 1
            src = gate_b[0, br:br + 1, 512 * c:512 * c + 512].to_broadcast([P, 512])
            t_gb = load(gbt[n % 2], src, gb_free[n % 2])
            bg, t_g = yield from stream_tokens(("gate", br, c), (hTh, hTl), 8, 512)
            for i in range(2):
                s = gt[i]
                t = dve(lambda e, s=s, b=bg[i]: e.tensor_tensor(s, ps(b)[:, :], gbt[n % 2], ALU.add), t_g, t_gb)
                gb_free[n % 2] = t
                banks.give(bg[i], t)
                t_s = act(lambda e, s=s: e.activation(s, s, ACT.Tanh, scale=0.5), t)
            bb, t_b = yield from stream_tokens(("br", br, c), y, nk, 512, t_y)
            for i in range(2):
                s = gt[i]
                m = merged[:, i, 512 * c:512 * c + 512]
                t = dve(lambda e, s=s: e.tensor_scalar(s, s, 0.5, 0.5, ALU.mult, ALU.add), t_s)
                o = m if br == 0 else s
                t = dve(lambda e, s=s, b=bb[i], o=o: e.tensor_tensor(o, s, ps(b)[:, :], ALU.mult), t_b)
                banks.give(bb[i], t)
                if br:
                    dve(lambda e, s=s, m=m: e.tensor_tensor(m, m, s, ALU.add))

        def middle():
            yield from pooling()
            t_yp = dve.tok()
            for c in range(2):
                yield from branch(0, c, (yph, ypl), 4, t_yp)
            for c in range(2):
                yield from branch(2, c, (ymh, yml), 4, t_ym)

        fill = middle()
        beside(attention(8, m_scores, m_soften, m_values, m_finish), fill, 2)
        t_mla = dve.tok()
        whole(fill)
        for c in range(2):
            whole(branch(1, c, (mTh, mTl), 8, t_mla))
        t = transposed(merged, 8, None, (hTh, hTl), dve.tok())
        t_sb = pe.tok()
        d_gffn = load(gb[:, 0, :], grow[0:1, :].to_broadcast([P, 1024]), t[1])
        d_gfin = load(gb[:, 1, :], grow[1:2, :].to_broadcast([P, 1024]), t[1])
        t_x = [None, None]
        wr = big[:, 0:288].rearrange("p (k n) -> p k n", k=8)
        d_wr = load(wr, w_route.rearrange("p (k n) -> p k n", k=8), t_sb)
        d_br = load(rt[:, 0:36], b_route.to_broadcast([P, 36]), dve.tok())
        for c in range(2):
            bs, tt = whole(stream_tokens(("out", c), (hTh, hTl), 8, 512, t[0], later=t[1]))
            for i, b in enumerate(bs):
                xs = X[:, i, 512 * c:512 * c + 512]
                t_x[i] = t2 = dve(lambda e, xs=xs, b=b: e.tensor_tensor(xs, xs, ps(b)[:, :], ALU.add), tt)
                banks.give(b, t2)
        for z in range(EXT):
            free_slots.append((RAW + z, pe.tok()))
        issue()

        h2T = big[:, 512:2560].rearrange("p (t n) -> p t n", t=8)
        rs, t = rstd_halves([X[:, 0, :], X[:, 1, :]], 1024, [t_x[0]], [t_x[1]])
        t_h2 = [dve(lambda e, i=i, rs=rs: e.scalar_tensor_tensor(
            H[:, i, :].rearrange("p (k c) -> p k c", k=8), X[:, i, :].rearrange("p (c k) -> p k c", k=8), rs[i],
            gb[:, 0, :].rearrange("p (c k) -> p k c", k=8), ALU.mult, ALU.mult), t[i], d_gffn) for i in range(2)]
        t = transposed(H, 8, None, (h2T,), d_wr, halves=t_h2)
        b = banks.take()
        for i in range(2):
            t = group(ps(b)[:, 64 * i:64 * i + 36], [(h2T[:, k, P * i:P * i + P], wr[:, k, :]) for k in range(8)],
                      banks.free[b], act.tok())
        R = rt[:, 64:640]

        def col(a, n):
            return R[:, a:a + n]

        def v2(a, n):
            return R[:, a:a + 2 * n].rearrange("p (i n) -> p i n", i=2)

        L, OG, EM, O1, O2, M, W, PX = v2(0, 36), v2(72, 4), v2(80, 32), v2(144, 32), v2(208, 32), v2(272, 32), v2(336, 32), v2(400, 32)
        E4, TT = v2(464, 4), v2(472, 32)
        g1, gs, m1, m2, tm_, pg, ex = (v2(536 + 2 * n, 1) for n in range(7))
        rank = C[:, C_RANK:C_RANK + 32].unsqueeze(1).to_broadcast([P, 2, 32])

        def bc(a, n):
            return a.to_broadcast([P, 2, n])

        dve(lambda e, b=b: e.tensor_tensor(L, ps(b)[:, 0:128].rearrange("p (i n) -> p i n", i=2)[:, :, 0:36],
                                           rt[:, 0:36].unsqueeze(1).to_broadcast([P, 2, 36]), ALU.add), t, d_br)
        banks.give(b, dve.tok())
        gl, el = L[:, :, 0:4], L[:, :, 4:36]

        def pick(vals, top, onehot, tmp, n):
            dve(lambda e: e.tensor_reduce(top, vals, AX, ALU.max))
            dve(lambda e: e.tensor_tensor(tmp, vals, bc(top, n), ALU.is_equal))
            dve(lambda e: e.tensor_tensor(tmp, tmp, rank[:, :, 0:n], ALU.mult))
            dve(lambda e: e.tensor_reduce(tm_, tmp, AX, ALU.max))
            dve(lambda e: e.tensor_tensor(onehot, tmp, bc(tm_, n), ALU.is_equal))

        pick(gl, g1, OG, E4, 4)
        dve(lambda e: e.tensor_tensor(E4, gl, bc(g1, 4), ALU.subtract))
        t = act(lambda e: e.activation(E4, E4, ACT.Exp), dve.tok())
        dve(lambda e: e.tensor_reduce(gs, E4, AX, ALU.add), t)
        dve(lambda e: e.reciprocal(pg, gs))
        dve(lambda e: e.tensor_scalar(OG, OG, -NEG, NEG, ALU.mult, ALU.add))
        for i in range(2):
            dve(lambda e, i=i: e.tensor_tensor(EM[:, i, :].rearrange("p (g k) -> p g k", g=4),
                                               el[:, i, :].rearrange("p (g k) -> p g k", g=4),
                                               OG[:, i, :].unsqueeze(2).to_broadcast([P, 4, 8]), ALU.add))
        pick(EM, m1, O1, TT, 32)
        dve(lambda e: e.tensor_scalar(TT, O1, 2 * NEG, None, ALU.mult))
        dve(lambda e: e.tensor_tensor(EM, EM, TT, ALU.add))
        pick(EM, m2, O2, TT, 32)
        dve(lambda e: e.tensor_tensor(ex, m2, m1, ALU.subtract))
        t = act(lambda e: e.activation(ex, ex, ACT.Exp), dve.tok())
        dve(lambda e: e.tensor_scalar(gs, ex, 1.0, None, ALU.add), t)
        dve(lambda e: e.reciprocal(gs, gs))
        dve(lambda e: e.tensor_tensor(m1, pg, gs, ALU.mult))
        dve(lambda e: e.tensor_tensor(m2, m1, ex, ALU.mult))
        t_M = dve(lambda e: e.tensor_tensor(M, O1, O2, ALU.add))
        dve(lambda e: e.tensor_tensor(O1, O1, bc(m1, 32), ALU.mult))
        dve(lambda e: e.tensor_tensor(O2, O2, bc(m2, 32), ALU.mult))
        t_W = dve(lambda e: e.tensor_tensor(W, O1, O2, ALU.add))
        tri, ones = C[:, C_TRI:C_TRI + P], C[:, C_ONE:C_ONE + 1].to_broadcast([P, P])
        b = banks.take()
        group(ps(b)[:, 0:32], [(tri, M[:, 0, :])], banks.free[b], t_M)
        group(ps(b)[:, 32:64], [(ones, M[:, 0, :]), (tri, M[:, 1, :])])
        t = group(ps(b)[:, 64:96], [(ones, M[:, 0, :]), (ones, M[:, 1, :])])
        dve(lambda e: e.tensor_scalar(PX, M, -1000.0, 1000.0, ALU.mult, ALU.add), t)
        dve(lambda e, b=b: e.tensor_tensor(PX, PX, ps(b)[:, 0:64].rearrange("p (i n) -> p i n", i=2), ALU.add))
        t_px = dve.tok()
        dve(lambda e, b=b: e.tensor_reduce(TT[:, 0, 0:1], ps(b)[:, 64:96], AX, ALU.max))
        banks.give(b, dve.tok())
        t_flag = dve(lambda e: e.tensor_copy(flag[:, :], TT[:, 0, 0:1]))

        MO = big[:, 2560:4608].rearrange("p (i n) -> p i n", i=2)
        sel = [big[:, 4608 + 512 * z:5120 + 512 * z] for z in range(2)]
        XE = [big[:, 5632 + 1024 * z:6656 + 1024 * z].rearrange("p (t n) -> p t n", t=8) for z in range(2)]
        CM = [big[:, 7680 + 256 * z:7936 + 256 * z] for z in range(2)]
        YE = big[:, 8192:9216]
        AE = [T[0][:, 0:256], T[1][:, 0:256]]
        AT = [S[0][:, 256:512], S[1][:, 256:512]]
        xe_tok, cm_tok = {}, {}
        iota = C[:, C_IOTA:C_IOTA + CAP]

        def select(g):
            z = g % 2
            for i in range(2):
                s_ = sel[z][:, 128 * i:128 * i + 128].rearrange("p (e s) -> p e s", e=4)
                w_ = sel[z][:, 256 + 128 * i:384 + 128 * i].rearrange("p (e s) -> p e s", e=4)
                px = PX[:, i, 4 * g:4 * g + 4].unsqueeze(2).to_broadcast([P, 4, CAP])
                wt = W[:, i, 4 * g:4 * g + 4].unsqueeze(2).to_broadcast([P, 4, CAP])
                io = iota.unsqueeze(1).to_broadcast([P, 4, CAP])
                dve(lambda e, s_=s_, px=px, io=io: e.tensor_tensor(s_, io, px, ALU.is_equal), sel_free[z])
                t = dve(lambda e, s_=s_, w_=w_, wt=wt: e.tensor_tensor(w_, s_, wt, ALU.mult))
            return t

        sel_free = [None, None]

        def gather(g, t):
            z = g % 2
            for a in range(2):
                b = banks.take()
                for j in range(4):
                    tt = group(ps(b)[:, P * j:P * j + P],
                               [(H[:, i, P * (4 * a + j):P * (4 * a + j) + P], sel[z][:, P * i:P * i + P]) for i in range(2)],
                               banks.free[b], t, *t_h2)
                t3 = copy_out(XE[z][:, 4 * a:4 * a + 4, :], b, ps(b)[:, :].rearrange("p (j n) -> p j n", j=4), tt,
                              xe_free[z])
            b = banks.take()
            for i in range(2):
                tt = pe(lambda e, b=b, i=i: e.transpose(ps(b)[:, P * i:P * i + P], sel[z][:, 256 + P * i:384 + P * i], ident),
                        banks.free[b], inc=i)
            sel_free[z] = tt
            xe_tok[g] = copy_out(CM[z], b, ps(b)[:, 0:256], tt, cm_free[z])

        xe_free, cm_free = [None, None], [None, None]

        def experts(g):
            z = g % 2
            b = banks.take()
            for half_ in range(2):
                for t4 in range(4):
                    u, w, tw = next_raw(("eg", "eu")[half_])
                    w = w.rearrange("p e (k n) -> p e k n", k=2)
                    for k in range(2):
                        kk = 2 * t4 + k
                        for j in range(4):
                            end = k == 1 and j == 3
                            t = pe(lambda e, w=w, k=k, kk=kk, j=j, half_=half_: e.matmul(
                                ps(b)[32 * j:32 * j + 32, 256 * half_:256 * half_ + 256],
                                XE[z][:, kk, 32 * j:32 * j + 32], w[:, j, k, :], start=(kk == 0), stop=(kk == 7)),
                                banks.free[b], tw, xe_tok[g], inc=1 if end else 0)
                    release(u, t)
            xe_free[z] = t
            a_, at_ = AE[z], AT[z]
            t2 = act(lambda e: e.activation(a_, ps(b)[:, 0:256], ACT.Silu), t, dve.tok())
            t2 = dve(lambda e: e.tensor_tensor(a_, a_, ps(b)[:, 256:512], ALU.mult), t2)
            banks.give(b, t2)
            return t2

        def experts_down(g, t2):
            z = g % 2
            a_, at_ = AE[z], AT[z]
            b = banks.take()
            for k in range(2):
                t = pe(lambda e, b=b, k=k: e.transpose(ps(b)[:, P * k:P * k + P], a_[:, P * k:P * k + P], ident),
                       banks.free[b], t2, inc=k)
            t = copy_out(at_, b, ps(b)[:, 0:256], t)
            for c in range(2):
                b = banks.take()
                for k in range(2):
                    u, w, tw = next_raw("ed")
                    for j in range(4):
                        tt = pe(lambda e, b=b, w=w, k=k, j=j: e.matmul(
                            ps(b)[32 * j:32 * j + 32, :], at_[:, P * k + 32 * j:P * k + 32 * j + 32], w[:, j, :],
                            start=(k == 0), stop=(k == 1)), banks.free[b], tw, t, inc=1 if j == 3 else 0)
                    release(u, tt)
                t_y = copy_out(YE[:, 512 * c:512 * c + 512], b, ps(b)[:, :], tt, ye_free[0])
            return t_y

        ye_free, t_mo = [None], [None, None]

        def combine(g, t_y):
            z = g % 2
            for i in range(2):
                for c in range(2):
                    b = banks.take()
                    t = group(ps(b)[:, :], [(CM[z][:, P * i:P * i + P], YE[:, 512 * c:512 * c + 512])], banks.free[b], t_y)
                    o = MO[:, i, 512 * c:512 * c + 512]
                    prior = X[:, i, 512 * c:512 * c + 512] if g == 0 else o
                    t = dve(lambda e, o=o, b=b, prior=prior: e.tensor_tensor(o, prior, ps(b)[:, :], ALU.add), t)
                    banks.give(b, t)
                t_mo[i] = t
            ye_free[0] = cm_free[z] = pe.tok()

        gather(0, select(0))
        for g in range(8):
            if g < 7:
                t_s = select(g + 1)
            t2 = experts(g)
            if g < 7:
                gather(g + 1, t_s)
            combine(g, experts_down(g, t2))

        fast = {q: q.n for q in (pe, act, dve)}
        marks = {q: len(q.items) for q in (pe, act, dve)}
        f_go, f_w, f_g, f_s, f_a, f_y, f_end = (sem(n) for n in ("f_go", "f_w", "f_g", "f_s", "f_a", "f_y", "f_end"))
        fast_pe, fast_dve = pe.tok(), dve.tok()
        AG = junk[:, 0:512].rearrange("p (k n) -> p k n", k=2)
        WC = T[0][:, 0:64].rearrange("p (i n) -> p i n", i=2)
        WD = T[0][:, 64:128].rearrange("p (i n) -> p i n", i=2)
        limit = -1 if force_general else CAP

        def general(eng, body):
            eng.wait_ge(*t_flag)
            n = eng.value_load(flag[0:1, 0:1], min_val=0, max_val=256)
            with eng.If(n > limit):
                body(eng)

        wg_, wu_, wd_ = raw[:, 0, :], raw[:, 1, :], raw[:, 2, :]

        def general_sp(e):
            e.wait_ge(*fast_dve)
            e.wait_ge(*fast_pe)
            with e.Fori(0, 32) as n:
                e.wait_ge(f_go, 1)
                e.sem_clear(f_go)
                e.dma_start(wg_, w_gate_e[0, bass.ds(n, 1)].rearrange("e (p k) n -> p (e k n)", p=P)).then_inc(f_w, 16)
                e.dma_start(wu_, w_up_e[0, bass.ds(n, 1)].rearrange("e (p k) n -> p (e k n)", p=P)).then_inc(f_w, 16)
                e.dma_start(wd_.rearrange("p (k n) -> p k n", k=2),
                            w_down_e[0, bass.ds(n, 1)].rearrange("e (k p) n -> p (e k) n", p=P)).then_inc(f_w, 16)
            e.wait_ge(f_go, 1)

        def general_pe(e):
            wg, wu = (v.rearrange("p (k n) -> p k n", k=8) for v in (wg_, wu_))
            wd = wd_.rearrange("p (k n) -> p k n", k=2)
            with e.Fori(0, 32):
                e.wait_ge(f_w, 48)
                e.sem_clear(f_w)
                for s_, w in enumerate((wg, wu)):
                    for j in range(2):
                        for k in range(8):
                            t = e.matmul(ps(s_)[:, 256 * j:256 * j + 256], w[:, k, P * j:P * j + P], h2T[:, k, :],
                                         start=(k == 0), stop=(k == 7))
                t.then_inc(f_g, 1)
                e.wait_ge(f_a, 1)
                e.sem_clear(f_a)
                for i in range(2):
                    for c in range(2):
                        for k in range(2):
                            t = e.matmul(ps(2 + 2 * i + c)[:, :], AG[:, k, P * i:P * i + P],
                                         wd[:, k, 512 * c:512 * c + 512], start=(k == 0), stop=(k == 1))
                t.then_inc(f_y, 1)

        def general_act(e):
            with e.Fori(0, 32):
                e.wait_ge(f_g, 1)
                e.sem_clear(f_g)
                e.activation(AG, ps(0)[:, :].rearrange("p (k n) -> p k n", k=2), ACT.Silu).then_inc(f_s, 1)

        def general_dve(e):
            chain = [0]
            e.wait_ge(*fast_pe)
            e.wait_ge(act.sem, fast[act])
            e.wait_ge(*fast_dve)
            e.tensor_copy(WC, W).then_inc(f_end, 1)
            e.wait_ge(f_end, 1)
            e.tensor_copy(MO, X[:, :, :]).then_inc(f_end, 1)
            e.wait_ge(f_end, 2)
            e.sem_clear(f_end)
            with e.Fori(0, 32):
                e.sem_inc(f_go, 1)
                e.wait_ge(f_s, 1)
                e.sem_clear(f_s)
                e.tensor_tensor(AG, AG, ps(1)[:, :].rearrange("p (k n) -> p k n", k=2), ALU.mult).then_inc(f_a, 1)
                e.wait_ge(f_y, 1)
                e.sem_clear(f_y)
                for i in range(2):
                    for c in range(2):
                        o = MO[:, i, 512 * c:512 * c + 512]
                        e.scalar_tensor_tensor(o, ps(2 + 2 * i + c)[:, :], WC[:, i, 0:1], o, ALU.mult,
                                               ALU.add).then_inc(f_end, 1)
                e.tensor_copy(WD[:, :, 0:31], WC[:, :, 1:32]).then_inc(f_end, 1)
                e.wait_ge(f_end, 5)
                e.tensor_copy(WC[:, :, 0:31], WD[:, :, 0:31]).then_inc(f_end, 1)
                e.wait_ge(f_end, 6)
                e.sem_clear(f_end)
            e.sem_inc(f_go, 1)

        split_upto(at["piece"] + AHEAD, pe.tok())
        t_all = dve.tok()
        rs, t = rstd_halves([MO[:, 0, :], MO[:, 1, :]], 1024, [t_mo[0]], [t_mo[1]])
        t = [dve(lambda e, i=i, rs=rs: e.scalar_tensor_tensor(X[:, i, :], MO[:, i, :], rs[i], gb[:, 1, :], ALU.mult, ALU.mult),
                 t[i], d_gfin) for i in range(2)]
        d_pm = load(gb[:, 0, :], grow[2:3, :].to_broadcast([P, 1024]), t_all)
        d_pf = load(gb[:, 1, :], grow[3:4, :].to_broadcast([P, 1024]), t[1])
        rs, t = rstd_halves([X[:, 0, :], X[:, 1, :]], 1024, [t[0]], [t[1]], one="act")
        t = scaled(H, X, rs, t, pe.tok())
        t_h = transposed(H, 8, G_MIX2, (hTh, hTl), halves=t)
        bias = big[:, 0:4096].rearrange("p (h n) -> p h n", h=16)
        d_bias = load(bias, rel_ext, dve.tok(), pe.tok())
        t_bias = pool(lambda e: e.memset(bias[0:64, :, 192:256], NEG), d_bias)
        qT = big[:, 4096:6144].rearrange("p (t n) -> p t n", t=8)
        kT = big[:, 6144:8192].rearrange("p (t n) -> p t n", t=8)
        v2_ = H
        def qk(c):
            bs, tt = yield from stream_features(("qkv", c), (hTh, hTl), 8, 512, t_h[0], later=t_h[1])
            for j, b in enumerate(bs):
                d = (qT, kT)[c // 2][:, 4 * (c % 2) + j, :]
                copy_out(d, b, ps(b)[:, 0:256], tt)

        def vals(c):
            bs, tt = yield from stream_tokens(("qkv", 4 + c), (hTh, hTl), 8, 512)
            for i, b in enumerate(bs):
                toks["q", c] = copy_out(v2_[:, i, 512 * c:512 * c + 512], b, ps(b)[:, :], tt)

        whole(qk(0))
        whole(qk(2))
        whole(vals(0))

        def r_scores(h):
            b = banks.take()
            o = 64 * (h % 2)
            for i in range(2):
                t = group(ps(b)[:, 0:128] if i == 0 else ps(b)[:, 128:384],
                          [(qT[o:o + 64, h // 2, P * i:P * i + P], kT[o:o + 64, h // 2, 0:P * (i + 1)])],
                          banks.free[b], toks["q", h // 8])
            return b, t

        def r_soften(h, b, t, s, sfree):
            mx = st[:, 80 + 2 * (h % 4):82 + 2 * (h % 4)]
            dve(lambda e: e.scalar_tensor_tensor(s[:, 0:128], ps(b)[:, 0:128], 0.125, bias[:, h, 128:256], ALU.mult,
                                                 ALU.add), t, sfree, t_bias)
            t = dve(lambda e: e.scalar_tensor_tensor(s[:, 128:384], ps(b)[:, 128:384], 0.125, bias[:, h, :], ALU.mult,
                                                     ALU.add), free=True)
            banks.give(b, t)
            dve(lambda e: e.tensor_reduce(mx[:, 0:1], s[:, 0:128], AX, ALU.max, negate=True))
            t = dve(lambda e: e.tensor_reduce(mx[:, 1:2], s[:, 128:384], AX, ALU.max, negate=True), t, free=True)
            return causal_view(s), mx, t

        def r_values(h, pt, t):
            if h % 2 == 0:
                pv_bank[0] = banks.take()
            b = pv_bank[0]
            o = 64 * (h % 2)
            return causal_values(ps(b)[o:o + 64, 0:256], lambda k: v2_[:, k, 64 * h:64 * h + 64], pt, b, t)

        def r_finish(h, t):
            if h % 2:
                b = pv_bank[0]
                split_out(mTh[:, h // 2, :], mTl[:, h // 2, :], b, ps(b)[:, 0:256], t)

        def second_half():
            yield from qk(1)
            yield from qk(3)
            yield from vals(1)

        def first_o():
            for c in range(2):
                o_banks.append((yield from stream_tokens(("o", 0, c), (mTh, mTl), 4, 512, toks["o"], total=8))[0])

        o_banks = []
        att = attention(16, r_scores, r_soften, r_values, r_finish)
        fill = second_half()
        for step in range(8):
            next(att)
            for _ in range(2 - step % 2):
                next(fill, None)
        whole(fill)
        for step in range(8, 12):
            next(att)
        toks["o"] = dve.tok()
        beside(att, first_o(), 1)
        t_o = dve.tok()

        def squares(k, c, i, b, t):
            return square_act(k[:, 2 * c + i:2 * c + i + 1], ps(b)[:, :], 512, t)

        def add_normed(k, bs, tsq, row, d_row, done):
            tr = [root(k[:, i:i + 1], k[:, 4 + i:5 + i], 1024, tsq[i], more=k[:, 2 + i:3 + i]) for i in range(2)]
            out_t = []
            for i in range(2):
                for c in range(2):
                    b = bs[c][i]
                    hs = H[:, i, 512 * c:512 * c + 512]
                    t = dve(lambda e, hs=hs, b=b, i=i, c=c: e.scalar_tensor_tensor(
                        hs, ps(b)[:, :], k[:, 4 + i:5 + i], gb[:, row, 512 * c:512 * c + 512], ALU.mult, ALU.mult),
                        tr[i], d_row, free=c > 0)
                    banks.give(b, t)
                out_t.append(dve(lambda e, i=i: e.tensor_tensor(X[:, i, :], X[:, i, :], H[:, i, :], ALU.add), t))
                done(i, out_t[i])
            return out_t

        k_o, tsq = columns(), {}
        tt = None
        for c in range(2):
            _, t1 = whole(stream_tokens(("o", 4, c), (mTh, mTl), 4, 512, t_o, k0=4, total=8, bs=o_banks[c]))
            for i in range(2):
                tsq[i] = squares(k_o, c, i, o_banks[c][i], t1)
        t = add_normed(k_o, o_banks, tsq, 0, d_pm, lambda i, t: None)
        rs, t = rstd_halves([X[:, 0, :], X[:, 1, :]], 1024, [t[0]], [t[1]], one="act")
        t = scaled(H, X, rs, t)
        t_h = transposed(H, 8, G_FFN2, (hTh, hTl), halves=t)

        acc = [banks.take() for _ in range(4)]
        ah = [frb[:, 512 * z:512 * z + 512].rearrange("p (k n) -> p k n", k=2) for z in range(2)]
        al = [frb[:, 1024 + 512 * z:1536 + 512 * z].rearrange("p (k n) -> p k n", k=2) for z in range(2)]
        a_free, acc_tok = [None, None], {}

        def ffn_down(c, t):
            z = c % 2
            for k in range(2):
                q, h, l, tp, _, _ = next_piece(("fd", c))
                for i in range(2):
                    sl = slice(P * i, P * i + P)
                    for cc in range(2):
                        for n, (a, w) in enumerate(((ah, h), (al, h), (ah, l))):
                            end = n == 2 and (c == 10 or (i == 1 and cc == 1))
                            tok = pe(lambda e, b=acc[2 * i + cc], a=a[z][:, k, sl], w=w[:, 0, 512 * cc:512 * cc + 512],
                                     s0=(c == 0 and k == 0 and n == 0), s1=(c == 10 and k == 1 and n == 2):
                                     e.matmul(ps(b)[:, :], a, w, start=s0, stop=s1),
                                     tp, t, banks.free[acc[2 * i + cc]] if c == 0 else None, inc=1 if end else 0)
                        acc_tok[i, cc] = tok
                done_piece(q, tok)
            a_free[z] = tok

        for c in range(12):
            z = c % 2
            if c < 11:
                bg, _ = whole(stream_features(("fg", c), (hTh, hTl), 8, 256, t_h[0], later=t_h[1]))
                bu, tt = whole(stream_features(("fu", c), (hTh, hTl), 8, 256))
                for j in range(2):
                    s, o = S[j][:, 0:256], S[j][:, 256:512]
                    t2 = act(lambda e, s=s, b=bg[j]: e.activation(s, ps(b)[:, 0:256], ACT.Silu), tt, dve.tok())
                    banks.give(bg[j], t2)
                    t2 = dve(lambda e, s=s, o=o, b=bu[j]: e.tensor_tensor(o, s, ps(b)[:, 0:256], ALU.mult), t2)
                    banks.give(bu[j], t2)
                    t2 = act(lambda e, o=o, j=j, z=z: e.copy(ah[z][:, j, :], o), t2, a_free[z])
                    t2 = dve(lambda e, o=o, j=j, z=z: e.tensor_tensor(al[z][:, j, :], o, ah[z][:, j, :].bitcast(F),
                                                                      ALU.subtract), t2)
            if c:
                ffn_down(c - 1, t_a)
            t_a = t2
        k_f = columns()
        for i in range(2):
            for cc in range(2):
                tsq[i] = squares(k_f, cc, i, acc[2 * i + cc], acc_tok[i, cc])
        s_out = sem("s_out")
        ov = out.rearrange("a (i p) n -> p (a i) n", p=P)
        add_normed(k_f, [[acc[cc], acc[2 + cc]] for cc in range(2)], tsq, 1, d_pf,
                   lambda i, t: sp(lambda e: e.dma_start(ov[:, i, :], X[:, i, :]).then_inc(s_out, 16), t))

        def emit(eng, q, mark, body):
            rest = q.items[mark:]
            q.items = q.items[:mark]
            q.emit(eng)
            general(eng, body)
            q.items = rest
            q.emit(eng)

        def emit_sp(eng, items, seen):
            for fn, waits in items:
                for s, val in waits:
                    if val > seen.get(id(s), 0):
                        eng.wait_ge(s, val)
                        seen[id(s)] = val
                fn(eng)

        first_late = at["late_sp"]
        block = ctx.enter_context(nc.Block())

        @block.sync
        def _(e):
            seen = {}
            emit_sp(e, sp_items[:first_late], seen)
            general(e, general_sp)
            emit_sp(e, sp_items[first_late:], seen)
            e.wait_ge(s_out, 32)

        @block.tensor
        def _(e):
            emit(e, pe, marks[pe], general_pe)

        @block.scalar
        def _(e):
            emit(e, act, marks[act], general_act)

        @block.vector
        def _(e):
            emit(e, dve, marks[dve], general_dve)

        @block.gpsimd
        def _(e):
            pool.emit(e)


def kernel(**inputs):
    import concourse.bacc as _bacc
    from concourse import mybir as _mybir
    from concourse.bass_utils import run_bass_kernel_spmd as _run

    a = {k: np.ascontiguousarray(v) for k, v in inputs.items()}

    def cols(*names):
        return np.ascontiguousarray(np.concatenate([a[n].reshape(-1, P).T for n in names], axis=1))

    c, pool = shape_constants()
    rel = a["rel_bias_2"][0]
    rel_ext = np.concatenate([np.repeat(rel[:, 191:192], 127, axis=1), rel[:, ::-1], np.repeat(rel[:, 0:1], 65, axis=1)],
                             axis=1)
    rel_ext = np.stack([rel_ext[:, 127 - p:383 - p] for p in range(P)])
    route = np.concatenate([a["w_router_group"][0], a["w_router_expert"][0]], axis=1)
    arrays = {
        "x": a["x"], "mem": a["mem"], "positions": np.ascontiguousarray(a["positions"].reshape(2, P).T),
        "w_in": a["w_in"], "gate_b": a["gate_b"], "w_uq": a["w_uq"], "w_uk": a["w_uk"], "w_uv": a["w_uv"],
        "pool_w": a["pool_w"], "w_mem_kv": a["w_mem_kv"], "w_br_pool": a["w_br_pool"], "w_br_mla": a["w_br_mla"],
        "w_br_mem": a["w_br_mem"], "w_out": a["w_out"], "w_gate_e": a["w_gate_e"], "w_up_e": a["w_up_e"],
        "w_down_e": a["w_down_e"], "w_qkv": a["w_qkv_2"], "w_o": a["w_o_2"], "w_gate": a["w_gate_2"],
        "w_up": a["w_up_2"], "w_down": a["w_down_2"],
        "gvec": cols("mix_norm_g", "mem_norm_g", "q_norm_g", "kv_norm_g", "pool_scale", "g_pre_mix_2", "g_pre_ffn_2"),
        "grow": np.ascontiguousarray(np.stack([a["ffn_norm_g"][0], a["final_norm_g"], a["g_post_mix_2"][0],
                                               a["g_post_ffn_2"][0]])),
        "w_route": np.ascontiguousarray(route.reshape(P, 288)),
        "b_route": np.ascontiguousarray(np.concatenate([a["b_router_group"], a["b_router_expert"]], axis=1)),
        "rel_ext": np.ascontiguousarray(rel_ext), "cst": c, "cst_pool": pool,
    }
    nc = _bacc.Bacc("TRN2", target_bir_lowering=False, num_devices=1)
    args = [nc.dram_tensor(f"in_{n}", v.shape, _mybir.dt.from_np(v.dtype), kind="ExternalInput").ap()
            for n, v in arrays.items()]
    args.append(nc.dram_tensor("out_0", (1, 256, 1024), _mybir.dt.float32, kind="ExternalOutput").ap())
    build(nc, *args)
    r = _run(nc, [{f"in_{n}": v for n, v in arrays.items()}], core_ids=[0])
    return r.results[0]["out_0"]
```

```python
from contextlib import ExitStack

import numpy as np

import concourse.bass as bass
from concourse import mybir

F = mybir.dt.float32
FR = mybir.dt.float32r
I32 = mybir.dt.int32
ALU = mybir.AluOpType
ACT = mybir.ActivationFunctionType
AX = mybir.AxisListType.X

P = 128
RAW = 6
EXT = 10
PIECES = 4
AHEAD = 3
FILL_X = 2
FILL_B = (2, 1, 2, 1, 2, 1, 2, 1)
TILE_AT = (7, 8, 10, 12, 14, 15, 18)
WARM = (24, 16, 12, 10, 3, 32, 18)
SPLITS = (0, 0, 0)
HOLD = 7
FILL_M = 2
CAP = 32
NEG = -1.0e30
EPS = 1e-6
MAGIC = 12582912.0
ABSENT = 3.0e38
TAKEN = 2.0e38
PI_IN = 3.1415925
TWO_PI_1 = 6.28125
TWO_PI_2 = float(np.float32(2 * np.pi - 6.28125))
TWO_PI_3 = float(2 * np.pi - 6.28125 - float(np.float32(2 * np.pi - 6.28125)))

C_ID, C_TRI, C_ONE, C_MASK, C_IOTA, C_RANK, C_INVF, C_END = np.cumsum([0, 128, 128, 1, 384, 32, 32, 32]).tolist()
G_MIX, G_MEM, G_Q, G_KV, G_POOL, G_MIX2, G_FFN2, G_END = np.cumsum([0, 8, 8, 3, 2, 4, 8, 8]).tolist()


def shape_constants():
    c = np.zeros((P, C_END), np.float32)
    c[:, C_ID:C_ID + P] = np.eye(P)
    c[:, C_TRI:C_TRI + P] = np.triu(np.ones((P, P)), 1)
    c[:, C_ONE] = 1.0
    causal = np.where(np.tril(np.ones((P, P))) > 0, 0.0, NEG)
    c[:, C_MASK:C_MASK + P] = causal
    c[:, C_MASK + 2 * P:C_MASK + 3 * P] = causal
    c[:, C_IOTA:C_IOTA + CAP] = np.arange(CAP)
    c[:, C_RANK:C_RANK + 32] = 32 - np.arange(32)
    c[:, C_INVF:C_INVF + 32] = (np.float32(1.0) / (np.float32(10000.0) ** (np.arange(0, 64, 2, dtype=np.float32) / np.float32(64)))).astype(np.float32)
    pool = np.zeros((4, 256, 256), np.float32)
    for g, w in enumerate((2, 4, 8, 16)):
        for s in range(256):
            n = min(s + 1, w)
            pool[g, s + 1 - n:s + 1, s] = np.float32(1.0) / np.float32(n)
            pool[g, s, s] -= 1.0
    pool = np.ascontiguousarray(pool.reshape(4, 2, P, 256).transpose(2, 1, 0, 3)).reshape(P, 2048)
    return c, pool


class Queue:

    def __init__(self, sem, chained):
        self.sem, self.chained, self.items, self.n = sem, chained, [], 0

    def tok(self):
        return (self.sem, self.n)

    def __call__(self, fn, *waits, inc=1, free=False):
        waits = [w for w in waits if w is not None]
        if self.chained and not free and self.n:
            waits.append(self.tok())
        self.items.append((fn, waits, inc))
        self.n += inc
        return self.tok()

    def emit(self, eng):
        seen = {}
        for fn, waits, inc in self.items:
            need = {}
            for sem, val in waits:
                key = id(sem)
                if val > seen.get(key, 0) and val > need.get(key, (None, 0))[1]:
                    need[key] = (sem, val)
            for key, (sem, val) in need.items():
                eng.wait_ge(sem, val)
                seen[key] = val
            ins = fn(eng)
            if inc:
                ins.then_inc(self.sem, inc)


class Banks:

    def __init__(self, tensors):
        self.t, self.free, self.order = tensors, [None] * len(tensors), list(range(len(tensors)))

    def take(self):
        b = self.order.pop(0)
        return b

    def give(self, b, tok):
        self.free[b] = tok
        self.order.append(b)


def build(nc, x, mem, positions, w_in, gate_b, w_uq, w_uk, w_uv, pool_w, w_mem_kv, w_br_pool, w_br_mla,
          w_br_mem, w_out, w_gate_e, w_up_e, w_down_e, w_qkv, w_o, w_gate, w_up, w_down,
          gvec, grow, w_route, b_route, rel_ext, cst, cst_pool, out, force_general=False):
    ctx = ExitStack()
    with ctx:
        def sb(name, shape, dt=F):
            return ctx.enter_context(nc.sbuf_tensor(name, shape, dt))

        def sem(name):
            return ctx.enter_context(nc.semaphore(name))

        pe = Queue(sem("q_pe"), False)
        act = Queue(sem("q_act"), True)
        dve = Queue(sem("q_dve"), True)
        pool = Queue(sem("q_pool"), True)
        sp_items = []

        def sp(fn, *waits):
            sp_items.append((fn, [w for w in waits if w is not None]))

        banks = Banks([ctx.enter_context(nc.psum_tensor(f"ps{i}", [P, 512], F)) for i in range(8)])

        def ps(b):
            return banks.t[b]

        raw = sb("raw", [P, RAW, 2048])
        with ExitStack() as rounded:
            wh, wl, fra, frb = (rounded.enter_context(nc.sbuf_tensor(n, s, FR)) for n, s in (
                ("wh", [P, PIECES, 1024]), ("wl", [P, PIECES, 1024]), ("fra", [P, 8192]), ("frb", [P, 4096])))
        ext = sb("ext", [P, EXT, 2048])
        hTh, hTl = (fra[:, a:a + 2048].rearrange("p (t n) -> p t n", t=8) for a in (0, 2048))
        mTh, mTl = (fra[:, a:a + 2048].rearrange("p (t n) -> p t n", t=8) for a in (4096, 6144))
        ymh, yml = (frb[:, a:a + 1024].rearrange("p (t n) -> p t n", t=4) for a in (0, 1024))
        moh, mol = (frb[:, a:a + 2048].rearrange("p (t n) -> p t n", t=8) for a in (0, 2048))
        yph, ypl = (frb[:, a:a + 1024].rearrange("p (t n) -> p t n", t=4) for a in (2048, 3072))
        X = sb("X", [P, 2, 1024])
        H = sb("H", [P, 2, 1024])
        junk = sb("junk", [P, 1024])
        C = sb("C", [P, C_END])
        G = sb("G", [P, G_END])
        st = sb("st", [P, 96])
        big = sb("big", [P, 9984])
        S3 = sb("S3", [P, 3, 512])
        S = [S3[:, i, :] for i in range(3)]
        scr = S3[:, 0:2, :].rearrange("p a n -> p (a n)")
        T = S
        PT = [junk[:, 0:512], junk[:, 512:1024]]
        cs = sb("cs", [P, 2, 2, 32])
        posi = sb("posi", [P, 2], I32)
        gb = sb("gb", [P, 2, 1024])
        rt = sb("rt", [P, 640])
        flag = sb("flag", [P, 1], I32)

        ident = C[:, C_ID:C_ID + P]

        def load(dst, src, *waits):
            s = sem(f"d_{len(sp_items)}")
            sp(lambda e: e.dma_start(dst, src).then_inc(s, 16), *waits)
            return (s, 16)

        mv, xv_ = (v.rearrange("a (i p) n -> p (a i) n", p=P) for v in (mem, x))
        d_mem = [load(H[:, i, :], mv[:, i, :]) for i in range(2)]
        d_g = load(G[:, :], gvec)
        d_c = load(C[:, :], cst)

        s_raw = [sem(f"s_raw{i}") for i in range(RAW + EXT)]
        raw_count, raw_tok, slot_of = [0] * (RAW + EXT), {}, {}
        free_slots = [(i, None) for i in range(RAW)]
        units, pieces = [], []
        taken = set()
        at = {"piece": 0, "loaded": 0, "split": 0, "late": None, "late_sp": None, "experts": None}

        def unit(key, src, shape, split):
            units.append((key, src, shape, split))
            if split:
                per = max(1, 1024 // shape[1])
                for a in range(0, shape[0], per):
                    pieces.append((len(units) - 1, a, min(per, shape[0] - a)))

        def raw_view(u):
            k, n = units[u][2]
            z = slot_of[u]
            v = raw[:, z, 0:k * n] if z < RAW else ext[:, z - RAW, 0:k * n]
            return v.rearrange("p (k n) -> p k n", k=k)

        def issue():
            while True:
                first = next(u for u in range(at["loaded"], len(units) + 1) if u not in raw_tok)
                at["loaded"] = first
                early = next((u for u in range(max(first, at["experts"]), at["late"]) if u not in raw_tok), None)
                for n, (z, tok) in enumerate(free_slots):
                    u = first if z < RAW else early
                    if u is not None and u < len(units):
                        break
                else:
                    return
                free_slots.pop(n)
                slot_of[u] = z
                src = units[u][1]
                if u == at["late"]:
                    at["late_sp"] = len(sp_items)
                if len(src.shape) == 4:
                    parts = [(raw_view(u)[:, a, :].rearrange("p (b c) -> p b c", b=src.shape[2]), src[:, a])
                             for a in range(src.shape[1])]
                else:
                    parts = [(raw_view(u), src)]
                for dst, part in parts:
                    sp(lambda e, dst=dst, part=part, z=z: e.dma_start(dst, part).then_inc(s_raw[z], 16), tok)
                raw_count[z] += 16 * len(parts)
                raw_tok[u] = (s_raw[z], raw_count[z])

        def landed(u):
            return raw_tok[u]

        def release(u, tok):
            free_slots.append((slot_of[u], tok))
            issue()

        toks = {}
        wfree = [None] * PIECES
        piece_tok = {}

        def split_upto(n, *more):
            while at["split"] <= min(n, len(pieces) - 1):
                q = at["split"]
                u, a, k = pieces[q]
                if u not in raw_tok:
                    return
                if isinstance(wfree[q % PIECES], str):
                    return
                cols = units[u][2][1]
                v = raw_view(u)[:, a:a + k, :]
                h = wh[:, q % PIECES, 0:k * cols].rearrange("p (k n) -> p k n", k=k)
                l = wl[:, q % PIECES, 0:k * cols].rearrange("p (k n) -> p k n", k=k)
                t = act(lambda e, h=h, v=v: e.copy(h, v), landed(u), wfree[q % PIECES], *more, free=True)
                t = dve(lambda e, h=h, l=l, v=v: e.tensor_tensor(l, v, h.bitcast(F), ALU.subtract), t,
                        landed(u), wfree[q % PIECES], free=True)
                wfree[q % PIECES] = "taken"
                piece_tok[q] = (h, l, t)
                at["split"] += 1
                if a + k == units[u][2][0]:
                    release(u, t)

        def next_piece(key):
            q = at["piece"]
            assert units[pieces[q][0]][0] == key, (units[pieces[q][0]][0], key)
            split_upto(q)
            at["piece"] += 1
            return (q,) + piece_tok[q] + pieces[q][1:]

        def done_piece(q, tok):
            wfree[q % PIECES] = tok
            split_upto(q + AHEAD)

        def next_raw(key):
            u = next(u for u in range(len(units)) if units[u][0] == key and u not in taken)
            taken.add(u)
            assert u in raw_tok, (u, at["loaded"], key)
            return u, raw_view(u), landed(u)

        def k8(w, c0, c1, key, split=True):
            v = w.rearrange("(k p) n -> p k n", p=P)
            nk = v.shape[1]
            for a in range(0, nk, 4):
                unit(key, v[:, a:a + 4, c0:c1], (min(4, nk - a), c1 - c0), split)

        for c in range(2):
            k8(w_mem_kv[0], 512 * c, 512 * c + 512, ("mkv", c))
        k8(w_in[0], 1216, 1728, "xq")
        k8(w_in[0], 512, 896, "qd")
        k8(w_in[0], 896, 1216, "kvd")
        uq = w_uq[0].rearrange("(k p) (h c) -> p k h c", p=P, h=8)
        k8(w_in[0], 0, 512, "pool")
        unit("uqr", uq[:, :, :, 128:192], (3, 512), True)
        unit("poolc", cst_pool.rearrange("p (k n) -> p k n", k=8), (8, 256), False)
        unit("poolw", pool_w[0].rearrange("g c d -> c g d"), (4, 128), False)
        for a in range(2):
            unit("uqn", uq[:, :, 4 * a:4 * a + 4, 0:128], (3, 512), True)
        g0 = w_in[0].rearrange("(k p) n -> p k n", p=P)[:, :, 1728:2240]
        for key, w in (("uk", w_uk), ("uv", w_uv)):
            for a in range(2):
                unit(key, w[0].rearrange("(k p) n -> p k n", p=P)[:, :, 512 * a:512 * a + 512], (2, 512), True)
        for a in (0, 4):
            unit(("gate", 0, 0), g0[:, a:a + 4], (4, 512), True)
        for br, w in ((0, w_br_pool), (2, w_br_mem), (1, w_br_mla)):
            for c in range(2):
                col = 1728 + 1024 * br + 512 * c
                if br or c:
                    k8(w_in[0], col, col + 512, ("gate", br, c))
                k8(w[0], 512 * c, 512 * c + 512, ("br", br, c))
        for c in range(2):
            k8(w_out[0], 512 * c, 512 * c + 512, ("out", c))
        at["experts"] = len(units)
        for g in range(8):
            for key, w in (("eg", w_gate_e), ("eu", w_up_e)):
                v = w[0, 4 * g:4 * g + 4].rearrange("e (p k) n -> p e (k n)", p=P)
                for t in range(4):
                    unit(key, v[:, :, 512 * t:512 * t + 512], (4, 512), False)
            v = w_down_e[0, 4 * g:4 * g + 4].rearrange("e (k p) n -> p e k n", p=P)
            for c in range(2):
                for t in range(2):
                    unit("ed", v[:, :, t, 512 * c:512 * c + 512], (4, 512), False)
        at["late"] = len(units)
        for c in (0, 2, 4, 1, 3, 5):
            k8(w_qkv[0], 512 * c, 512 * c + 512, ("qkv", c))
        for a in range(0, 8, 2):
            unit("o", w_o[0].rearrange("(k p) n -> p k n", p=P)[:, a:a + 2, :], (2, 1024), True)
        for c in range(12):
            if c < 11:
                for key, w in (("fg", w_gate), ("fu", w_up)):
                    unit((key, c), w[0].rearrange("(k p) n -> p k n", p=P)[:, :, 256 * c:256 * c + 256], (8, 256), True)
            if c:
                unit(("fd", c - 1), w_down[0, 256 * c - 256:256 * c, :].rearrange("(k p) n -> p k n", p=P), (2, 1024),
                     True)
        issue()
        d_x = [load(X[:, i, :], xv_[:, i, :]) for i in range(2)]
        d_pos = load(posi[:, :], positions)

        def group(o, pairs, *waits, check=True):
            t = None
            for n, (a, b) in enumerate(pairs):
                last = n == len(pairs) - 1
                t = pe(lambda e, a=a, b=b, n=n, last=last: e.matmul(
                    o, a, b, start=(n == 0), stop=last, skip_group_check=not check),
                    *(waits if n == 0 else ()), inc=1 if last else 0)
            return t

        def warm(n, *waits, src=None):
            src = C if src is None else src
            b = banks.take()
            for k in range(n):
                t = pe(lambda e, b=b: e.matmul(ps(b)[:, 0:P], src[:, 0:P], src[:, 0:P], start=True, stop=True),
                       banks.free[b], *waits, inc=k == n - 1)
            banks.give(b, t)

        def stream_tokens(key, aT, nk, cols, *waits, k0=0, total=None, bs=None, later=None):
            ah, al = aT
            total = total or nk
            first = list(waits)
            if bs is None:
                bs = [banks.take() for _ in range(2)]
                first += [banks.free[b] for b in bs]
            stop_k = k0 + nk
            while k0 < stop_k:
                q, h, l, t, _, k = next_piece(key)
                assert not (later and k0 < 4 < k0 + k)
                first += [later() if callable(later) else later] if k0 >= 4 else []
                ends = k0 + k == total
                for kk, i in ((kk, i) for i in range(2) for kk in range(k)) if ends else (
                        (kk, i) for kk in range(k) for i in range(2)):
                    sl = slice(P * i, P * i + P)
                    for n, (a, w) in enumerate(((ah, h), (al, h), (ah, l))):
                        s0, s1 = k0 + kk == 0 and n == 0, k0 + kk == total - 1 and n == 2
                        end = s1 or (kk == k - 1 and i == 1 and n == 2)
                        tok = pe(lambda e, o=ps(bs[i])[:, 0:cols], a=a[:, k0 + kk, sl], w=w[:, kk, :],
                                 s0=s0, s1=s1: e.matmul(o, a, w, start=s0, stop=s1),
                                 t, *first, inc=1 if end else 0)
                        first = []
                        if s1:
                            toks["end", i] = tok
                done_piece(q, tok)
                k0 += k
                yield
            return bs, tok

        def stream_features(key, aT, nk, cols, *waits, later=None):
            ah, al = aT
            m = cols // P
            bs = [banks.take() for _ in range(m)]
            first, k0 = list(waits) + [banks.free[b] for b in bs], 0
            while k0 < nk:
                q, h, l, t, _, k = next_piece(key)
                assert not (later and k0 < 4 < k0 + k)
                first += [later() if callable(later) else later] if k0 >= 4 else []
                for kk in range(k):
                    for j in range(m):
                        sl = slice(P * j, P * j + P)
                        for n, (a, w) in enumerate(((ah, h), (al, h), (ah, l))):
                            s0, s1 = k0 + kk == 0 and n == 0, k0 + kk == nk - 1 and n == 2
                            end = s1 or (kk == k - 1 and j == m - 1 and n == 2)
                            tok = pe(lambda e, o=ps(bs[j])[:, 0:256], a=a[:, k0 + kk, :], w=w[:, kk, sl],
                                     s0=s0, s1=s1: e.matmul(o, w, a, start=s0, stop=s1),
                                     t, *first, inc=1 if end else 0)
                            first = []
                done_piece(q, tok)
                k0 += k
                yield
            return bs, tok

        def whole(steps):
            while True:
                try:
                    next(steps)
                except StopIteration as end:
                    return end.value

        def beside(main, fill, n):
            for _ in main:
                for _ in range(n):
                    next(fill, None)

        def copy_out(o, b, src, *waits, eng=None):
            t = (eng or act)(lambda e: (e.copy if (eng or act) is act else e.tensor_copy)(o, src), *waits)
            banks.give(b, t)
            return t

        def split_out(oh, ol, b, src, *waits):
            t = act(lambda e: e.copy(oh, src), *waits)
            t = dve(lambda e: e.tensor_tensor(ol, src, oh.bitcast(F), ALU.subtract), t)
            banks.give(b, t)
            return t
            return t

        turns = []
        half = st[:, 88:90]
        pool_last = [pool(lambda e: e.memset(half, -0.5))]

        def columns():
            c = 8 * (len(turns) % 10)
            turns.append(dve.tok())
            return st[:, c:c + 8]

        def square_act(acc, part, width, *waits, scratch=None):
            o = junk[:, 0:width] if scratch is None else scratch[:, 0:width]
            return act(lambda e: e.activation(o, part, ACT.Square, accum_out=acc), pool_last[0], *waits)

        def square_dve(acc, part, width, *waits):
            return dve(lambda e: e.tensor_tensor_reduce(scr[:, 0:width], part, part, 1.0, 0.0, ALU.mult, ALU.add, acc),
                       pool_last[0], pe.tok(), *waits)

        def root(ss, r, width, *waits, more=None):
            if more is not None:
                pool(lambda e: e.tensor_tensor(ss, ss, more, ALU.add), *waits)
            pool(lambda e: e.tensor_scalar(ss, ss, 1.0 / width, EPS, ALU.mult, ALU.add), *waits, turns[-5] if len(turns) > 4 else None)
            t = pool(lambda e: e.tensor_tensor(r, ss, half[:, 0:ss.shape[1]], ALU.pow))
            pool_last[0] = t
            return t

        def rstd(parts, width, *waits, scratch=None):
            k, n = columns(), len(parts)
            for i, part in enumerate(parts):
                t = square_act(k[:, i:i + 1], part, width, *waits, scratch=scratch)
            t = root(k[:, 0:n], k[:, 4:4 + n], width, t)
            return [k[:, 4 + i:5 + i] for i in range(n)], t

        def rstd_halves(parts, width, w0, w1, one="dve"):
            k = columns()
            ss = [k[:, i:i + 1] for i in range(2)]
            r = [k[:, 4 + i:5 + i] for i in range(2)]
            a0 = square_act(ss[0], parts[0], width, *w0)
            a1 = (square_dve if one == "dve" else square_act)(ss[1], parts[1], width, *w1)
            return r, [root(ss[0], r[0], width, a0), root(ss[1], r[1], width, a1)]

        def transposed(src, nt, gcol, keep_to, *waits, halves=None, only=None):
            toks_ = {}
            for a in range(0, nt, 4) if only is None else only:
                for i in range(2):
                    k = min(4, nt - a)
                    b = banks.take()
                    for j in range(k):
                        t = pe(lambda e, b=b, i=i, a=a, j=j: e.transpose(
                            ps(b)[:, P * j:P * j + P], src[:, i, P * (a + j):P * (a + j) + P], ident),
                            banks.free[b], *waits, halves[i] if halves else None, inc=1 if j == k - 1 else 0)
                    v = ps(b)[:, 0:k * P].rearrange("p (k n) -> p k n", k=k)
                    o = [d[:, a:a + k, P * i:P * i + P] for d in keep_to]
                    if gcol is None:
                        t = act(lambda e, o=o, v=v: e.copy(o[0], v), t)
                        if len(o) == 2:
                            t = dve(lambda e, o=o, v=v: e.tensor_tensor(o[1], v, o[0].bitcast(F), ALU.subtract), t)
                    else:
                        t0 = t
                        for j in range(k):
                            g = G[:, gcol + a + j:gcol + a + j + 1]
                            t = act(lambda e, o=o, v=v, g=g, j=j: e.activation(o[0][:, j, :], v[:, j, :], ACT.Copy,
                                                                              scale=g), t0, free=True)
                        for j in range(k if len(o) == 2 else 0):
                            g = G[:, gcol + a + j:gcol + a + j + 1]
                            t2 = dve(lambda e, o=o, v=v, g=g, j=j: e.scalar_tensor_tensor(
                                o[1][:, j, :], v[:, j, :], g, o[0][:, j, :].bitcast(F), ALU.mult, ALU.subtract),
                                t, free=True)
                        t = t2 if len(o) == 2 else t
                    banks.give(b, t)
                    toks_[a] = t
            return [toks_[a] for a in sorted(toks_)]

        def scaled(dst, src, rs, ts, *waits):
            return [dve(lambda e, i=i: e.tensor_scalar(dst[:, i, :], src[:, i, :], rs[i], None, ALU.mult), ts[i], *waits)
                    for i in range(2)]

        def attention(heads, scores, soften, values, finish):
            s_free, pt_free = [None] * 3, [None] * 2
            exps, norms, turned = {}, {}, {}
            for step in range(heads + 3):
                if step < heads:
                    b, t = scores(step)
                if 0 <= step - 2 < heads:
                    h = step - 2
                    parts, tn = norms.pop(h)
                    bt = banks.take()
                    for n, src in enumerate(parts):
                        t2 = pe(lambda e, bt=bt, n=n, src=src: e.transpose(ps(bt)[:, P * n:P * n + P], src, ident),
                                banks.free[bt], tn, inc=1 if n == len(parts) - 1 else 0)
                    s_free[h % 3] = t2
                    w = P * len(parts)
                    t3 = act(lambda e, bt=bt, h=h, w=w: e.copy(PT[h % 2][:, 0:w], ps(bt)[:, 0:w]), t2, pt_free[h % 2])
                    banks.give(bt, t3)
                    turned[h] = t3
                if step >= 3:
                    h = step - 3
                    tv = values(h, PT[h % 2], turned.pop(h))
                    pt_free[h % 2] = tv
                if step < heads:
                    view, mx, t = soften(step, b, t, S[step % 3], s_free[step % 3])
                    c = 4 * (step % 4)
                    for i in range(2):
                        t = act(lambda e, i=i, view=view, c=c, mx=mx: e.activation(
                            view[i][1], view[i][0], ACT.Exp, bias=mx[:, i:i + 1], scale=view[i][2],
                            accum_out=rt[:, c + i:c + i + 1]), t)
                    if view[0][3] is not None:
                        banks.give(view[0][3], t)
                    exps[step] = (view, c, t)
                if 0 <= step - 1 < heads:
                    h = step - 1
                    view, c, t = exps.pop(h)
                    dve(lambda e, c=c: e.reciprocal(rt[:, c + 2:c + 4], rt[:, c:c + 2]), t)
                    t = dve.tok()
                    for i in range(2):
                        tn = dve(lambda e, i=i, view=view, c=c: e.tensor_scalar(
                            view[i][1], view[i][1], rt[:, c + 2 + i:c + 3 + i], None, ALU.mult), t, free=True)
                    norms[h] = ([view[i][1][:, P * off:P * off + P] for i, off in view[2]], tn)
                if step >= 3:
                    finish(step - 3, tv)
                yield

        warm(WARM[0], pool(lambda e: e.memset(gb[:, 0, 0:P], 0.0)), src=gb[:, 0, :])
        rs, t = rstd_halves([H[:, 0, :], H[:, 1, :]], 1024, [d_mem[0]], [d_mem[1]])
        t = scaled(H, H, rs, t)
        t_mT = transposed(H, 8, G_MEM, (mTh, mTl), d_c, d_g, halves=t)
        t_h0 = pe.tok()
        warm(WARM[1])
        xkT = big[:, 0:1024].rearrange("p (t n) -> p t n", t=4)
        xv = big[:, 1024:2048].rearrange("p (t n) -> p t n", t=2)
        xqT = big[:, 2048:3072].rearrange("p (t n) -> p t n", t=4)
        bs, t = whole(stream_features(("mkv", 0), (mTh, mTl), 8, 512, t_mT[0], later=t_mT[1]))
        rs, t2 = rstd_halves([X[:, 0, :], X[:, 1, :]], 1024, [d_x[0]], [d_x[1]])
        for j, b in enumerate(bs):
            copy_out(xkT[:, j, :], b, ps(b)[:, 0:256], t)
        t2 = scaled(H, X, rs, t2, t_h0)

        fr = [big[:, 8000:8064].rearrange("p (i c) -> p i c", i=2), big[:, 8064:8128].rearrange("p (i c) -> p i c", i=2)]
        posf = st[:, 92:94]
        dve(lambda e: e.tensor_copy(posf, posi[:, :]), d_pos)
        for i in range(2):
            dve(lambda e, i=i: e.tensor_scalar(fr[0][:, i, :], C[:, C_INVF:C_INVF + 32], posf[:, i:i + 1], None,
                                               ALU.mult), d_c)
        for f, shift in ((0, 0.25), (1, 0.0)):
            o = cs[:, f, :, :]
            dve(lambda e, shift=shift: e.tensor_scalar(fr[1], fr[0], float(1 / (2 * np.pi)), shift, ALU.mult, ALU.add))
            dve(lambda e: e.tensor_scalar(fr[1], fr[1], MAGIC, None, ALU.add))
            dve(lambda e: e.tensor_scalar(fr[1], fr[1], -MAGIC, None, ALU.add))
            for n, c in enumerate((TWO_PI_1, TWO_PI_2, TWO_PI_3)):
                src = fr[0] if n == 0 else o
                dve(lambda e, src=src, c=c, o=o: e.scalar_tensor_tensor(o, fr[1], -c, src, ALU.mult, ALU.add))
            if f == 0:
                dve(lambda e, o=o: e.tensor_scalar(o, o, float(np.pi / 2), None, ALU.add))
            dve(lambda e, o=o: e.tensor_scalar(o, o, PI_IN, -PI_IN, ALU.min, ALU.max))
        t_cs0 = dve.tok()
        cosb = cs[:, 0, :, :]
        sinb = cs[:, 1, :, :]

        bs, t = whole(stream_tokens(("mkv", 1), (mTh, mTl), 8, 512))
        t_hT = transposed(H, 8, G_MIX, (hTh, hTl), halves=t2)
        for i, b in enumerate(bs):
            copy_out(xv[:, i, :], b, ps(b)[:, :], t)
        t_cs = act(lambda e: e.activation(cs[:, :, :, :], cs[:, :, :, :], ACT.Sin), t_cs0)
        bs, t = whole(stream_features("xq", (hTh, hTl), 8, 512, t_hT[0], later=t_hT[1]))
        for j, b in enumerate(bs):
            t_xq = copy_out(xqT[:, j, :], b, ps(b)[:, 0:256], t)

        XS = float(128 ** -0.5)

        def x_scores(h):
            b = banks.take()
            for i in range(2):
                t = group(ps(b)[:, 256 * i:256 * i + 256], [(xqT[:, h, P * i:P * i + P], xkT[:, h, :])],
                          banks.free[b], t_xq)
            return b, t

        def x_soften(h, b, t, s, sfree):
            mx = st[:, 80 + 2 * (h % 4):82 + 2 * (h % 4)]
            v = ps(b)[:, :].rearrange("p (i n) -> p i n", i=2)
            dve(lambda e: e.tensor_reduce(mx, v, AX, ALU.max, negate=True), t)
            t = dve(lambda e: e.tensor_scalar(mx, mx, XS, None, ALU.mult), sfree)
            view = [(v[:, i, :], s[:, 256 * i:256 * i + 256], XS, b) for i in range(2)]
            return view + [[(0, 0), (1, 0), (0, 1), (1, 1)]], mx, t

        pv_bank = {}

        def x_values(h, pt, t):
            b = banks.take()
            pv_bank[h] = b
            return group(ps(b)[:, 0:256], [(xv[:, k, P * h:P * h + P], pt[:, 256 * k:256 * k + 256]) for k in range(2)],
                         banks.free[b], t)

        def x_finish(h, t):
            b = pv_bank.pop(h)
            toks["ym"] = split_out(ymh[:, h, :], yml[:, h, :], b, ps(b)[:, 0:256], t)

        cqh, cql = (fra[:, a:a + 768].rearrange("p (t n) -> p t n", t=3) for a in (4096, 4864))
        ckh, ckl = (fra[:, a:a + 512].rearrange("p (t n) -> p t n", t=2) for a in (5632, 6144))
        krT = [big[:, 4352 + 256 * a:4608 + 256 * a] for a in range(2)]
        qrT = big[:, 4864:5888].rearrange("p (t n) -> p t n", t=4)
        qnT = big[:, 5888:7936].rearrange("p (t n) -> p t n", t=8)
        knT = big[:, 7936:9984].rearrange("p (t n) -> p t n", t=8)
        vv = H
        lat = big[:, 5888:6656].rearrange("p (i n) -> p i n", i=2)
        kr = big[:, 6656:6912].rearrange("p (i n) -> p i n", i=2)
        lat2 = big[:, 6912:7424].rearrange("p (i n) -> p i n", i=2)
        square = big[:, 7424:7936]
        L3 = [big[:, 8448 + 512 * z:8960 + 512 * z] for z in range(3)]

        def latents():
            bs, t = yield from stream_tokens("qd", (hTh, hTl), 8, 384)
            rs, t = rstd([ps(b)[:, 0:384] for b in bs], 384, t, scratch=square)
            yield
            for i, b in enumerate(bs):
                t2 = dve(lambda e, i=i, b=b, rs=rs: e.tensor_scalar(lat[:, i, :], ps(b)[:, 0:384], rs[i], None,
                                                                    ALU.mult), t)
                banks.give(b, t2)
            bs, tt = yield from stream_tokens("kvd", (hTh, hTl), 8, 320)
            t_cq, = transposed(lat, 3, G_Q, (cqh, cql), t2)
            yield True
            rs, t = rstd([ps(b)[:, 0:256] for b in bs], 256, tt, scratch=square)
            yield True
            for i, b in enumerate(bs):
                src = ps(b)
                dve(lambda e, i=i, src=src, rs=rs: e.tensor_scalar(lat2[:, i, :], src[:, 0:256], rs[i], None,
                                                                   ALU.mult), t, t_cs)
                x1, x2 = src[:, 256:288], src[:, 288:320]
                ct, sn = cosb[:, i, :], sinb[:, i, :]
                tm = L3[2][:, 128 * i:128 * i + 128]
                dve(lambda e, x1=x1, ct=ct, tm=tm: e.tensor_tensor(tm[:, 0:32], x1, ct, ALU.mult))
                dve(lambda e, x2=x2, sn=sn, tm=tm: e.tensor_tensor(tm[:, 32:64], x2, sn, ALU.mult), free=True)
                dve(lambda e, x2=x2, ct=ct, tm=tm: e.tensor_tensor(tm[:, 64:96], x2, ct, ALU.mult), free=True)
                t2 = dve(lambda e, x1=x1, sn=sn, tm=tm: e.tensor_tensor(tm[:, 96:128], x1, sn, ALU.mult), free=True)
                banks.give(b, t2)
                for z in (0, 64):
                    dve(lambda e, i=i, tm=tm, z=z: e.tensor_tensor(kr[:, i, z:z + 32], tm[:, 0:32], tm[:, 32:64],
                                                                   ALU.subtract), t2, free=True)
                    t3 = dve(lambda e, i=i, tm=tm, z=z: e.tensor_tensor(kr[:, i, z + 32:z + 64], tm[:, 64:96],
                                                                        tm[:, 96:128], ALU.add), t2, free=True)
            yield True
            t_ck, = transposed(lat2, 2, G_KV, (ckh, ckl), t3)
            b = banks.take()
            for i in range(2):
                t = pe(lambda e, i=i, b=b: e.transpose(ps(b)[:, P * i:P * i + P], kr[:, i, :], ident), banks.free[b], t3,
                       inc=i)
            dve(lambda e: e.memset(krT[0][64:128, :], 0.0))
            dve(lambda e: e.memset(krT[1][0:64, :], 0.0))
            dve(lambda e, b=b: e.tensor_copy(krT[0][0:64, :], ps(b)[0:64, 0:256]), t)
            toks["kr"] = dve(lambda e, b=b: e.tensor_copy(krT[1][64:128, :], ps(b)[64:128, 0:256]), t)
            banks.give(b, toks["kr"])
            yield True

            bs, t_q = yield from stream_tokens("uqr", (cqh, cql), 3, 512, t_cq)
            for i, b in enumerate(bs):
                t = t_q
                v = ps(b)[:, :].rearrange("p (h c) -> p h c", h=8)
                x1, x2 = v[:, :, 0:32], v[:, :, 32:64]
                ct = cosb[:, i, :].unsqueeze(1).to_broadcast([P, 8, 32])
                sn = sinb[:, i, :].unsqueeze(1).to_broadcast([P, 8, 32])
                ta, tb = (L3[z][:, 0:256].rearrange("p (h c) -> p h c", h=8) for z in (0, 1))
                tc, td = (L3[z][:, 256:512].rearrange("p (h c) -> p h c", h=8) for z in (0, 1))
                o = L3[2][:, :].rearrange("p (h c) -> p h c", h=8)
                dve(lambda e, x1=x1, ct=ct, ta=ta: e.tensor_tensor(ta, x1, ct, ALU.mult), t, act.tok())
                dve(lambda e, x2=x2, sn=sn, tb=tb: e.tensor_tensor(tb, x2, sn, ALU.mult), free=True)
                dve(lambda e, x2=x2, ct=ct, tc=tc: e.tensor_tensor(tc, x2, ct, ALU.mult), free=True)
                t2 = dve(lambda e, x1=x1, sn=sn, td=td: e.tensor_tensor(td, x1, sn, ALU.mult), free=True)
                banks.give(b, t2)
                dve(lambda e, o=o, ta=ta, tb=tb: e.tensor_tensor(o[:, :, 0:32], ta, tb, ALU.subtract), pe.tok())
                t2 = dve(lambda e, o=o, tc=tc, td=td: e.tensor_tensor(o[:, :, 32:64], tc, td, ALU.add), free=True)
                yield True
                b = banks.take()
                for j in range(4):
                    t = pe(lambda e, b=b, j=j: e.transpose(ps(b)[:, P * j:P * j + P], L3[2][:, P * j:P * j + P], ident),
                           banks.free[b], t2, inc=1 if j == 3 else 0)
                copy_out(qrT[:, :, P * i:P * i + P], b, ps(b)[:, :].rearrange("p (j n) -> p j n", j=4), t)
            t_w = dve.tok()
            for a in range(2):
                bs, t = yield from stream_features("uqn", (cqh, cql), 3, 512)
                for j, b in enumerate(bs):
                    copy_out(qnT[:, 4 * a + j, :], b, ps(b)[:, 0:256], t, t_w)
            for a in range(2):
                bs, t = yield from stream_features("uk", (ckh, ckl), 2, 512, t_ck)
                for j, b in enumerate(bs):
                    copy_out(knT[:, 4 * a + j, :], b, ps(b)[:, 0:256], t, t_w)
            for c in range(2):
                bs, t = yield from stream_tokens("uv", (ckh, ckl), 2, 512)
                for i, b in enumerate(bs):
                    toks["v"] = copy_out(vv[:, i, 512 * c:512 * c + 512], b, ps(b)[:, :], t)

        def mixed():
            for waiting in latents():
                if waiting:
                    next(mid)
                yield

        att_x, mixed_ = attention(4, x_scores, x_soften, x_values, x_finish), mixed()

        MS = float(192 ** -0.5)

        def m_scores(h):
            b = banks.take()
            for i in range(2):
                o = ps(b)[:, 0:128] if i == 0 else ps(b)[:, 128:384]
                n = P * (i + 1)
                sl = slice(P * i, P * i + P)
                t = group(o, [(qnT[:, h, sl], knT[:, h, 0:n]), (qrT[:, h // 2, sl], krT[h % 2][:, 0:n])],
                          banks.free[b], toks["v"], toks["kr"])
            return b, t

        def m_soften(h, b, t, s, sfree):
            mx = st[:, 80 + 2 * (h % 4):82 + 2 * (h % 4)]
            t = dve(lambda e: e.scalar_tensor_tensor(s[:, 0:384], ps(b)[:, 0:384], MS, C[:, C_MASK:C_MASK + 384],
                                                     ALU.mult, ALU.add), t, sfree)
            banks.give(b, t)
            dve(lambda e: e.tensor_reduce(mx[:, 0:1], s[:, 0:128], AX, ALU.max, negate=True))
            t = dve(lambda e: e.tensor_reduce(mx[:, 1:2], s[:, 128:384], AX, ALU.max, negate=True), t, free=True)
            return causal_view(s), mx, t

        def causal_view(s):
            return [(s[:, 0:128], s[:, 0:128], 1.0, None), (s[:, 128:384], s[:, 128:384], 1.0, None),
                    [(0, 0), (1, 0), (1, 1)]]

        def causal_values(o, w, pt, b, t):
            pe(lambda e: e.matmul(o, w(0), pt[:, 0:256], start=True, stop=False), banks.free[b], t, inc=0)
            return pe(lambda e: e.matmul(o[:, 128:256], w(1), pt[:, 256:384], start=False, stop=True))

        def m_values(h, pt, t):
            b = banks.take()
            pv_bank[h] = b
            return causal_values(ps(b)[:, 0:256], lambda k: vv[:, k, P * h:P * h + P], pt, b, t)

        def m_finish(h, t):
            b = pv_bank.pop(h)
            split_out(mTh[:, h, :], mTl[:, h, :], b, ps(b)[:, 0:256], t)

        merged = big[:, 0:2048].rearrange("p (i n) -> p i n", i=2)
        uu = big[:, 2048:3072].rearrange("p (i n) -> p i n", i=2)
        pT = gb[:, 0, :].rearrange("p (g n) -> p g n", g=4)
        gbt = [gb[:, 0, 0:512], gb[:, 0, 512:1024]]
        gt = [gb[:, 1, 0:512], gb[:, 1, 512:1024]]
        gb_free = [None, None]
        n_gate = [0]

        def pooling():
            bs, t = yield from stream_tokens("pool", (hTh, hTl), 8, 512)
            for i, b in enumerate(bs):
                t_u = copy_out(uu[:, i, :], b, ps(b)[:, :], t)
            u, w, tw = next_raw("poolc")
            u2, w2, tw2 = next_raw("poolw")
            tb = {}
            for g in range(5):
                if g < 4:
                    b = banks.take()
                    t = group(ps(b)[:, 0:256], [(uu[:, k, P * g:P * g + P], w[:, 4 * k + g, :]) for k in range(2)],
                              banks.free[b], t_u, tw)
                    tb[g] = copy_out(pT[:, g, :], b, ps(b)[:, 0:256], t)
                if g:
                    yield
                    h = g - 1
                    b = banks.take()
                    t = group(ps(b)[:, 0:256], [(w2[:, h, :], pT[:, h, :])], banks.free[b], tb[h], tw2)
                    tv = gt[h % 2][:, 0:256]
                    t = dve(lambda e, tv=tv, b=b, h=h: e.tensor_scalar(
                        tv, ps(b)[:, 0:256], G[:, G_POOL + h:G_POOL + h + 1], None, ALU.mult), t)
                    banks.give(b, t)
                    t = act(lambda e, tv=tv, h=h: e.copy(yph[:, h, :], tv), t)
                    dve(lambda e, tv=tv, h=h: e.tensor_tensor(ypl[:, h, :], tv, yph[:, h, :].bitcast(F), ALU.subtract), t)
            release(u, pe.tok())
            release(u2, pe.tok())
            gb_free[0] = gb_free[1] = pe.tok()

        def branch(br, c, y, nk, t_y):
            n = n_gate[0]
            n_gate[0] += 1
            src = gate_b[0, br:br + 1, 512 * c:512 * c + 512].to_broadcast([P, 512])
            t_gb = load(gbt[n % 2], src, gb_free[n % 2])
            bg, t_g = yield from stream_tokens(("gate", br, c), (hTh, hTl), 8, 512)
            for i in range(2):
                s = gt[i]
                t = dve(lambda e, s=s, b=bg[i]: e.tensor_tensor(s, ps(b)[:, :], gbt[n % 2], ALU.add), t_g, t_gb)
                gb_free[n % 2] = t
                banks.give(bg[i], t)
                t_s = act(lambda e, s=s: e.activation(s, s, ACT.Tanh, scale=0.5), t)
            bb, t_b = yield from stream_tokens(("br", br, c), y, nk, 512, t_y)
            for i in range(2):
                s = gt[i]
                m = merged[:, i, 512 * c:512 * c + 512]
                t = dve(lambda e, s=s: e.tensor_scalar(s, s, 0.5, 0.5, ALU.mult, ALU.add), t_s)
                o = m if br == 0 else s
                t = dve(lambda e, s=s, b=bb[i], o=o: e.tensor_tensor(o, s, ps(b)[:, :], ALU.mult), t_b)
                banks.give(bb[i], t)
                if br:
                    dve(lambda e, s=s, m=m: e.tensor_tensor(m, m, s, ALU.add))

        def middle():
            yield from pooling()
            t_yp = dve.tok()
            for c in range(2):
                yield from branch(0, c, (yph, ypl), 4, t_yp)
            for c in range(2):
                yield from branch(2, c, (ymh, yml), 4, toks["ym"])

        mid = middle()
        beside(att_x, mixed_, FILL_X)
        whole(mixed_)
        beside(attention(8, m_scores, m_soften, m_values, m_finish), mid, FILL_M)
        t_mla = dve.tok()
        whole(mid)
        whole(branch(1, 0, (mTh, mTl), 8, t_mla))
        t_half = dve.tok()
        last = branch(1, 1, (mTh, mTl), 8, t_mla)
        for _ in range(5):
            next(last)
        t_m = transposed(merged, 8, None, (moh, mol), t_half, only=(0,))
        whole(last)
        for z in (4, 5, 6, 7):
            free_slots.append((RAW + z, pe.tok()))
        issue()
        toks["merged"] = dve.tok()
        out0 = stream_tokens(("out", 0), (moh, mol), 8, 512, t_m[0], later=lambda: toks["m4"])
        for _ in range(2):
            next(out0)
        toks["m4"], = transposed(merged, 8, None, (moh, mol), toks["merged"], only=(4,))
        t_sb = pe.tok()
        d_gffn = load(gb[:, 0, :], grow[0:1, :].to_broadcast([P, 1024]), toks["merged"])
        d_gfin = load(gb[:, 1, :], grow[1:2, :].to_broadcast([P, 1024]), toks["merged"])
        k_x, tsq = columns(), {}
        wr = big[:, 0:288].rearrange("p (k n) -> p k n", k=8)
        d_wr = load(wr, w_route.rearrange("p (k n) -> p k n", k=8), t_sb)
        d_br = load(rt[0:36, 0:1], b_route.rearrange("o n -> n o"), dve.tok())
        for c in range(2):
            bs, tt = whole(out0 if c == 0 else stream_tokens(("out", 1), (moh, mol), 8, 512))
            for i, b in enumerate(bs):
                xs = X[:, i, 512 * c:512 * c + 512]
                t2 = dve(lambda e, xs=xs, b=b: e.tensor_tensor(xs, xs, ps(b)[:, :], ALU.add), toks["end", i])
                banks.give(b, t2)
                tsq[i] = square_act(k_x[:, 2 * c + i:2 * c + i + 1], xs, 512, t2)
        for z in (0, 1, 2, 3, 8, 9):
            free_slots.append((RAW + z, pe.tok()))
        issue()

        h2T = big[:, 512:2560].rearrange("p (t n) -> p t n", t=8)
        rs = [k_x[:, 4 + i:5 + i] for i in range(2)]
        t = [root(k_x[:, i:i + 1], rs[i], 1024, tsq[i], more=k_x[:, 2 + i:3 + i]) for i in range(2)]
        t_h2 = [dve(lambda e, i=i, rs=rs: e.scalar_tensor_tensor(
            H[:, i, :].rearrange("p (k c) -> p k c", k=8), X[:, i, :].rearrange("p (c k) -> p k c", k=8), rs[i],
            gb[:, 0, :].rearrange("p (c k) -> p k c", k=8), ALU.mult, ALU.mult), t[i], d_gffn) for i in range(2)]
        warm(WARM[2])
        t = transposed(H, 8, None, (h2T,), d_wr, halves=t_h2)
        b = banks.take()
        for k in range(8):
            tr = pe(lambda e, k=k, b=b: e.matmul(ps(b)[0:36, 0:256], wr[:, k, :], h2T[:, k, :], start=(k == 0), stop=(k == 7)),
                    banks.free[b], t[k // 4], inc=k == 7)
        logT = big[0:36, 4608:4864]
        t = dve(lambda e, b=b: e.tensor_scalar(logT, ps(b)[0:36, 0:256], rt[0:36, 0:1], None, ALU.add), tr, d_br)
        banks.give(b, t)
        b = banks.take()
        for i in range(2):
            t = pe(lambda e, b=b, i=i: e.transpose(ps(b)[:, 64 * i:64 * i + 36], logT[:, P * i:P * i + P], ident[0:36, 0:36]),
                   banks.free[b], t, inc=i)
        R = rt[:, 64:640]

        def col(a, n):
            return R[:, a:a + n]

        def v2(a, n):
            return R[:, a:a + 2 * n].rearrange("p (i n) -> p i n", i=2)

        L, EM, M, W, PX, E32 = v2(0, 36), v2(72, 32), v2(136, 32), v2(200, 32), v2(264, 32), v2(328, 32)
        E4, OG, top, BIG, TT = v2(392, 4), v2(400, 4), v2(408, 8), v2(424, 8), v2(440, 32)
        g1, ng, gs, nm, tm_, sm = (v2(504 + 2 * n, 1) for n in range(6))
        rank4 = C[:, C_RANK:C_RANK + 4]

        dve(lambda e, b=b: e.tensor_copy(L, ps(b)[:, 0:128].rearrange("p (i n) -> p i n", i=2)[:, :, 0:36]), t)
        banks.give(b, dve.tok())
        gl, el = L[:, :, 0:4], L[:, :, 4:36]
        dve(lambda e: e.tensor_reduce(g1, gl, AX, ALU.max))
        t = dve.tok()
        for i in range(2):
            dve(lambda e, i=i: e.scalar_tensor_tensor(OG[:, i, :], gl[:, i, :], g1[:, i, :], rank4, ALU.is_equal,
                                                      ALU.mult), t, free=True)
        dve(lambda e: e.tensor_scalar(ng, g1, -1.0, None, ALU.mult), t, free=True)
        t_ng = dve(lambda e: e.tensor_reduce(tm_, OG, AX, ALU.max))
        t = t_ng
        for i in range(2):
            dve(lambda e, i=i: e.tensor_scalar(OG[:, i, :], OG[:, i, :], tm_[:, i, :], NEG, ALU.is_lt, ALU.mult), t,
                free=True)
        t = dve.tok()
        for i in range(2):
            dve(lambda e, i=i: e.tensor_tensor(EM[:, i, :].rearrange("p (g k) -> p g k", g=4),
                                               el[:, i, :].rearrange("p (g k) -> p g k", g=4),
                                               OG[:, i, :].unsqueeze(2).to_broadcast([P, 4, 8]), ALU.add), t, free=True)
        t = dve.tok()
        for i in range(2):
            dve(lambda e, i=i: e.max(top[:, i, :], EM[:, i, :]), t, free=True)
        dve(lambda e: e.tensor_scalar(nm, top[:, :, 0:1], -1.0, None, ALU.mult))
        t_nm = dve(lambda e: e.memset(top[:, :, 2:8], ABSENT), free=True)
        t = dve.tok()
        for i in range(2):
            dve(lambda e, i=i: e.match_replace(TT[:, i, :], top[:, i, :], EM[:, i, :], TAKEN), t, free=True)
        t_M = dve(lambda e: e.tensor_scalar(M, TT, TAKEN, None, ALU.is_equal))
        warm(WARM[3])
        tri, ones = C[:, C_TRI:C_TRI + P], C[:, C_ONE:C_ONE + 1].to_broadcast([P, P])
        b = banks.take()
        group(ps(b)[:, 0:32], [(tri, M[:, 0, :])], banks.free[b], t_M)
        t_rank = group(ps(b)[:, 32:64], [(ones, M[:, 0, :]), (tri, M[:, 1, :])])
        b_count = banks.take()
        t_count = group(ps(b_count)[:, 64:96], [(ones, M[:, 0, :]), (ones, M[:, 1, :])], banks.free[b_count])
        dve(lambda e: e.tensor_scalar(PX, M, -1000.0, 1000.0, ALU.mult, ALU.add))
        for i in range(2):
            act(lambda e, i=i: e.activation(E4[:, i, :], gl[:, i, :], ACT.Exp, bias=ng[:, i, :],
                                            accum_out=gs[:, i, :]), t_ng, free=True)
        for i in range(2):
            t = act(lambda e, i=i: e.activation(E32[:, i, :], EM[:, i, :], ACT.Exp, bias=nm[:, i, :]), t_nm, free=True)
        dve(lambda e, b=b: e.tensor_tensor(PX, PX, ps(b)[:, 0:64].rearrange("p (i n) -> p i n", i=2), ALU.add), t_rank)
        banks.give(b, dve.tok())
        t_exp = t
        warm(WARM[4])

        def weigh():
            t = dve.tok()
            for i in range(2):
                dve(lambda e, i=i: e.tensor_tensor_reduce(W[:, i, :], E32[:, i, :], M[:, i, :], 1.0, 0.0, ALU.mult,
                                                          ALU.add, sm[:, i, :]), t_exp, t, free=True)
            dve(lambda e: e.tensor_tensor(sm, sm, gs, ALU.mult), t_exp)
            dve(lambda e: e.reciprocal(sm, sm))
            t = dve.tok()
            for i in range(2):
                dve(lambda e, i=i: e.tensor_scalar(W[:, i, :], W[:, i, :], sm[:, i, :], None, ALU.mult), t, free=True)

        def count():
            dve(lambda e: e.tensor_reduce(tm_[:, 0, :], ps(b_count)[:, 64:96], AX, ALU.max), t_count)
            banks.give(b_count, dve.tok())
            return dve(lambda e: e.tensor_copy(flag[:, :], tm_[:, 0, :]))

        MO = big[:, 2560:4608].rearrange("p (i n) -> p i n", i=2)
        sel = [big[:, 4608 + 512 * z:5120 + 512 * z] for z in range(2)]
        XE = [big[:, 5632 + 1024 * z:6656 + 1024 * z].rearrange("p (t n) -> p t n", t=8) for z in range(2)]
        CM = [big[:, 7680 + 256 * z:7936 + 256 * z] for z in range(2)]
        YE = big[:, 8192:9216]
        AE = [T[0][:, 0:256], T[1][:, 0:256]]
        AT = [S[0][:, 256:512], S[1][:, 256:512]]
        xe_tok, cm_tok, ye_free = {}, {}, [None]
        iota = C[:, C_IOTA:C_IOTA + CAP]

        def select(g):
            z = g % 2
            t = dve.tok()
            for part in range(2):
                for i in range(2):
                    s_ = sel[z][:, 128 * i:128 * i + 128].rearrange("p (e s) -> p e s", e=4)
                    w_ = sel[z][:, 256 + 128 * i:384 + 128 * i].rearrange("p (e s) -> p e s", e=4)
                    px = PX[:, i, 4 * g:4 * g + 4].unsqueeze(2).to_broadcast([P, 4, CAP])
                    wt = W[:, i, 4 * g:4 * g + 4].unsqueeze(2).to_broadcast([P, 4, CAP])
                    io = iota.unsqueeze(1).to_broadcast([P, 4, CAP])
                    if part == 0:
                        dve(lambda e, s_=s_, px=px, io=io: e.tensor_tensor(s_, io, px, ALU.is_equal), t, sel_free[z],
                            free=True)
                    else:
                        dve(lambda e, s_=s_, w_=w_, wt=wt: e.tensor_tensor(w_, s_, wt, ALU.mult), t, free=True)
                t = dve.tok()
                if part == 0:
                    t_s = t
                    if g == 0:
                        weigh()
                        t = dve.tok()
            return t_s, t

        sel_free = [None, None]

        def gather(g, ts):
            z = g % 2
            for c in range(2):
                b = banks.take()
                t = group(ps(b)[:, :], [(sel[z][:, P * i:P * i + P], H[:, i, 512 * c:512 * c + 512]) for i in range(2)],
                          banks.free[b], ts[0], *t_h2)
                t = copy_out(YE[:, 512 * c:512 * c + 512], b, ps(b)[:, :], t, ye_free[0], eng=(act, dve)[c])
                got[c] = t
            for a in range(2):
                b = banks.take()
                for j in range(4):
                    t = pe(lambda e, a=a, j=j, b=b: e.transpose(
                        ps(b)[:, P * j:P * j + P], YE[:, P * (4 * a + j):P * (4 * a + j) + P], ident),
                        banks.free[b], got[a], inc=j == 3)
                xe_tok[g, a] = copy_out(XE[z][:, 4 * a:4 * a + 4, :], b, ps(b)[:, :].rearrange("p (j n) -> p j n", j=4),
                                        t, xe_free[z])
            ye_free[0] = pe.tok()

        got = {}

        def gather_weights(g, ts):
            z = g % 2
            b = banks.take()
            for i in range(2):
                tt = pe(lambda e, b=b, i=i: e.transpose(ps(b)[:, P * i:P * i + P], sel[z][:, 256 + P * i:384 + P * i], ident),
                        banks.free[b], ts[1], inc=i)
            sel_free[z] = tt
            cm_tok[g] = copy_out(CM[z], b, ps(b)[:, 0:256], tt, cm_free[z])

        xe_free, cm_free = [None, None], [None, None]

        def experts(g):
            z = g % 2
            b = banks.take()
            for half_ in range(2):
                for t4 in range(4):
                    u, w, tw = next_raw(("eg", "eu")[half_])
                    w = w.rearrange("p e (k n) -> p e k n", k=2)
                    for k in range(2):
                        kk = 2 * t4 + k
                        for j in range(4):
                            end = k == 1 and j == 3
                            t = pe(lambda e, w=w, k=k, kk=kk, j=j, half_=half_: e.matmul(
                                ps(b)[32 * j:32 * j + 32, 256 * half_:256 * half_ + 256],
                                XE[z][:, kk, 32 * j:32 * j + 32], w[:, j, k, :], start=(kk == 0), stop=(kk == 7)),
                                banks.free[b], tw, xe_tok[g, kk // 4], inc=1 if end else 0)
                    release(u, t)
            xe_free[z] = t
            a_, at_ = AE[z], AT[z]
            t2 = act(lambda e: e.activation(a_, ps(b)[:, 0:256], ACT.Silu), t, dve.tok())
            t2 = dve(lambda e: e.tensor_tensor(a_, a_, ps(b)[:, 256:512], ALU.mult), t2)
            banks.give(b, t2)
            return t2

        def experts_down(g, t2):
            z = g % 2
            a_, at_ = AE[z], AT[z]
            b = banks.take()
            for k in range(2):
                t = pe(lambda e, b=b, k=k: e.transpose(ps(b)[:, P * k:P * k + P], a_[:, P * k:P * k + P], ident),
                       banks.free[b], t2, inc=k)
            t = copy_out(at_, b, ps(b)[:, 0:256], t)
            for c in range(2):
                b = banks.take()
                for k in range(2):
                    u, w, tw = next_raw("ed")
                    for j in range(4):
                        tt = pe(lambda e, b=b, w=w, k=k, j=j: e.matmul(
                            ps(b)[32 * j:32 * j + 32, :], at_[:, P * k + 32 * j:P * k + 32 * j + 32], w[:, j, :],
                            start=(k == 0), stop=(k == 1)), banks.free[b], tw, t, inc=1 if j == 3 else 0)
                    release(u, tt)
                t_y = copy_out(YE[:, 512 * c:512 * c + 512], b, ps(b)[:, :], tt, ye_free[0])
            return t_y

        t_mo = [None, None]

        def combine(g, t_y):
            z = g % 2
            for i in range(2):
                for c in range(2):
                    b = banks.take()
                    t = group(ps(b)[:, :], [(CM[z][:, P * i:P * i + P], YE[:, 512 * c:512 * c + 512])], banks.free[b], t_y,
                              cm_tok[g])
                    o = MO[:, i, 512 * c:512 * c + 512]
                    prior = X[:, i, 512 * c:512 * c + 512] if g == 0 else o
                    t = dve(lambda e, o=o, b=b, prior=prior: e.tensor_tensor(o, prior, ps(b)[:, :], ALU.add), t)
                    banks.give(b, t)
                t_mo[i] = t
            ye_free[0] = cm_free[z] = pe.tok()

        full = {}

        def load_flag(e):
            full[e.engine] = e.value_load(flag[0:1, 0:1], min_val=0, max_val=256)

        t_s = select(0)
        gather(0, t_s)
        t_flag = count()
        for g in range(8):
            if g == 4:
                for q in (pe, act, dve):
                    q(load_flag, t_flag, inc=0)
            t_w = t_s
            if g < 7:
                t_s = select(g + 1)
            t2 = experts(g)
            gather_weights(g, t_w)
            if g < 7:
                gather(g + 1, t_s)
            combine(g, experts_down(g, t2))

        fast = {q: q.n for q in (pe, act, dve)}
        marks = {q: len(q.items) for q in (pe, act, dve)}
        f_go, f_w, f_g, f_s, f_a, f_y, f_end, f_done = (
            sem(n) for n in ("f_go", "f_w", "f_g", "f_s", "f_a", "f_y", "f_end", "f_done"))
        fast_pe, fast_dve = pe.tok(), dve.tok()
        AG = junk[:, 0:512].rearrange("p (k n) -> p k n", k=2)
        WC = T[0][:, 0:64].rearrange("p (i n) -> p i n", i=2)
        WD = T[0][:, 64:128].rearrange("p (i n) -> p i n", i=2)
        limit = -1 if force_general else CAP

        def general(eng, body):
            with eng.If(full[eng.engine] > limit):
                body(eng)

        wg_, wu_, wd_ = raw[:, 0, :], raw[:, 1, :], raw[:, 2, :]

        def general_sp(e):
            e.wait_ge(*fast_dve)
            e.wait_ge(*fast_pe)
            with e.Fori(0, 32) as n:
                e.wait_ge(f_go, 1)
                e.sem_clear(f_go)
                e.dma_start(wg_, w_gate_e[0, bass.ds(n, 1)].rearrange("e (p k) n -> p (e k n)", p=P)).then_inc(f_w, 16)
                e.dma_start(wu_, w_up_e[0, bass.ds(n, 1)].rearrange("e (p k) n -> p (e k n)", p=P)).then_inc(f_w, 16)
                e.dma_start(wd_.rearrange("p (k n) -> p k n", k=2),
                            w_down_e[0, bass.ds(n, 1)].rearrange("e (k p) n -> p (e k) n", p=P)).then_inc(f_w, 16)
            e.wait_ge(f_go, 1)

        def general_pe(e):
            wg, wu = (v.rearrange("p (k n) -> p k n", k=8) for v in (wg_, wu_))
            wd = wd_.rearrange("p (k n) -> p k n", k=2)
            with e.Fori(0, 32):
                e.wait_ge(f_w, 48)
                e.sem_clear(f_w)
                for s_, w in enumerate((wg, wu)):
                    for j in range(2):
                        for k in range(8):
                            t = e.matmul(ps(s_)[:, 256 * j:256 * j + 256], w[:, k, P * j:P * j + P], h2T[:, k, :],
                                         start=(k == 0), stop=(k == 7))
                t.then_inc(f_g, 1)
                e.wait_ge(f_a, 1)
                e.sem_clear(f_a)
                for i in range(2):
                    for c in range(2):
                        for k in range(2):
                            t = e.matmul(ps(2 + 2 * i + c)[:, :], AG[:, k, P * i:P * i + P],
                                         wd[:, k, 512 * c:512 * c + 512], start=(k == 0), stop=(k == 1))
                t.then_inc(f_y, 1)
            e.wait_ge(f_done, 2)

        def general_act(e):
            with e.Fori(0, 32):
                e.wait_ge(f_g, 1)
                e.sem_clear(f_g)
                e.activation(AG, ps(0)[:, :].rearrange("p (k n) -> p k n", k=2), ACT.Silu).then_inc(f_s, 1)
            e.wait_ge(f_done, 2)

        def general_dve(e):
            chain = [0]
            e.wait_ge(*fast_pe)
            e.wait_ge(act.sem, fast[act])
            e.wait_ge(*fast_dve)
            e.tensor_copy(WC, W).then_inc(f_end, 1)
            e.wait_ge(f_end, 1)
            e.tensor_copy(MO, X[:, :, :]).then_inc(f_end, 1)
            e.wait_ge(f_end, 2)
            e.sem_clear(f_end)
            with e.Fori(0, 32):
                e.sem_inc(f_go, 1)
                e.wait_ge(f_s, 1)
                e.sem_clear(f_s)
                e.tensor_tensor(AG, AG, ps(1)[:, :].rearrange("p (k n) -> p k n", k=2), ALU.mult).then_inc(f_a, 1)
                e.wait_ge(f_y, 1)
                e.sem_clear(f_y)
                for i in range(2):
                    for c in range(2):
                        o = MO[:, i, 512 * c:512 * c + 512]
                        e.scalar_tensor_tensor(o, ps(2 + 2 * i + c)[:, :], WC[:, i, 0:1], o, ALU.mult,
                                               ALU.add).then_inc(f_end, 1)
                e.tensor_copy(WD[:, :, 0:31], WC[:, :, 1:32]).then_inc(f_end, 1)
                e.wait_ge(f_end, 5)
                e.tensor_copy(WC[:, :, 0:31], WD[:, :, 0:31]).then_inc(f_end, 1)
                e.wait_ge(f_end, 6)
                e.sem_clear(f_end)
            e.sem_inc(f_go, 1)
            e.sem_inc(f_done, 2)

        t_done = pe.tok()
        t_all = dve.tok()
        rs, t = rstd_halves([MO[:, 0, :], MO[:, 1, :]], 1024, [t_mo[0]], [t_mo[1]])
        split_upto(at["piece"] + SPLITS[0], t_done)
        t = [dve(lambda e, i=i, rs=rs: e.scalar_tensor_tensor(X[:, i, :], MO[:, i, :], rs[i], gb[:, 1, :], ALU.mult, ALU.mult),
                 t[i], d_gfin) for i in range(2)]
        d_pm = load(gb[:, 0, :], grow[2:3, :].to_broadcast([P, 1024]), t_all)
        d_pf = load(gb[:, 1, :], grow[3:4, :].to_broadcast([P, 1024]), t[1])
        rs, t = rstd_halves([X[:, 0, :], X[:, 1, :]], 1024, [t[0]], [t[1]], one="act")
        split_upto(at["piece"] + SPLITS[1], t_done)
        t = scaled(H, X, rs, t, t_done)
        warm(WARM[5])
        split_upto(at["piece"] + SPLITS[2], t_done)
        t_h = transposed(H, 8, G_MIX2, (hTh, hTl), halves=t)
        bias = big[:, 0:4096].rearrange("p (h n) -> p h n", h=16)
        d_bias = load(bias, rel_ext, dve.tok(), pe.tok())
        t_bias = pool(lambda e: e.memset(bias[0:64, :, 192:256], NEG), d_bias)
        qT = big[:, 4096:6144].rearrange("p (t n) -> p t n", t=8)
        kT = big[:, 6144:8192].rearrange("p (t n) -> p t n", t=8)
        v2_ = H
        def qk(c):
            bs, tt = yield from stream_features(("qkv", c), (hTh, hTl), 8, 512, t_h[0], later=t_h[1])
            for j, b in enumerate(bs):
                d = (qT, kT)[c // 2][:, 4 * (c % 2) + j, :]
                copy_out(d, b, ps(b)[:, 0:256], tt)

        def vals(c):
            bs, tt = yield from stream_tokens(("qkv", 4 + c), (hTh, hTl), 8, 512)
            for i, b in enumerate(bs):
                toks["q", c] = copy_out(v2_[:, i, 512 * c:512 * c + 512], b, ps(b)[:, :], tt)

        whole(qk(0))
        whole(qk(2))
        whole(vals(0))

        def r_scores(h):
            b = banks.take()
            o = 64 * (h % 2)
            for i in range(2):
                t = group(ps(b)[:, 0:128] if i == 0 else ps(b)[:, 128:384],
                          [(qT[o:o + 64, h // 2, P * i:P * i + P], kT[o:o + 64, h // 2, 0:P * (i + 1)])],
                          banks.free[b], toks["q", h // 8])
            return b, t

        def r_soften(h, b, t, s, sfree):
            mx = st[:, 80 + 2 * (h % 4):82 + 2 * (h % 4)]
            dve(lambda e: e.scalar_tensor_tensor(s[:, 0:128], ps(b)[:, 0:128], 0.125, bias[:, h, 128:256], ALU.mult,
                                                 ALU.add), t, sfree, t_bias)
            t = dve(lambda e: e.scalar_tensor_tensor(s[:, 128:384], ps(b)[:, 128:384], 0.125, bias[:, h, :], ALU.mult,
                                                     ALU.add), free=True)
            banks.give(b, t)
            dve(lambda e: e.tensor_reduce(mx[:, 0:1], s[:, 0:128], AX, ALU.max, negate=True))
            t = dve(lambda e: e.tensor_reduce(mx[:, 1:2], s[:, 128:384], AX, ALU.max, negate=True), t, free=True)
            return causal_view(s), mx, t

        def r_values(h, pt, t):
            if h % 2 == 0:
                pv_bank[0] = banks.take()
            b = pv_bank[0]
            o = 64 * (h % 2)
            return causal_values(ps(b)[o:o + 64, 0:256], lambda k: v2_[:, k, 64 * h:64 * h + 64], pt, b, t)

        def r_finish(h, t):
            if h % 2:
                b = pv_bank[0]
                toks["f", h // 2] = split_out(mTh[:, h // 2, :], mTl[:, h // 2, :], b, ps(b)[:, 0:256], t)

        def second_half():
            yield from qk(1)
            yield from qk(3)
            yield from vals(1)

        def wide(key, acc, aT, first, last, *waits, hold=False):
            ah_, al_ = aT
            q, h, l, tp, _, _ = next_piece(key)
            ts, first_wait = {}, list(waits)
            for i in range(2):
                for c in range(2):
                    b = acc[c][i]
                    for n, (a, w) in enumerate(((ah_, h), (al_, h), (ah_, l))):
                        end = n == 2 and (last or (i == 1 and c == 1))
                        ts[c, i] = pe(lambda e, b=b, a=a[:, P * i:P * i + P], w=w[:, 0, 512 * c:512 * c + 512],
                                      s0=first and n == 0, s1=last and n == 2: e.matmul(ps(b)[:, :], a, w, start=s0, stop=s1),
                                      tp, banks.free[b] if first else None, *first_wait, inc=1 if end else 0)
                        first_wait = []
            wfree[q % PIECES] = ts[1, 1]
            if not hold:
                split_upto(q + AHEAD)
            return ts

        def o_tile(k):
            return wide("o", o_banks, (mTh[:, k, :], mTl[:, k, :]), k == 0, k == 7, toks["f", k], hold=k >= HOLD)

        att = attention(16, r_scores, r_soften, r_values, r_finish)
        fill = second_half()
        tile_at = {step: k for k, step in enumerate(TILE_AT)}
        for step in range(19):
            next(att)
            if step < 8:
                for _ in range(FILL_B[step]):
                    next(fill, None)
            if step == 7:
                whole(fill)
                o_banks = [[banks.take() for _ in range(2)] for _ in range(2)]
            if step in tile_at:
                o_tile(tile_at[step])
        whole(att)
        t_o = o_tile(7)

        def squares(k, c, i, b, t):
            return square_act(k[:, 2 * c + i:2 * c + i + 1], ps(b)[:, :], 512, t)

        def add_normed(k, bs, tsq, row, d_row, done):
            tr = [root(k[:, i:i + 1], k[:, 4 + i:5 + i], 1024, tsq[i], more=k[:, 2 + i:3 + i]) for i in range(2)]
            out_t = []
            for i in range(2):
                for c in range(2):
                    b = bs[c][i]
                    hs = H[:, i, 512 * c:512 * c + 512]
                    t = dve(lambda e, hs=hs, b=b, i=i, c=c: e.scalar_tensor_tensor(
                        hs, ps(b)[:, :], k[:, 4 + i:5 + i], gb[:, row, 512 * c:512 * c + 512], ALU.mult, ALU.mult),
                        tr[i], d_row, free=c > 0)
                    banks.give(b, t)
                out_t.append(dve(lambda e, i=i: e.tensor_tensor(X[:, i, :], X[:, i, :], H[:, i, :], ALU.add), t))
                done(i, out_t[i])
            return out_t

        k_o, tsq = columns(), {}
        for i in range(2):
            for c in range(2):
                tsq[i] = squares(k_o, c, i, o_banks[c][i], t_o[c, i])
        t = add_normed(k_o, o_banks, tsq, 0, d_pm, lambda i, t: None)
        rs, t = rstd_halves([X[:, 0, :], X[:, 1, :]], 1024, [t[0]], [t[1]], one="act")
        t = scaled(H, X, rs, t)
        split_upto(at["piece"] + AHEAD - 1)
        warm(WARM[6])
        t_h = transposed(H, 8, G_FFN2, (hTh, hTl), halves=t)

        acc = [[banks.take() for _ in range(2)] for _ in range(2)]
        ah = [frb[:, 512 * z:512 * z + 512].rearrange("p (k n) -> p k n", k=2) for z in range(2)]
        al = [frb[:, 1024 + 512 * z:1536 + 512 * z].rearrange("p (k n) -> p k n", k=2) for z in range(2)]
        a_free = [None, None]

        def ffn_down(c, t):
            z = c % 2
            for k in range(2):
                ts = wide(("fd", c), acc, (ah[z][:, k, :], al[z][:, k, :]), c == 0 and k == 0, c == 10 and k == 1, t)
            a_free[z] = ts[1, 1]
            return ts

        s_read = dve.tok()
        for c in range(12):
            z = c % 2
            if c < 11:
                bg, tg = whole(stream_features(("fg", c), (hTh, hTl), 8, 256, t_h[0], later=t_h[1]))
                t_s = [None, None]
                for j in range(2):
                    t_s[j] = act(lambda e, s=S[j][:, 0:256], b=bg[j]: e.activation(s, ps(b)[:, 0:256], ACT.Silu), tg,
                                 s_read)
                    banks.give(bg[j], t_s[j])
                bu, tt = whole(stream_features(("fu", c), (hTh, hTl), 8, 256))
                for j in range(2):
                    s, o = S[j][:, 0:256], S[j][:, 256:512]
                    t2 = dve(lambda e, s=s, o=o, b=bu[j]: e.tensor_tensor(o, s, ps(b)[:, 0:256], ALU.mult), t_s[j], tt)
                    banks.give(bu[j], t2)
                    s_read = t2
                    t2 = act(lambda e, o=o, j=j, z=z: e.copy(ah[z][:, j, :], o), t2, a_free[z])
                    t2 = dve(lambda e, o=o, j=j, z=z: e.tensor_tensor(al[z][:, j, :], o, ah[z][:, j, :].bitcast(F),
                                                                      ALU.subtract), t2)
            if c:
                t_acc = ffn_down(c - 1, t_a)
            t_a = t2
        k_f = columns()
        for i in range(2):
            for cc in range(2):
                tsq[i] = squares(k_f, cc, i, acc[cc][i], t_acc[cc, i])
        s_out = sem("s_out")
        ov = out.rearrange("a (i p) n -> p (a i) n", p=P)
        add_normed(k_f, acc, tsq, 1, d_pf,
                   lambda i, t: sp(lambda e: e.dma_start(ov[:, i, :], X[:, i, :]).then_inc(s_out, 16), t))

        def emit(eng, q, mark, body):
            rest = q.items[mark:]
            q.items = q.items[:mark]
            q.emit(eng)
            general(eng, body)
            q.items = rest
            q.emit(eng)

        def emit_sp(eng, items, seen):
            for fn, waits in items:
                for s, val in waits:
                    if val > seen.get(id(s), 0):
                        eng.wait_ge(s, val)
                        seen[id(s)] = val
                fn(eng)

        first_late = at["late_sp"]
        block = ctx.enter_context(nc.Block())

        @block.sync
        def _(e):
            seen = {}
            emit_sp(e, sp_items[:first_late], seen)
            e.wait_ge(*t_flag)
            load_flag(e)
            general(e, general_sp)
            emit_sp(e, sp_items[first_late:], seen)
            e.wait_ge(s_out, 32)

        @block.tensor
        def _(e):
            emit(e, pe, marks[pe], general_pe)

        @block.scalar
        def _(e):
            emit(e, act, marks[act], general_act)

        @block.vector
        def _(e):
            emit(e, dve, marks[dve], general_dve)

        @block.gpsimd
        def _(e):
            pool.emit(e)


def kernel(**inputs):
    import concourse.bacc as _bacc
    from concourse import mybir as _mybir
    from concourse.bass_utils import run_bass_kernel_spmd as _run

    a = {k: np.ascontiguousarray(v) for k, v in inputs.items()}

    def cols(*names):
        return np.ascontiguousarray(np.concatenate([a[n].reshape(-1, P).T for n in names], axis=1))

    c, pool = shape_constants()
    rel = a["rel_bias_2"][0]
    rel_ext = np.concatenate([np.repeat(rel[:, 191:192], 127, axis=1), rel[:, ::-1], np.repeat(rel[:, 0:1], 65, axis=1)],
                             axis=1)
    rel_ext = np.stack([rel_ext[:, 127 - p:383 - p] for p in range(P)])
    route = np.concatenate([a["w_router_group"][0], a["w_router_expert"][0]], axis=1)
    arrays = {
        "x": a["x"], "mem": a["mem"], "positions": np.ascontiguousarray(a["positions"].reshape(2, P).T),
        "w_in": a["w_in"], "gate_b": a["gate_b"], "w_uq": a["w_uq"], "w_uk": a["w_uk"], "w_uv": a["w_uv"],
        "pool_w": a["pool_w"], "w_mem_kv": a["w_mem_kv"], "w_br_pool": a["w_br_pool"], "w_br_mla": a["w_br_mla"],
        "w_br_mem": a["w_br_mem"], "w_out": a["w_out"], "w_gate_e": a["w_gate_e"], "w_up_e": a["w_up_e"],
        "w_down_e": a["w_down_e"], "w_qkv": a["w_qkv_2"], "w_o": a["w_o_2"], "w_gate": a["w_gate_2"],
        "w_up": a["w_up_2"], "w_down": a["w_down_2"],
        "gvec": cols("mix_norm_g", "mem_norm_g", "q_norm_g", "kv_norm_g", "pool_scale", "g_pre_mix_2", "g_pre_ffn_2"),
        "grow": np.ascontiguousarray(np.stack([a["ffn_norm_g"][0], a["final_norm_g"], a["g_post_mix_2"][0],
                                               a["g_post_ffn_2"][0]])),
        "w_route": np.ascontiguousarray(route.reshape(P, 288)),
        "b_route": np.ascontiguousarray(np.concatenate([a["b_router_group"], a["b_router_expert"]], axis=1)),
        "rel_ext": np.ascontiguousarray(rel_ext), "cst": c, "cst_pool": pool,
    }
    nc = _bacc.Bacc("TRN2", target_bir_lowering=False, num_devices=1)
    args = [nc.dram_tensor(f"in_{n}", v.shape, _mybir.dt.from_np(v.dtype), kind="ExternalInput").ap()
            for n, v in arrays.items()]
    args.append(nc.dram_tensor("out_0", (1, 256, 1024), _mybir.dt.float32, kind="ExternalOutput").ap())
    build(nc, *args)
    r = _run(nc, [{f"in_{n}": v for n, v in arrays.items()}], core_ids=[0])
    return r.results[0]["out_0"]
```
